# Optimizing a Trainium2 kernel written in Bass

```python
import math
import jax
import jax.numpy as jnp
from jax import lax
import numpy as np

D_MODEL = 1024
BATCH = 1
SEQ = 512
DEPTH = 2

CTX_LEN = 256
GRID_W = 64
HEAD_DIM = 64
N_BRANCH = 4
BRANCH_W = D_MODEL // N_BRANCH
N_HEADS = BRANCH_W // HEAD_DIM
EPS = 1e-6

RWKV_W_RANK = 64
RWKV_A_RANK = 64
RWKV_G_RANK = 128
GDN_CONV = 5
GDN_CHUNK = 64
SGU_CHUNK = 128
CONV_W = 31
PEER_HEADS = 8
PEER_NKEYS = 128
PEER_EXPERTS = PEER_NKEYS * PEER_NKEYS
PEER_DKEY = 256
PEER_TOPK = 16
PEER_BLOCK = 128

RWKV_COLS = 3 * BRANCH_W + RWKV_W_RANK + RWKV_A_RANK + RWKV_G_RANK
GDN_COLS = 4 * BRANCH_W + 4 * N_HEADS
SGU_COLS = 2 * BRANCH_W
CONF_COLS = 2 * BRANCH_W
GATE_COLS = N_BRANCH * D_MODEL
IN_COLS = RWKV_COLS + GDN_COLS + SGU_COLS + CONF_COLS + GATE_COLS
IN_SPLITS = (RWKV_COLS, RWKV_COLS + GDN_COLS, RWKV_COLS + GDN_COLS + SGU_COLS,
             RWKV_COLS + GDN_COLS + SGU_COLS + CONF_COLS)
RWKV_SPLITS = (BRANCH_W, 2 * BRANCH_W, 3 * BRANCH_W, 3 * BRANCH_W + RWKV_W_RANK,
               3 * BRANCH_W + RWKV_W_RANK + RWKV_A_RANK)
GDN_SPLITS = (3 * BRANCH_W, 4 * BRANCH_W, 4 * BRANCH_W + 2 * N_HEADS)

kernel_name = 'hybrid_rwkv7_gdn_sgu_conformer_peer_dit'

def rms_norm(x, gain):
    xf = x.astype(jnp.float32)
    y = xf * lax.rsqrt(jnp.mean(xf * xf, -1, keepdims=True) + EPS)
    return (y * gain).astype(x.dtype)

def layer_norm(x, gain, bias):
    xf = x.astype(jnp.float32)
    mu = jnp.mean(xf, -1, keepdims=True)
    var = jnp.mean(jnp.square(xf - mu), -1, keepdims=True)
    return ((xf - mu) * lax.rsqrt(var + EPS) * gain + bias).astype(x.dtype)

def l2_normalize(x):
    xf = x.astype(jnp.float32)
    return (xf * lax.rsqrt(jnp.sum(xf * xf, -1, keepdims=True) + EPS)).astype(x.dtype)

def modulate(x, gain, shift, scale):
    return rms_norm(x, gain) * (1.0 + scale) + shift

def split_heads(t):
    return t.reshape(t.shape[:-1] + (N_HEADS, HEAD_DIM))

def depthwise_conv(x, w):
    pad = w.shape[0] // 2
    return lax.conv_general_dilated(x, w[:, None, :], window_strides=(1,), padding=[(pad, pad)],
                                    dimension_numbers=('NWC', 'WIO', 'NWC'),
                                    feature_group_count=x.shape[-1])

def quad_shift(p, rows, width):
    B, T, C = p.shape
    g = p.reshape(B, rows, width, C // 4, 4)
    left = jnp.pad(g[:, :, :-1, :, 0], ((0, 0), (0, 0), (1, 0), (0, 0)))
    right = jnp.pad(g[:, :, 1:, :, 1], ((0, 0), (0, 0), (0, 1), (0, 0)))
    up = jnp.pad(g[:, :-1, :, :, 2], ((0, 0), (1, 0), (0, 0), (0, 0)))
    down = jnp.pad(g[:, 1:, :, :, 3], ((0, 0), (0, 1), (0, 0), (0, 0)))
    return jnp.stack([left, right, up, down], -1).reshape(B, T, C)

def time_major_dirs(x):
    x = jnp.stack([x[0], jnp.flip(x[1], 1)])
    x = x.reshape((-1,) + x.shape[2:])
    return jnp.moveaxis(x, 1, 0).astype(jnp.float32)

def sum_dirs(y, batch):
    y = jnp.moveaxis(y, 0, 1)
    y = y.reshape((2, batch) + y.shape[1:])
    return y[0] + jnp.flip(y[1], 1)

def dir_major(x):
    x = jnp.stack([x[0], jnp.flip(x[1], 1)])
    x = jnp.moveaxis(x, 3, 2)
    return x.reshape((-1,) + x.shape[3:]).astype(jnp.float32)

def both_dirs(t):
    return jnp.broadcast_to(t, (2,) + t.shape)

def rwkv7_scan(r, decay, k, v, kk, b, s0):
    def step(s, inp):
        r_t, w_t, k_t, v_t, kk_t, b_t = inp
        sa = jnp.einsum('zhij,zhj->zhi', s, kk_t)
        s = s * w_t[:, :, None, :] - sa[..., None] * b_t[:, :, None, :] + v_t[..., None] * k_t[:, :, None, :]
        return s, jnp.einsum('zhij,zhj->zhi', s, r_t)
    return lax.scan(step, s0, (r, decay, k, v, kk, b))

def rwkv7_mix(p, rows, width, s0, mu, w0, w2, a0, a2, g2, k_k, k_a, r_k, gn_g, gn_b):
    B, T, _ = p.shape
    p = p + mu * (quad_shift(p, rows, width) - p)
    r, k, v, xw, xa, xg = jnp.split(p, RWKV_SPLITS, axis=-1)
    gate = jax.nn.sigmoid(xg) @ g2
    kk = l2_normalize(split_heads(k * k_k))
    w_log = w0[:, None, None] + jnp.einsum('btr,drw->dbtw', jnp.tanh(xw), w2)
    decay = jnp.exp(-jnp.exp(-jax.nn.softplus(-w_log.astype(jnp.float32)) - 0.5))
    a = jax.nn.sigmoid(a0[:, None, None] + jnp.einsum('btr,drw->dbtw', xa, a2))
    kd = k * (1.0 + (a - 1.0) * k_a)
    r_h, v_h, kd_h, a_h = split_heads(r), split_heads(v), split_heads(kd), split_heads(a)
    s, y = rwkv7_scan(time_major_dirs(both_dirs(r_h)), time_major_dirs(split_heads(decay)),
                      time_major_dirs(kd_h), time_major_dirs(both_dirs(v_h)),
                      time_major_dirs(both_dirs(kk)), time_major_dirs(kk * a_h), s0)
    y = sum_dirs(layer_norm(y, gn_g, gn_b), B)
    bonus = jnp.sum(r_h * kd_h * r_k, -1, keepdims=True).sum(0) * v_h
    out = (y.astype(p.dtype) + bonus).reshape(B, T, BRANCH_W) * gate
    return out, s

def gated_delta_chunked(q, k, v, g, beta, s0):
    Z, T, dk = q.shape
    dv = v.shape[-1]
    C = GDN_CHUNK
    n = T // C
    q = q.reshape(Z, n, C, dk) * (dk ** -0.5)
    k = k.reshape(Z, n, C, dk)
    v = v.reshape(Z, n, C, dv)
    beta = beta.reshape(Z, n, C, 1)
    gc = jnp.cumsum(g.reshape(Z, n, C), -1)
    incl = jnp.tril(jnp.ones((C, C), bool))
    strict = jnp.tril(jnp.ones((C, C), bool), -1)
    diff = gc[..., :, None] - gc[..., None, :]
    gamma = jnp.where(incl, jnp.exp(jnp.where(incl, diff, 0.0)), 0.0)
    kb = k * beta
    lower = jnp.where(strict, jnp.einsum('znid,znjd->znij', kb, k) * gamma, 0.0)
    rhs = jnp.concatenate([v * beta, kb * jnp.exp(gc)[..., None]], -1)
    sol = lax.linalg.triangular_solve(lower, rhs, left_side=True, lower=True, unit_diagonal=True)
    u, w = sol[..., :dv], sol[..., dv:]
    intra = jnp.einsum('znid,znjd->znij', q, k) * gamma
    qg = q * jnp.exp(gc)[..., None]
    kg = k * jnp.exp(gc[..., -1:] - gc)[..., None]
    glast = jnp.exp(gc[..., -1])

    def step(s, xs):
        qg_i, kg_i, u_i, w_i, intra_i, gl_i = xs
        v_new = u_i - jnp.einsum('zcd,zde->zce', w_i, s)
        o = jnp.einsum('zcd,zde->zce', qg_i, s) + jnp.einsum('zcs,zse->zce', intra_i, v_new)
        s = s * gl_i[:, None, None] + jnp.einsum('zcd,zce->zde', kg_i, v_new)
        return s, o

    xs = tuple(jnp.moveaxis(t, 1, 0) for t in (qg, kg, u, w, intra, glast))
    s, o = lax.scan(step, s0, xs)
    return jnp.moveaxis(o, 0, 1).reshape(Z, T, dv), s

def gdn_mix(p, s0, conv_w, a_log, dt_bias, norm_g):
    B, T, _ = p.shape
    qkv, z, a, b = jnp.split(p, GDN_SPLITS, axis=-1)
    qkv = jax.nn.silu(depthwise_conv(qkv, conv_w))
    q, k, v = (split_heads(t) for t in jnp.split(qkv, 3, axis=-1))
    q, k = l2_normalize(q), l2_normalize(k)
    a = jnp.moveaxis(a.reshape(B, T, 2, N_HEADS), 2, 0).astype(jnp.float32)
    b = jnp.moveaxis(b.reshape(B, T, 2, N_HEADS), 2, 0).astype(jnp.float32)
    g = -jnp.exp(a_log)[:, None, None] * jax.nn.softplus(a + dt_bias[:, None, None])
    beta = jax.nn.sigmoid(b)
    o, s = gated_delta_chunked(dir_major(both_dirs(q)), dir_major(both_dirs(k)), dir_major(both_dirs(v)),
                               dir_major(g), dir_major(beta), s0)
    o = jnp.swapaxes(o.reshape(2, B, N_HEADS, T, HEAD_DIM), 2, 3)
    o = o[0] + jnp.flip(o[1], 1)
    out = rms_norm(o, norm_g) * jax.nn.silu(split_heads(z).astype(jnp.float32))
    return out.reshape(B, T, BRANCH_W).astype(p.dtype), s

def sgu_mix(p, ln_g, ln_b, w_s, b_s):
    B, T, _ = p.shape
    u, v = jnp.split(jax.nn.gelu(p), 2, axis=-1)
    v = layer_norm(v, ln_g, ln_b).reshape(B, T // SGU_CHUNK, SGU_CHUNK, N_HEADS, HEAD_DIM)
    sv = jnp.einsum('gps,bnsgc->bnpgc', w_s, v) + b_s.T[:, :, None]
    return u * sv.reshape(B, T, BRANCH_W)

def conformer_mix(p, dw_w, dw_b, ln_g, ln_b):
    val, gate = jnp.split(p, 2, axis=-1)
    y = depthwise_conv(val * jax.nn.sigmoid(gate), dw_w) + dw_b
    return jax.nn.silu(layer_norm(y, ln_g, ln_b))

def merge_branches(branches, gate_pre, w_branch, w_out):
    gates = jnp.split(gate_pre, N_BRANCH, axis=-1)
    m = jax.nn.sigmoid(gates[0]) * (branches[0] @ w_branch[0])
    for i in range(1, N_BRANCH):
        m = m + jax.nn.sigmoid(gates[i]) * (branches[i] @ w_branch[i])
    return m @ w_out

def peer_ffn(h, w_q, sub_keys, expert_u, expert_v):
    M, D = h.shape
    half = PEER_DKEY // 2

    def block(hb):
        t = hb.shape[0]
        q = (hb @ w_q).reshape(t, PEER_HEADS, 2, half)
        s = jnp.einsum('thpd,hpkd->thpk', q, sub_keys).astype(jnp.float32)
        s_top, i_top = lax.top_k(s, PEER_TOPK)
        cand = s_top[..., 0, :, None] + s_top[..., 1, None, :]
        cidx = i_top[..., 0, :, None] * PEER_NKEYS + i_top[..., 1, None, :]
        best, pos = lax.top_k(cand.reshape(t, PEER_HEADS, -1), PEER_TOPK)
        idx = jnp.take_along_axis(cidx.reshape(t, PEER_HEADS, -1), pos, -1)
        gate = jax.nn.softmax(best, -1)
        act = jax.nn.gelu(jnp.einsum('td,thkd->thk', hb, expert_u[idx]))
        coef = (gate * act).astype(hb.dtype)
        return jnp.einsum('thk,thkd->td', coef, expert_v[idx])

    return lax.map(block, h.reshape(M // PEER_BLOCK, PEER_BLOCK, D)).reshape(M, D)

def setup_inputs(seed: int = 0) -> dict:
    key = jax.random.key(seed)
    keys = iter(jax.random.split(key, 64))

    def normal(shape, std):
        return std * jax.random.normal(next(keys), shape, jnp.float32)

    def uniform(shape, lo, hi):
        return jax.random.uniform(next(keys), shape, jnp.float32, lo, hi)

    def gain(shape):
        return 1.0 + normal(shape, 0.05)

    L, D, W, H, N = DEPTH, D_MODEL, BRANCH_W, N_HEADS, HEAD_DIM
    dt = jnp.exp(uniform((L, 2, H), math.log(1e-3), math.log(1e-1)))
    return {
        'x': normal((BATCH, SEQ, D), 1.0),
        'c': normal((BATCH, D), 1.0),
        'ctx': normal((BATCH, CTX_LEN, D), 1.0),
        'c_ctx': normal((D,), 1.0),
        'w_ada': normal((L, D, 6 * D), 0.5 * D ** -0.5),
        'b_ada': normal((L, 6 * D), 0.02),
        'norm1_g': gain((L, D)),
        'norm2_g': gain((L, D)),
        'w_in': normal((L, D, IN_COLS), D ** -0.5),
        'rwkv_mu': uniform((L, RWKV_COLS), 0.0, 1.0),
        'rwkv_w0': uniform((L, 2, W), -3.0, 1.0),
        'rwkv_w2': normal((L, 2, RWKV_W_RANK, W), 0.5 * RWKV_W_RANK ** -0.5),
        'rwkv_a0': normal((L, 2, W), 0.5),
        'rwkv_a2': normal((L, 2, RWKV_A_RANK, W), 0.5 * RWKV_A_RANK ** -0.5),
        'rwkv_g2': normal((L, RWKV_G_RANK, W), RWKV_G_RANK ** -0.5),
        'rwkv_k_k': 0.85 + normal((L, W), 0.05),
        'rwkv_k_a': gain((L, W)),
        'rwkv_r_k': normal((L, H, N), 0.1),
        'rwkv_gn_g': gain((L, H, N)),
        'rwkv_gn_b': normal((L, H, N), 0.02),
        'gdn_conv_w': normal((L, GDN_CONV, 3 * W), GDN_CONV ** -0.5),
        'gdn_a_log': jnp.log(uniform((L, 2, H), 1.0, 16.0)),
        'gdn_dt_bias': dt + jnp.log(-jnp.expm1(-dt)),
        'gdn_norm_g': gain((L, N)),
        'sgu_ln_g': gain((L, W)),
        'sgu_ln_b': normal((L, W), 0.02),
        'sgu_w_s': normal((L, H, SGU_CHUNK, SGU_CHUNK), 0.5 * SGU_CHUNK ** -0.5),
        'sgu_b_s': 1.0 + normal((L, H, SGU_CHUNK), 0.1),
        'conf_dw_w': normal((L, CONV_W, W), CONV_W ** -0.5),
        'conf_dw_b': normal((L, W), 0.02),
        'conf_ln_g': gain((L, W)),
        'conf_ln_b': normal((L, W), 0.02),
        'w_branch': normal((L, N_BRANCH, W, D), W ** -0.5),
        'w_out': normal((L, D, D), D ** -0.5),
        'peer_w_q': normal((L, D, PEER_HEADS * PEER_DKEY), D ** -0.5),
        'peer_keys': normal((L, PEER_HEADS, 2, PEER_NKEYS, PEER_DKEY // 2), (PEER_DKEY // 2) ** -0.5),
        'peer_u': normal((L, PEER_EXPERTS, D), D ** -0.5),
        'peer_v': normal((L, PEER_EXPERTS, D), PEER_HEADS ** -0.5),
        'final_g': gain((D,)),
    }

def reference(x, c, ctx, c_ctx, w_ada, b_ada, norm1_g, norm2_g, w_in,
              rwkv_mu, rwkv_w0, rwkv_w2, rwkv_a0, rwkv_a2, rwkv_g2, rwkv_k_k, rwkv_k_a, rwkv_r_k,
              rwkv_gn_g, rwkv_gn_b, gdn_conv_w, gdn_a_log, gdn_dt_bias, gdn_norm_g,
              sgu_ln_g, sgu_ln_b, sgu_w_s, sgu_b_s, conf_dw_w, conf_dw_b, conf_ln_g, conf_ln_b,
              w_branch, w_out, peer_w_q, peer_keys, peer_u, peer_v, final_g):
    B, T, D = x.shape
    n_ctx = ctx.shape[1]
    rows = T // GRID_W
    silu_c = jax.nn.silu(c)
    silu_cc = jax.nn.silu(c_ctx)
    xc = ctx

    def token_mix(h, rows_, width_, s_r, s_g, l, states_only):
        p_r, p_g, p_s, p_c, p_gate = jnp.split(h @ w_in[l], IN_SPLITS, axis=-1)
        o_r, s_r = rwkv7_mix(p_r, rows_, width_, s_r, rwkv_mu[l], rwkv_w0[l], rwkv_w2[l], rwkv_a0[l],
                             rwkv_a2[l], rwkv_g2[l], rwkv_k_k[l], rwkv_k_a[l], rwkv_r_k[l],
                             rwkv_gn_g[l], rwkv_gn_b[l])
        o_g, s_g = gdn_mix(p_g, s_g, gdn_conv_w[l], gdn_a_log[l], gdn_dt_bias[l], gdn_norm_g[l])
        if states_only:
            return None, s_r, s_g
        o_s = sgu_mix(p_s, sgu_ln_g[l], sgu_ln_b[l], sgu_w_s[l], sgu_b_s[l])
        o_c = conformer_mix(p_c, conf_dw_w[l], conf_dw_b[l], conf_ln_g[l], conf_ln_b[l])
        y = merge_branches((o_r, o_g, o_s, o_c), p_gate, w_branch[l], w_out[l])
        return y, s_r, s_g

    for l in range(DEPTH):
        last = l == DEPTH - 1
        m = [t[:, None] for t in jnp.split(silu_c @ w_ada[l] + b_ada[l], 6, axis=-1)]
        mc = jnp.split(silu_cc @ w_ada[l] + b_ada[l], 6, axis=-1)
        s_r0 = jnp.zeros((2 * B, N_HEADS, HEAD_DIM, HEAD_DIM), jnp.float32)
        s_g0 = jnp.zeros((2 * B * N_HEADS, HEAD_DIM, HEAD_DIM), jnp.float32)

        hc = modulate(xc, norm1_g[l], mc[0], mc[1])
        yc, s_r, s_g = token_mix(hc, 1, n_ctx, s_r0, s_g0, l, last)

        h = modulate(x, norm1_g[l], m[0], m[1])
        y, _, _ = token_mix(h, rows, GRID_W, s_r, s_g, l, False)
        x = x + m[2] * y
        h2 = modulate(x, norm2_g[l], m[3], m[4])

        if last:
            x = x + m[5] * peer_ffn(h2.reshape(-1, D), peer_w_q[l], peer_keys[l], peer_u[l], peer_v[l]).reshape(B, T, D)
        else:
            xc = xc + mc[2] * yc
            hc2 = modulate(xc, norm2_g[l], mc[3], mc[4])
            rows_all = jnp.concatenate([hc2.reshape(-1, D), h2.reshape(-1, D)], 0)
            f = peer_ffn(rows_all, peer_w_q[l], peer_keys[l], peer_u[l], peer_v[l])
            xc = xc + mc[5] * f[:B * n_ctx].reshape(B, n_ctx, D)
            x = x + m[5] * f[B * n_ctx:].reshape(B, T, D)

    return rms_norm(x, final_g)


_drawn_inputs = setup_inputs


def setup_inputs(seed=0):
    import zlib

    import numpy as np

    out = dict(_drawn_inputs(seed))
    spreads = {}
    factors = {'c_ctx': 3.177,
     'norm2_g': 2.915,
     'rwkv_w2': 3.388,
     'rwkv_k_k': 5.964,
     'rwkv_k_a': 3.658,
     'rwkv_gn_g': 4.42,
     'rwkv_gn_b': 7.66,
     'gdn_norm_g': 4.878,
     'sgu_ln_g': 8.0,
     'sgu_ln_b': 33.109,
     'sgu_b_s': 3.035,
     'conf_dw_b': 7.417,
     'conf_ln_g': 4.849,
     'conf_ln_b': 8.0}
    for name, (base, spread) in spreads.items():
        noise = np.random.default_rng([zlib.crc32(name.encode()), seed]).standard_normal(out[name].shape)
        drawn = base * np.exp(spread * noise) if base else spread * noise
        out[name] = jnp.asarray(drawn.astype(out[name].dtype))
    for name, factor in factors.items():
        out[name] = (out[name] * factor).astype(out[name].dtype)
    return out
```

```python
from contextlib import ExitStack

import numpy as np
import concourse.bass as bass
from concourse import mybir

ALU = mybir.AluOpType
ACT = mybir.ActivationFunctionType
F32 = mybir.dt.float32
U32 = mybir.dt.uint32
AX_X = mybir.AxisListType.X

P = 128
D = 1024
KD = D // P
W = 256
WT = W // P
H = 4
HD = W // H
CTX, SEQ = 256, 512
T = CTX + SEQ
TT = T // P
CT = CTX // P
GW = 64
GR = SEQ // GW
C = 64
LEVELS = 6
EPS = 1e-6
DECAY = float(np.exp(-0.5))
DEPTH = 2

RWKV0, GDN0 = 0, 1024
AB0, SGU0, CONF0, GATE0 = 2048, 2064, 2576, 3088

HEADS = 8
NKEYS = 128
EXPERTS = NKEYS * NKEYS
TOPK = 16
PICKS = HEADS * TOPK
RING = 16
NEG = -3.0e38

CONV_G, CONV_C = 5, 31

IDENT, ONES, BLK = 0, 128, 256
MASKS = 384
NMI = MASKS + 4 * P
CHUNK = NMI + 2 * P
LEVEL = CHUNK + 2 * P
QUAD = LEVEL + 2 * LEVELS * P
IOTA = QUAD + 4
NCONST = IOTA + TOPK


class Program:
    pass


def constants():
    s, t = np.arange(P)[:, None], np.arange(P)[None, :]
    same = s // C == t // C
    cols = [s == t, np.ones((P, P)), s // HD == t // HD]
    for later, strictly in ((s <= t, s < t), (s >= t, s > t)):
        cols += [same & later, same & strictly]
    cols += [-1.0 * (same & (s <= t)), -1.0 * (same & (s >= t))]
    cols += [(s // C == c) & (t >= 0) for c in range(2)]
    for k in range(LEVELS):
        b = 1 << k
        fwd = (s // (2 * b) == t // (2 * b)) & (s // b % 2 == 0) & (t // b % 2 == 1)
        cols += [fwd, fwd.T]
    cols += [s % 4 == np.arange(4)[None, :], np.broadcast_to(np.arange(TOPK)[None, :], (P, TOPK))]
    out = np.concatenate([np.asarray(c, np.float32) for c in cols], 1)
    assert out.shape == (P, NCONST)
    return out


def sbuf(nc, name, shape, dt=F32):
    return nc.sbuf_tensor(f"{name}_{nc.next_id()}", shape, dt)


def psum(nc, name, shape, dt=F32):
    return nc.psum_tensor(f"{name}_{nc.next_id()}", shape, dt)


class Line:

    def __init__(self, eng, chain, pace):
        self.eng, self.chain, self.pace, self.n = eng, chain, pace, 0

    def link(self, ins):
        self.n += 1
        ins.then_inc(self.chain, 1)
        self.eng.wait_ge(self.chain, self.n)

    def restart(self):
        if self.n:
            self.eng.sem_inc(self.chain, -self.n)
            self.n = 0

    def hold(self, sem, value):
        self.eng.wait_ge(sem, value)
        if not isinstance(value, int):
            self.eng.sem_inc(self.pace, 1)

    def tell(self, sem, n=1):
        self.eng.sem_inc(sem, n)

    def credit(self, *sems):
        for sem in sems:
            self.eng.sem_inc(sem, 1)


ENGINES = ("pe", "act", "dve", "pool", "sp")


class Stage:

    def __init__(self, nc, name, sems=""):
        self.nc, self.name, self.names = nc, name, sems.split()

    def __enter__(self):
        self.ctx = ExitStack()
        made = {n: self.ctx.enter_context(self.nc.semaphore(f"{self.name}_{n}"))
                for n in self.names + [f"chain_{e}" for e in ENGINES] + [f"pace_{e}" for e in ENGINES]}
        self.sem = made
        self.block = self.nc.Block()
        self.body = self.block.__enter__()
        return self

    def line(self, eng, name):
        return Line(eng, self.sem[f"chain_{name}"], self.sem[f"pace_{name}"])

    def __exit__(self, *e):
        self.block.__exit__(*e)
        if e[0] is None:
            with self.nc.Block() as clear:
                @clear.gpsimd
                def _(pool):
                    for s in self.sem.values():
                        pool.sem_clear(s)
        self.ctx.close()


SEG_ALL = ((0, CTX, 1), (CTX, T, 0))
SEG_X = ((CTX, T, 0),)


def load_tokens(nc, g):
    with ExitStack() as mem, Stage(nc, "load", "rows_in turned moved consts_in") as s:
        rows = mem.enter_context(sbuf(nc, "rows", [P, TT, D], F32))
        ps = [mem.enter_context(psum(nc, f"ld{i}", [P, 4, P], F32)) for i in range(2)]
        q = s.sem

        @s.body.sync
        def _(sp):
            sp.dma_start(g.cst[:, :], g.consts).then_inc(q["consts_in"], 16)
            sp.dma_start(rows[:, 0:CT, :], g.ctx[0].rearrange("(t p) d -> p t d", p=P)).then_inc(q["rows_in"], 16)
            sp.dma_start(rows[:, CT:TT, :], g.x[0].rearrange("(t p) d -> p t d", p=P)).then_inc(q["rows_in"], 16)

        @s.body.tensor
        def _(pe):
            pe.wait_ge(q["consts_in"], 16)
            pe.wait_ge(q["rows_in"], 32)
            for n in range(TT * 2):
                if n >= 2:
                    pe.wait_ge(q["moved"], n - 1)
                for j in range(4):
                    k = n % 2 * 4 + j
                    last = pe.transpose(ps[n % 2][:, j, :], rows[:, n // 2, k * P:(k + 1) * P], g.c(IDENT))
                last.then_inc(q["turned"], 1)

        @s.body.vector
        def _(v):
            for n in range(TT * 2):
                v.wait_ge(q["turned"], n + 1)
                v.tensor_copy(g.xT[:, n % 2 * 4:n % 2 * 4 + 4, n // 2 * P:(n // 2 + 1) * P],
                              ps[n % 2][:, :, :]).then_inc(q["moved"], 1)

    with Stage(nc, "cond", "cond_in sig_ready") as s:
        q = s.sem

        @s.body.sync
        def _(sp):
            with nc.allow_non_contiguous_dma(reason="2048 numbers, once"):
                sp.dma_start(g.cond[:, :, 0], g.cvec.rearrange("a (k p) -> p (a k)", p=P)).then_inc(q["cond_in"], 16)
                sp.dma_start(g.cond[:, :, 1], g.c_ctx.rearrange("(k p) -> p k", p=P)).then_inc(q["cond_in"], 16)

        @s.body.scalar
        def _(act):
            act.wait_ge(q["cond_in"], 32)
            act.activation(g.cond_sig[:, :, :], g.cond[:, :, :], ACT.Sigmoid).then_inc(q["sig_ready"], 1)

        @s.body.vector
        def _(v):
            v.wait_ge(q["sig_ready"], 1)
            ln = s.line(v, "dve")
            ln.link(v.tensor_tensor(g.cond[:, :, :], g.cond[:, :, :], g.cond_sig[:, :, :], ALU.mult))


def ada(nc, g, l):
    SLAB = 4 * P
    with ExitStack() as mem, Stage(nc, f"ada{l}", "w0_in w1_in w0_used w1_used full0 full1 free0 free1 vec_in") as s:
        wt = [mem.enter_context(sbuf(nc, f"ada_w{i}", [P, KD, SLAB], F32)) for i in range(2)]
        bias = mem.enter_context(sbuf(nc, "ada_b", [P, 6 * KD], F32))
        gain = mem.enter_context(sbuf(nc, "ada_g", [P, 2, KD], F32))
        ps = [mem.enter_context(psum(nc, f"ada_p{i}", [P, 512], F32)) for i in range(2)]
        q = s.sem
        w_in, w_used, full, free = [q["w0_in"], q["w1_in"]], [q["w0_used"], q["w1_used"]], [q["full0"], q["full1"]], [q["free0"], q["free1"]]
        rounds = 6 * D // SLAB // 2

        @s.body.sync
        def _(sp):
            ln = s.line(sp, "sp")
            with nc.allow_non_contiguous_dma(reason="vectors onto partitions"):
                sp.dma_start(bias[:, :], g.b_ada[l].rearrange("(j p) -> p j", p=P)).then_inc(q["vec_in"], 16)
                sp.dma_start(gain[:, 0, :], g.norm1_g[l].rearrange("(j p) -> p j", p=P)).then_inc(q["vec_in"], 16)
                sp.dma_start(gain[:, 1, :], g.norm2_g[l].rearrange("(j p) -> p j", p=P)).then_inc(q["vec_in"], 16)
            w = g.w_ada[l].rearrange("(k p) n -> p k n", p=P)
            with sp.Fori(0, rounds) as i:
                for j in range(2):
                    ln.hold(w_used[j], i + 1)
                    sp.dma_start(wt[j][:, :, :], w[:, :, bass.ds(i * (2 * SLAB) + j * SLAB, SLAB)]).then_inc(w_in[j], 16)

        @s.body.tensor
        def _(pe):
            ln = s.line(pe, "pe")
            ln.credit(*w_used)
            with pe.Fori(0, rounds) as i:
                for j in range(2):
                    ln.hold(w_in[j], i * 16 + 16)
                    ln.hold(free[j], i + 1)
                    for m in range(4):
                        for k in range(KD):
                            last = pe.matmul(ps[j][:, 2 * m:2 * m + 2], wt[j][:, k, m * P:(m + 1) * P],
                                             g.cond[:, k, :], start=k == 0, stop=k == KD - 1)
                    last.then_inc(full[j], 1)
                    ln.hold(full[j], i + 1)
                    ln.tell(w_used[j])

        @s.body.vector
        def _(v):
            ln = s.line(v, "dve")
            ln.credit(*free)
            v.wait_ge(q["vec_in"], 48)
            with v.Fori(0, rounds) as i:
                for j in range(2):
                    ln.hold(full[j], i + 1)
                    at = bass.ds(i * 8 + j * 4, 4)
                    ln.link(v.tensor_tensor(g.mods[:, at, :], ps[j][:, 0:8].rearrange("p (m v) -> p m v", v=2),
                                            bias[:, at].unsqueeze(2).broadcast_to([P, 4, 2]), ALU.add))
                    ln.tell(free[j])
                ln.restart()
            for n in range(2):
                sc = g.mods[:, (3 * n + 1) * KD:(3 * n + 2) * KD, :]
                ln.link(v.tensor_scalar(g.gs[:, n, :, :], sc, 1.0, None, ALU.add))
                ln.link(v.tensor_tensor(g.gs[:, n, :, :], g.gs[:, n, :, :],
                                        gain[:, n, :].unsqueeze(2).broadcast_to([P, KD, 2]), ALU.mult))


def norm(nc, g, name, segs, which, gain=None):
    with ExitStack() as mem, Stage(nc, name, "sq_ready sq_used mean_ready rstd_ready scaled gain_in") as s:
        sq = [mem.enter_context(sbuf(nc, f"sq{i}", [P, T], F32)) for i in range(2)]
        rs = mem.enter_context(sbuf(nc, "rs", [P, T], F32))
        fg = mem.enter_context(sbuf(nc, "fg", [P, KD], F32))
        ps = [mem.enter_context(psum(nc, f"np{i}", [P, 512], F32)) for i in range(len(segs))]
        q = s.sem
        lo, hi = segs[0][0], segs[-1][1]

        @s.body.sync
        def _(sp):
            if gain is not None:
                with nc.allow_non_contiguous_dma(reason="a vector onto partitions"):
                    sp.dma_start(fg[:, :], gain.rearrange("(j p) -> p j", p=P)).then_inc(q["gain_in"], 16)

        @s.body.scalar
        def _(act):
            ln = s.line(act, "act")
            for k in range(KD):
                if k >= 2:
                    act.wait_ge(q["sq_used"], k - 1)
                ln.link(act.activation(sq[k % 2][:, lo:hi], g.xT[:, k, lo:hi], ACT.Square))
                ln.tell(q["sq_ready"])
            act.wait_ge(q["mean_ready"], 1)
            ln.link(act.activation(rs[:, lo:hi], rs[:, lo:hi], ACT.Sqrt))
            ln.tell(q["rstd_ready"])
            if gain is not None:
                act.wait_ge(q["gain_in"], 16)
            for k in range(KD):
                act.wait_ge(q["scaled"], k + 1)
                for a, b, v in segs:
                    if gain is None:
                        ln.link(act.activation(g.hT[:, k, a:b], g.hT[:, k, a:b], ACT.Identity,
                                               scale=g.gs[:, which, k, v:v + 1],
                                               bias=g.mods[:, 3 * which * KD + k, v:v + 1]))
                    else:
                        ln.link(act.activation(g.hT[:, k, a:b], g.hT[:, k, a:b], ACT.Copy, scale=fg[:, k:k + 1]))

        @s.body.tensor
        def _(pe):
            for k in range(KD):
                pe.wait_ge(q["sq_ready"], k + 1)
                for n, (a, b, v) in enumerate(segs):
                    last = pe.matmul(ps[n][:, 0:b - a], g.c(ONES), sq[k % 2][:, a:b], start=k == 0, stop=k == KD - 1)
                last.then_inc(q["sq_used"], 1)

        @s.body.vector
        def _(v):
            ln = s.line(v, "dve")
            v.wait_ge(q["sq_used"], KD)
            for n, (a, b, _) in enumerate(segs):
                ln.link(v.tensor_scalar(rs[:, a:b], ps[n][:, 0:b - a], 1.0 / D, EPS, ALU.mult, ALU.add))
            ln.link(v.reciprocal(rs[:, lo:hi], rs[:, lo:hi]))
            ln.tell(q["mean_ready"])
            v.wait_ge(q["rstd_ready"], 1)
            for k in range(KD):
                ln.link(v.tensor_tensor(g.hT[:, k, lo:hi], g.xT[:, k, lo:hi], rs[:, lo:hi], ALU.mult))
                ln.tell(q["scaled"])


def project(nc, g, name, w, tiles, rhs, segs, out=None, residual=None):
    with ExitStack() as mem, Stage(nc, name, "w0_in w1_in w0_used w1_used full0 full1 full2 full3 a0 a1 a2 a3 v0 v1 v2 v3") as s:
        wt = [mem.enter_context(sbuf(nc, f"w{i}", [P, KD, 2 * P], F32)) for i in range(2)]
        ps = [mem.enter_context(psum(nc, f"pp{i}", [P, 512], F32)) for i in range(8)]
        q = s.sem
        w_in, w_used = [q["w0_in"], q["w1_in"]], [q["w0_used"], q["w1_used"]]
        full, a_free, v_free = [q["full0"], q["full1"], q["full2"], q["full3"]], [q["a0"], q["a1"], q["a2"], q["a3"]], [q["v0"], q["v1"], q["v2"], q["v3"]]
        rounds = tiles // 4
        both = len(segs) == 2 and residual is None

        @s.body.sync
        def _(sp):
            ln = s.line(sp, "sp")
            wv = w.rearrange("(k p) n -> p k n", p=P)
            with sp.Fori(0, rounds) as i:
                for j in range(2):
                    ln.hold(w_used[j], i + 1)
                    sp.dma_start(wt[j][:, :, :], wv[:, :, bass.ds(i * (4 * P) + j * 2 * P, 2 * P)]).then_inc(w_in[j], 16)

        @s.body.tensor
        def _(pe):
            ln = s.line(pe, "pe")
            ln.credit(*w_used)
            with pe.Fori(0, rounds) as i:
                for j in range(4):
                    if j % 2 == 0:
                        ln.hold(w_in[j // 2], i * 16 + 16)
                    if both:
                        ln.hold(a_free[j], i + 1)
                    ln.hold(v_free[j], i + 1)
                    for n, (a, b, _) in enumerate(segs):
                        for k in range(KD):
                            last = pe.matmul(ps[2 * j + n][:, 0:b - a], wt[j // 2][:, k, j % 2 * P:(j % 2 + 1) * P],
                                             rhs[:, k, a:b], start=k == 0, stop=k == KD - 1)
                    last.then_inc(full[j], 1)
                    if j % 2:
                        ln.hold(full[j], i + 1)
                        ln.tell(w_used[j // 2])

        if both:
            @s.body.scalar
            def _(act):
                ln = s.line(act, "act")
                ln.credit(*a_free)
                with act.Fori(0, rounds) as i:
                    for j in range(4):
                        a, b, _ = segs[0]
                        ln.hold(full[j], i + 1)
                        ln.link(act.activation(out[:, bass.ds(i * 4 + j, 1), a:b], ps[2 * j][:, 0:b - a].unsqueeze(1), ACT.Copy))
                        ln.tell(a_free[j])
                    ln.restart()

        @s.body.vector
        def _(v):
            ln = s.line(v, "dve")
            ln.credit(*v_free)
            with v.Fori(0, rounds) as i:
                for j in range(4):
                    ln.hold(full[j], i + 1)
                    for n, (a, b, c) in enumerate(segs):
                        tile = bass.ds(i * 4 + j, 1)
                        if residual is not None:
                            ln.link(v.scalar_tensor_tensor(
                                g.xT[:, tile, a:b], ps[2 * j + n][:, 0:b - a].unsqueeze(1),
                                g.mods[:, bass.ds(i * 4 + j + residual * KD, 1), c:c + 1],
                                g.xT[:, tile, a:b], ALU.mult, ALU.add))
                        elif n or not both:
                            ln.link(v.tensor_copy(out[:, tile, a:b], ps[2 * j + n][:, 0:b - a].unsqueeze(1)))
                    ln.tell(v_free[j])
                ln.restart()


def normalize(nc, g, name, x, const, factor, center=False, pooled=False):
    G = x.shape[1]
    per = 2 if pooled else 1
    units = G // per
    HALF = T // 2
    with ExitStack() as mem, Stage(nc, name, "asked summed used sums_read root_asked root_done") as s:
        sq = mem.enter_context(sbuf(nc, "nsq", [P, 2, per, T]))
        rs = mem.enter_context(sbuf(nc, "nrs", [P, 2, T]))
        ps = [[mem.enter_context(psum(nc, "nps", [P, 512])) for _ in range(2)] for _ in range(2)]
        q = s.sem
        passes = 2 if center else 1

        @s.body.tensor
        def _(pe):
            n = 0
            for ps_no in range(passes):
                for u in range(units):
                    pe.wait_ge(q["asked"], n + 1)
                    if n >= 2:
                        pe.wait_ge(q["sums_read"], n - 1)
                    for half in range(2):
                        for j in range(per):
                            src = x[:, u * per + j, :] if center and ps_no == 0 else sq[:, u % 2, j, :]
                            last = pe.matmul(ps[n % 2][half][:, 0:HALF], g.c(const), src[:, half * HALF:(half + 1) * HALF],
                                             start=j == 0, stop=j == per - 1)
                    last.then_inc(q["summed"], 1)
                    n += 1

        @s.body.vector
        def _(v):
            ln = s.line(v, "dve")
            n = 0
            if center:
                ln.tell(q["asked"], units)
                for u in range(units):
                    v.wait_ge(q["summed"], n + 1)
                    for half in range(2):
                        cut = slice(half * HALF, (half + 1) * HALF)
                        for j in range(per):
                            xs = x[:, u * per + j, cut]
                            ln.link(v.scalar_tensor_tensor(xs, ps[n % 2][half][:, 0:HALF], -factor, xs, ALU.mult, ALU.add))
                    ln.tell(q["sums_read"])
                    n += 1

            def square(u):
                for j in range(per):
                    ln.link(v.tensor_tensor(sq[:, u % 2, j, :], x[:, u * per + j, :], x[:, u * per + j, :], ALU.mult))
                ln.tell(q["asked"])

            def scale(u):
                v.wait_ge(q["root_done"], u + 1)
                for j in range(per):
                    ln.link(v.tensor_tensor(x[:, u * per + j, :], x[:, u * per + j, :], rs[:, u % 2, :], ALU.mult))

            square(0)
            for u in range(units):
                v.wait_ge(q["summed"], n + 1)
                for half in range(2):
                    ln.link(v.tensor_scalar(rs[:, u % 2, half * HALF:(half + 1) * HALF], ps[n % 2][half][:, 0:HALF],
                                            factor, EPS, ALU.mult, ALU.add))
                ln.tell(q["sums_read"])
                n += 1
                ln.link(v.reciprocal(rs[:, u % 2, :], rs[:, u % 2, :]))
                ln.tell(q["root_asked"])
                if u + 1 < units:
                    square(u + 1)
                if u >= 1:
                    scale(u - 1)
            scale(units - 1)

        @s.body.scalar
        def _(act):
            ln = s.line(act, "act")
            for u in range(units):
                act.wait_ge(q["root_asked"], u + 1)
                ln.link(act.activation(rs[:, u % 2, :], rs[:, u % 2, :], ACT.Sqrt))
                ln.tell(q["root_done"])


PADC = CONV_C // 2
LONG = PADC + CTX + PADC + SEQ + PADC
X_AT = CTX + PADC


def conv(v, ln, out, padded, tap, taps, bias, pad):
    n = CTX + pad + SEQ
    order = [taps // 2] + [k for k in range(taps) if k != taps // 2]
    for k in order:
        src = padded[:, k:k + n]
        if k == taps // 2:
            if bias is None:
                ln.link(v.tensor_scalar(out[:, 0:n], src, tap(k), None, ALU.mult))
            else:
                ln.link(v.tensor_scalar(out[:, 0:n], src, tap(k), bias, ALU.mult, ALU.add))
        else:
            ln.link(v.scalar_tensor_tensor(out[:, 0:n], src, tap(k), out[:, 0:n], ALU.mult, ALU.add))


def conformer(nc, g, l):
    with ExitStack() as top:
        pc = top.enter_context(sbuf(nc, "conf_p", [P, 4, T]))
        y = top.enter_context(sbuf(nc, "conf_y", [P, WT, T]))
        vec = top.enter_context(sbuf(nc, "conf_v", [P, 3, WT]))
        project(nc, g, f"confp{l}", g.w_in[l][:, CONF0:CONF0 + 2 * W], 4, g.hT, SEG_ALL, out=pc)
        with ExitStack() as mem, Stage(nc, f"conf{l}", "vec_in sig_ready") as s:
            pad = mem.enter_context(sbuf(nc, "conf_pad", [P, WT, LONG]))
            acc = mem.enter_context(sbuf(nc, "conf_acc", [P, WT, LONG]))
            taps = mem.enter_context(sbuf(nc, "conf_w", [P, WT, CONV_C]))
            q = s.sem

            @s.body.sync
            def _(sp):
                with nc.allow_non_contiguous_dma(reason="small weights onto partitions"):
                    for n, a in enumerate((g.conf_dw_b, g.conf_ln_g, g.conf_ln_b)):
                        sp.dma_start(vec[:, n, :], a[l].rearrange("(t p) -> p t", p=P)).then_inc(q["vec_in"], 16)
                    for n in range(WT):
                        sp.dma_start(taps[:, n, :], g.conf_dw_w[l][:, n * P:(n + 1) * P].rearrange("k p -> p k")).then_inc(q["vec_in"], 16)

            @s.body.scalar
            def _(act):
                ln = s.line(act, "act")
                ln.link(act.activation(pc[:, 2:4, :], pc[:, 2:4, :], ACT.Sigmoid))
                ln.tell(q["sig_ready"])

            @s.body.vector
            def _(v):
                ln = s.line(v, "dve")
                ln.link(v.memset(pad[:, :, :], 0.0))
                v.wait_ge(q["sig_ready"], 1)
                ln.link(v.tensor_tensor(pad[:, :, PADC:PADC + CTX], pc[:, 0:2, 0:CTX], pc[:, 2:4, 0:CTX], ALU.mult))
                ln.link(v.tensor_tensor(pad[:, :, PADC + X_AT:PADC + X_AT + SEQ], pc[:, 0:2, CTX:T], pc[:, 2:4, CTX:T], ALU.mult))
                v.wait_ge(q["vec_in"], 80)
                for n in range(WT):
                    conv(v, ln, acc[:, n, :], pad[:, n, :], lambda k: taps[:, n, k:k + 1], CONV_C, vec[:, 0, n:n + 1], PADC)
                ln.link(v.tensor_copy(y[:, :, 0:CTX], acc[:, :, 0:CTX]))
                ln.link(v.tensor_copy(y[:, :, CTX:T], acc[:, :, X_AT:X_AT + SEQ]))
        normalize(nc, g, f"confn{l}", y[:, :, :], ONES, 1.0 / W, center=True, pooled=True)
        with ExitStack() as mem, Stage(nc, f"confo{l}", "lin_ready sig_ready") as s:
            sig = mem.enter_context(sbuf(nc, "conf_s", [P, WT, T]))
            q = s.sem

            @s.body.vector
            def _(v):
                ln = s.line(v, "dve")
                for n in range(WT):
                    ln.link(v.tensor_scalar(y[:, n, :], y[:, n, :], vec[:, 1, n:n + 1], vec[:, 2, n:n + 1], ALU.mult, ALU.add))
                    ln.tell(q["lin_ready"])
                for n in range(WT):
                    v.wait_ge(q["sig_ready"], n + 1)
                    ln.link(v.tensor_tensor(g.oT[:, 3, n, :], y[:, n, :], sig[:, n, :], ALU.mult))

            @s.body.scalar
            def _(act):
                ln = s.line(act, "act")
                for n in range(WT):
                    act.wait_ge(q["lin_ready"], n + 1)
                    ln.link(act.activation(sig[:, n, :], y[:, n, :], ACT.Sigmoid))
                    ln.tell(q["sig_ready"])


def sgu(nc, g, l):
    with ExitStack() as top:
        pc = top.enter_context(sbuf(nc, "sgu_p", [P, 4, T]))
        project(nc, g, f"sgup{l}", g.w_in[l][:, SGU0:SGU0 + 2 * W], 4, g.hT, SEG_ALL, out=pc)
        with Stage(nc, f"sgug{l}", "") as s:
            @s.body.scalar
            def _(act):
                ln = s.line(act, "act")
                ln.link(act.activation(pc[:, :, :], pc[:, :, :], ACT.Gelu_apprx_tanh))
        normalize(nc, g, f"sgun{l}", pc[:, 2:4, :], ONES, 1.0 / W, center=True, pooled=True)
        with ExitStack() as mem, Stage(nc, f"sgu{l}", "w_in turned moved mixed read lin_ready") as s:
            vec = mem.enter_context(sbuf(nc, "sgu_v", [P, 2, WT]))
            ws = mem.enter_context(sbuf(nc, "sgu_w", [P, H, P]))
            wsT = mem.enter_context(sbuf(nc, "sgu_wT", [P, H, P]))
            bs = mem.enter_context(sbuf(nc, "sgu_b", [1, H * P]))
            vt = mem.enter_context(sbuf(nc, "sgu_vt", [P, TT, W]))
            ps = [mem.enter_context(psum(nc, "sgu_ps", [P, 512])) for _ in range(4)]
            q = s.sem

            @s.body.sync
            def _(sp):
                with nc.allow_non_contiguous_dma(reason="small weights onto partitions"):
                    sp.dma_start(vec[:, 0, :], g.sgu_ln_g[l].rearrange("(t p) -> p t", p=P)).then_inc(q["w_in"], 16)
                    sp.dma_start(vec[:, 1, :], g.sgu_ln_b[l].rearrange("(t p) -> p t", p=P)).then_inc(q["w_in"], 16)
                sp.dma_start(ws[:, :, :], g.sgu_w_s[l].rearrange("g p s -> p g s")).then_inc(q["w_in"], 16)
                sp.dma_start(bs[:, :], g.sgu_b_s[l:l + 1].rearrange("a g p -> a (g p)")).then_inc(q["w_in"], 16)

            @s.body.tensor
            def _(pe):
                pe.wait_ge(q["w_in"], 64)
                for h in range(H):
                    last = pe.transpose(ps[0][:, h * P:(h + 1) * P], ws[:, h, :], g.c(IDENT))
                last.then_inc(q["turned"], 1)
                pe.wait_ge(q["lin_ready"], WT)
                for t in range(TT):
                    if t >= 1:
                        pe.wait_ge(q["moved"], t)
                    for n in range(WT):
                        last = pe.transpose(ps[(t + 1) % 2][:, n * P:(n + 1) * P], pc[:, 2 + n, t * P:(t + 1) * P], g.c(IDENT))
                    last.then_inc(q["turned"], 1)
                pe.wait_ge(q["moved"], TT + 1)
                for t in range(TT):
                    if t >= 2:
                        pe.wait_ge(q["read"], t - 1)
                    for h in range(H):
                        o = ps[2 + t % 2][h % 2 * HD:(h % 2 + 1) * HD, h // 2 * P:(h // 2 + 1) * P]
                        pe.matmul(o, vt[:, t, h * HD:(h + 1) * HD], wsT[:, h, :], start=True, stop=False)
                        last = pe.matmul(o, g.c(ONES)[0:1, 0:HD], bs[0:1, h * P:(h + 1) * P], start=False, stop=True)
                    last.then_inc(q["mixed"], 1)

            @s.body.vector
            def _(v):
                ln = s.line(v, "dve")
                v.wait_ge(q["w_in"], 64)
                for n in range(WT):
                    ln.link(v.tensor_scalar(pc[:, 2 + n, :], pc[:, 2 + n, :], vec[:, 0, n:n + 1], vec[:, 1, n:n + 1], ALU.mult, ALU.add))
                    ln.tell(q["lin_ready"])
                v.wait_ge(q["turned"], 1)
                ln.link(v.tensor_copy(wsT[:, :, :], ps[0][:, :].rearrange("p (h s) -> p h s", h=H)))
                ln.tell(q["moved"])
                for t in range(TT):
                    v.wait_ge(q["turned"], t + 2)
                    ln.link(v.tensor_copy(vt[:, t, :], ps[(t + 1) % 2][:, 0:W]))
                    ln.tell(q["moved"])
                for t in range(TT):
                    v.wait_ge(q["mixed"], t + 1)
                    ln.link(v.tensor_tensor(g.oT[:, 2, :, t * P:(t + 1) * P], pc[:, 0:2, t * P:(t + 1) * P],
                                            ps[2 + t % 2][:, 0:2 * P].rearrange("p (n t) -> p n t", n=2), ALU.mult))
                    ln.tell(q["read"])


def merge(nc, g, l, segs):
    with ExitStack() as mem, Stage(nc, f"merge{l}", "g0_in g1_in b0_in b1_in w0_used w1_used gate0 gate1 val0 val1 sig0 sig1 free0 free1") as s:
        wg = [mem.enter_context(sbuf(nc, "wg", [P, KD, 4, P])) for _ in range(2)]
        wb = [mem.enter_context(sbuf(nc, "wb", [P, 4, WT, P])) for _ in range(2)]
        sg = [mem.enter_context(sbuf(nc, "sg", [P, T])) for _ in range(2)]
        tmp = mem.enter_context(sbuf(nc, "tmp", [P, T]))
        pg = [[mem.enter_context(psum(nc, "pg", [P, 512])) for _ in segs] for _ in range(2)]
        pv = [[mem.enter_context(psum(nc, "pv", [P, 512])) for _ in segs] for _ in range(2)]
        q = s.sem
        g_in, b_in, used = [q["g0_in"], q["g1_in"]], [q["b0_in"], q["b1_in"]], [q["w0_used"], q["w1_used"]]
        gate, val, sig, free = [q["gate0"], q["gate1"]], [q["val0"], q["val1"]], [q["sig0"], q["sig1"]], [q["free0"], q["free1"]]
        lo, hi = segs[0][0], segs[-1][1]

        @s.body.sync
        def _(sp):
            ln = s.line(sp, "sp")
            gw = g.w_in[l][:, GATE0:].rearrange("(k p) (b n) -> p k b n", p=P, b=4)
            bw = g.w_branch[l].rearrange("b (k p) n -> p b k n", p=P)
            with sp.Fori(0, KD // 2) as i:
                for j in range(2):
                    ln.hold(used[j], i + 1)
                    at = bass.ds(i * (2 * P) + j * P, P)
                    for b in range(4):
                        sp.dma_start(wg[j][:, :, b, :], gw[:, :, b, at]).then_inc(g_in[j], 16)
                        sp.dma_start(wb[j][:, b, :, :], bw[:, b, :, at]).then_inc(b_in[j], 16)

        @s.body.tensor
        def _(pe):
            ln = s.line(pe, "pe")
            ln.credit(*used)
            with pe.Fori(0, KD // 2) as i:
                for j in range(2):
                    ln.hold(g_in[j], i * 64 + 64)
                    ln.hold(b_in[j], i * 64 + 64)
                    for b in range(4):
                        u = b % 2
                        ln.hold(free[u], i * 4 + j * 2 + b // 2 + 1)
                        for n, (a, e, _) in enumerate(segs):
                            for k in range(KD):
                                last = pe.matmul(pg[u][n][:, 0:e - a], wg[j][:, k, b, :], g.hT[:, k, a:e], start=k == 0, stop=k == KD - 1)
                        last.then_inc(gate[u], 1)
                        for n, (a, e, _) in enumerate(segs):
                            for k in range(WT):
                                last = pe.matmul(pv[u][n][:, 0:e - a], wb[j][:, b, k, :], g.oT[:, b, k, a:e], start=k == 0, stop=k == WT - 1)
                        last.then_inc(val[u], 1)
                    ln.hold(val[1], i * 4 + j * 2 + 2)
                    ln.tell(used[j])

        @s.body.scalar
        def _(act):
            ln = s.line(act, "act")
            with act.Fori(0, KD // 2) as i:
                for j in range(2):
                    for b in range(4):
                        u, n_done = b % 2, i * 4 + j * 2 + b // 2
                        ln.hold(gate[u], n_done + 1)
                        ln.hold(free[u], n_done + 1)
                        for n, (a, e, _) in enumerate(segs):
                            ln.link(act.activation(sg[u][:, a:e], pg[u][n][:, 0:e - a], ACT.Sigmoid))
                        ln.tell(sig[u])
                ln.restart()

        @s.body.vector
        def _(v):
            ln = s.line(v, "dve")
            ln.credit(*free)
            with v.Fori(0, KD // 2) as i:
                for j in range(2):
                    m = g.mT[:, bass.ds(i * 2 + j, 1), lo:hi]
                    for b in range(4):
                        u, n_done = b % 2, i * 4 + j * 2 + b // 2
                        ln.hold(sig[u], n_done + 1)
                        ln.hold(val[u], n_done + 1)
                        for n, (a, e, _) in enumerate(segs):
                            o = m[:, :, a - lo:e - lo] if b == 0 else tmp[:, a:e].unsqueeze(1)
                            ln.link(v.tensor_tensor(o, sg[u][:, a:e].unsqueeze(1), pv[u][n][:, 0:e - a].unsqueeze(1), ALU.mult))
                        ln.tell(free[u])
                        if b:
                            ln.link(v.tensor_tensor(m, m, tmp[:, lo:hi].unsqueeze(1), ALU.add))
                ln.restart()


def shift_tiles(v, ln, src, out, mmu, omu):
    for t in range(src.shape[1]):
        ln.link(v.tensor_scalar(out[:, t, :], src[:, t, :], omu[:, t:t + 1], None, ALU.mult))

        def add(o, i, kind):
            ln.link(v.scalar_tensor_tensor(o, i, mmu[:, t, kind:kind + 1], o, ALU.mult, ALU.add))

        add(out[:, t, 1:CTX], src[:, t, 0:CTX - 1], 0)
        add(out[:, t, 0:CTX - 1], src[:, t, 1:CTX], 1)
        og = out[:, t, CTX:T].rearrange("p (r w) -> p r w", w=GW)
        sg = src[:, t, CTX:T].rearrange("p (r w) -> p r w", w=GW)
        add(og[:, :, 1:GW], sg[:, :, 0:GW - 1], 0)
        add(og[:, :, 0:GW - 1], sg[:, :, 1:GW], 1)
        add(og[:, 1:GR, :], sg[:, 0:GR - 1, :], 2)
        add(og[:, 0:GR - 1, :], sg[:, 1:GR, :], 3)


def rwkv(nc, g, l):
    HALF = T // 2
    with ExitStack() as top:
        def keep(name, shape):
            return top.enter_context(sbuf(nc, name, shape))

        gate, bonus = keep("rk_gate", [P, WT, T]), keep("rk_bonus", [P, WT, T])
        vec = keep("rk_vec", [P, 5, WT])
        with ExitStack() as prep:
            def tmp(name, shape):
                return prep.enter_context(sbuf(nc, name, shape))

            pq = tmp("rk_q", [P, 8, T])
            with ExitStack() as first:
                raw = first.enter_context(sbuf(nc, "rk_p", [P, 8, T]))
                project(nc, g, f"rkp{l}", g.w_in[l][:, RWKV0:RWKV0 + 8 * P], 8, g.hT, SEG_ALL, out=raw)
                with ExitStack() as mem, Stage(nc, f"rks{l}", "vec_in") as s:
                    mu = mem.enter_context(sbuf(nc, "mu", [P, 2, 8]))
                    mmu = mem.enter_context(sbuf(nc, "mmu", [P, 8, 4]))
                    q = s.sem

                    @s.body.sync
                    def _(sp):
                        with nc.allow_non_contiguous_dma(reason="vectors onto partitions"):
                            sp.dma_start(mu[:, 0, :], g.rwkv_mu[l].rearrange("(t p) -> p t", p=P)).then_inc(q["vec_in"], 16)
                            for n, a in enumerate((g.rwkv_k_k[l], g.rwkv_k_a[l], g.rwkv_r_k[l].rearrange("h n -> (h n)"),
                                                   g.rwkv_gn_g[l].rearrange("h n -> (h n)"), g.rwkv_gn_b[l].rearrange("h n -> (h n)"))):
                                sp.dma_start(vec[:, n, :], a.rearrange("(t p) -> p t", p=P)).then_inc(q["vec_in"], 16)

                    @s.body.vector
                    def _(v):
                        ln = s.line(v, "dve")
                        v.wait_ge(q["vec_in"], 96)
                        ln.link(v.tensor_scalar(mu[:, 1, :], mu[:, 0, :], -1.0, 1.0, ALU.mult, ALU.add))
                        ln.link(v.tensor_tensor(mmu[:, :, :], mu[:, 0, :].unsqueeze(2).broadcast_to([P, 8, 4]),
                                                g.c(QUAD, 4).unsqueeze(1).broadcast_to([P, 8, 4]), ALU.mult))
                        shift_tiles(v, ln, raw, pq, mmu, mu[:, 1, :])

            aT, kd = tmp("rk_a", [P, 2 * WT, T]), tmp("rk_kd", [P, 2 * WT, T])
            kk, lw = tmp("rk_kk", [P, WT, T]), tmp("rk_lw", [P, TT, 2 * W])
            with ExitStack() as mem, Stage(nc, f"rkl{l}", "w_in act_ready full read") as s:
                g2 = mem.enter_context(sbuf(nc, "g2", [P, W]))
                wa = mem.enter_context(sbuf(nc, "w2a2", [P, 2, W]))
                w0 = mem.enter_context(sbuf(nc, "w0", [1, 2 * W]))
                a0 = mem.enter_context(sbuf(nc, "a0", [P, 2, WT]))
                ps = [mem.enter_context(psum(nc, "lps", [P, 512])) for _ in range(8)]
                q = s.sem
                jobs = [("gate", 0, n) for n in range(WT)] + [("a", d, n) for d in range(2) for n in range(WT)]
                jobs += [("w", t, 0) for t in range(TT)]

                @s.body.sync
                def _(sp):
                    sp.dma_start(g2[:, :], g.rwkv_g2[l]).then_inc(q["w_in"], 16)
                    sp.dma_start(wa[0:HD, :, :], g.rwkv_w2[l].rearrange("d r w -> r d w")).then_inc(q["w_in"], 16)
                    sp.dma_start(wa[HD:P, :, :], g.rwkv_a2[l].rearrange("d r w -> r d w")).then_inc(q["w_in"], 16)
                    sp.dma_start(w0[:, :], g.rwkv_w0[l:l + 1].rearrange("a d w -> a (d w)")).then_inc(q["w_in"], 16)
                    with nc.allow_non_contiguous_dma(reason="vectors onto partitions"):
                        for d in range(2):
                            sp.dma_start(a0[:, d, :], g.rwkv_a0[l, d].rearrange("(t p) -> p t", p=P)).then_inc(q["w_in"], 16)

                @s.body.tensor
                def _(pe):
                    pe.wait_ge(q["w_in"], 96)
                    pe.wait_ge(q["act_ready"], 1)
                    for n, (kind, d, j) in enumerate(jobs):
                        if n >= 4:
                            pe.wait_ge(q["read"], n - 3)
                        b = n % 4 * 2
                        if kind == "w":
                            pe.matmul(ps[b][:, :], pq[0:HD, 6, d * P:(d + 1) * P], wa[0:HD, :, :].rearrange("r d w -> r (d w)"),
                                      start=True, stop=False)
                            last = pe.matmul(ps[b][:, :], g.c(ONES)[0:1, :], w0[0:1, :], start=False, stop=True)
                        for half in range(2 if kind != "w" else 0):
                            cut = slice(half * HALF, (half + 1) * HALF)
                            lhs, rhs = ((g2[:, j * P:(j + 1) * P], pq[:, 7, cut]) if kind == "gate" else
                                        (wa[HD:P, d, j * P:(j + 1) * P], pq[HD:P, 6, cut]))
                            last = pe.matmul(ps[b + half][:, 0:HALF], lhs, rhs, start=True, stop=True)
                        last.then_inc(q["full"], 1)

                @s.body.scalar
                def _(act):
                    ln = s.line(act, "act")
                    ln.link(act.activation(pq[0:HD, 6, :], pq[0:HD, 6, :], ACT.Tanh))
                    ln.link(act.activation(pq[:, 7, :], pq[:, 7, :], ACT.Sigmoid))
                    ln.tell(q["act_ready"])
                    act.wait_ge(q["w_in"], 96)
                    for n, (kind, d, j) in enumerate(jobs):
                        act.wait_ge(q["full"], n + 1)
                        b = n % 4 * 2
                        if kind == "w":
                            ln.link(act.activation(lw[:, d, :], ps[b][:, :], ACT.Sigmoid))
                        for half in range(2 if kind != "w" else 0):
                            cut = slice(half * HALF, (half + 1) * HALF)
                            if kind == "gate":
                                ln.link(act.activation(gate[:, j, cut], ps[b + half][:, 0:HALF], ACT.Copy))
                            else:
                                ln.link(act.activation(aT[:, d * WT + j, cut], ps[b + half][:, 0:HALF], ACT.Sigmoid, bias=a0[:, d, j:j + 1]))
                        ln.tell(q["read"])

                @s.body.vector
                def _(v):
                    ln = s.line(v, "dve")
                    for n in range(WT):
                        ln.link(v.tensor_scalar(kk[:, n, :], pq[:, 2 + n, :], vec[:, 0, n:n + 1], None, ALU.mult))
            normalize(nc, g, f"rkn{l}", kk[:, :, :], BLK, 1.0)
            with ExitStack() as mem, Stage(nc, f"rkb{l}", "prod_ready summed ready stored") as s:
                one_ka = mem.enter_context(sbuf(nc, "one_ka", [P, WT]))
                t = mem.enter_context(sbuf(nc, "rk_t", [P, WT, T]))
                ps = [mem.enter_context(psum(nc, "bps", [P, 512])) for _ in range(4)]
                q = s.sem

                @s.body.vector
                def _(v):
                    ln = s.line(v, "dve")
                    ln.link(v.tensor_scalar(one_ka[:, :], vec[:, 1, :], -1.0, 1.0, ALU.mult, ALU.add))
                    for d in range(2):
                        for n in range(WT):
                            m = d * WT + n
                            ln.link(v.tensor_scalar(kd[:, m, :], aT[:, m, :], vec[:, 1, n:n + 1], one_ka[:, n:n + 1], ALU.mult, ALU.add))
                            ln.link(v.tensor_tensor(kd[:, m, :], kd[:, m, :], pq[:, 2 + n, :], ALU.mult))
                            ln.link(v.tensor_tensor(aT[:, m, :], aT[:, m, :], kk[:, n, :], ALU.mult))
                    ln.tell(q["ready"])
                    ln.link(v.tensor_tensor(t[:, :, :], kd[:, 0:WT, :], kd[:, WT:2 * WT, :], ALU.add))
                    for n in range(WT):
                        ln.link(v.scalar_tensor_tensor(t[:, n, :], t[:, n, :], vec[:, 2, n:n + 1], pq[:, n, :], ALU.mult, ALU.mult))
                    ln.tell(q["prod_ready"])
                    v.wait_ge(q["summed"], 1)
                    for n in range(WT):
                        for half in range(2):
                            cut = slice(half * HALF, (half + 1) * HALF)
                            ln.link(v.tensor_tensor(bonus[:, n, cut], pq[:, 4 + n, cut], ps[2 * n + half][:, 0:HALF], ALU.mult))

                @s.body.tensor
                def _(pe):
                    pe.wait_ge(q["prod_ready"], 1)
                    for n in range(WT):
                        for half in range(2):
                            last = pe.matmul(ps[2 * n + half][:, 0:HALF], g.c(BLK), t[:, n, half * HALF:(half + 1) * HALF], start=True, stop=True)
                    last.then_inc(q["summed"], 1)

                @s.body.sync
                def _(sp):
                    f = g.rk_feat.rearrange("n p t -> p n t")
                    sp.dma_start(f[:, 0:2, :], pq[:, 0:2, :]).then_inc(q["stored"], 16)
                    sp.dma_start(f[:, 2:4, :], pq[:, 4:6, :]).then_inc(q["stored"], 16)
                    sp.dma_start(f[:, 4:6, :], kk[:, :, :]).then_inc(q["stored"], 16)
                    sp.dma_start(g.rk_logw.rearrange("(t p) n -> p t n", p=P), lw[:, :, :]).then_inc(q["stored"], 16)
                    sp.wait_ge(q["ready"], 1)
                    sp.dma_start(f[:, 6:10, :], kd[:, :, :]).then_inc(q["stored"], 16)
                    sp.dma_start(f[:, 10:14, :], aT[:, :, :]).then_inc(q["stored"], 16)
                    sp.wait_ge(q["stored"], 96)

        y = keep("rk_y", [P, 2 * WT, T])
        recurrence(nc, g, f"rkr{l}", y, "rwkv")
        normalize(nc, g, f"rky{l}", y[:, :, :], BLK, 1.0 / HD, center=True)
        with Stage(nc, f"rko{l}") as s:
            @s.body.vector
            def _(v):
                ln = s.line(v, "dve")
                for m in range(2 * WT):
                    n = m % WT
                    ln.link(v.tensor_scalar(y[:, m, :], y[:, m, :], vec[:, 3, n:n + 1], vec[:, 4, n:n + 1], ALU.mult, ALU.add))
                ln.link(v.tensor_tensor(y[:, 0:WT, :], y[:, 0:WT, :], y[:, WT:2 * WT, :], ALU.add))
                ln.link(v.tensor_tensor(y[:, 0:WT, :], y[:, 0:WT, :], bonus[:, :, :], ALU.add))
                ln.link(v.tensor_tensor(g.oT[:, 0, :, :], y[:, 0:WT, :], gate[:, :, :], ALU.mult))


def gdn(nc, g, l):
    PADG = CONV_G // 2
    LONGG = PADG + CTX + PADG + SEQ + PADG
    with ExitStack() as top:
        def keep(name, shape):
            return top.enter_context(sbuf(nc, name, shape))

        zs = keep("gd_z", [P, WT, T])
        gd = keep("gd_g", [P, TT, 8])
        beta = keep("gd_beta", [P, TT, 8])
        with ExitStack() as prep:
            raw = prep.enter_context(sbuf(nc, "gd_p", [P, 8, T]))
            f = prep.enter_context(sbuf(nc, "gd_f", [P, 6, T]))
            project(nc, g, f"gdp{l}", g.w_in[l][:, GDN0:GDN0 + 8 * P], 8, g.hT, SEG_ALL, out=raw)
            with ExitStack() as mem, Stage(nc, f"gdc{l}", "w_in full conv_ready sig_ready asked given") as s:
                pad = mem.enter_context(sbuf(nc, "gd_pad", [P, 6, LONGG]))
                acc = mem.enter_context(sbuf(nc, "gd_acc", [P, LONGG]))
                taps = mem.enter_context(sbuf(nc, "gd_taps", [P, 6, CONV_G]))
                wab = mem.enter_context(sbuf(nc, "gd_wab", [P, KD, 16]))
                rowv = mem.enter_context(sbuf(nc, "gd_rowv", [P, 2, 8]))
                sp0 = mem.enter_context(sbuf(nc, "gd_sp0", [P, TT, 8]))
                sp1 = mem.enter_context(sbuf(nc, "gd_sp1", [P, TT, 8]))
                sig = mem.enter_context(sbuf(nc, "gd_sig", [P, 8, T]))
                ps = mem.enter_context(psum(nc, "gab", [P, 512]))
                q = s.sem
                ab = mem.enter_context(sbuf(nc, "gd_ab", [P, TT, 16]))

                @s.body.sync
                def _(sp):
                    with nc.allow_non_contiguous_dma(reason="small weights onto partitions"):
                        for n in range(6):
                            sp.dma_start(taps[:, n, :], g.gdn_conv_w[l][:, n * P:(n + 1) * P].rearrange("k p -> p k")).then_inc(q["w_in"], 16)
                        sp.dma_start(wab[:, :, :], g.w_in[l][:, AB0:AB0 + 16].rearrange("(k p) n -> p k n", p=P)).then_inc(q["w_in"], 16)
                        for n, a in enumerate((g.gdn_a_log, g.gdn_dt_bias)):
                            sp.dma_start(rowv[:, n, :], a[l].rearrange("d h -> (d h)").partition_broadcast(P)).then_inc(q["w_in"], 16)

                @s.body.tensor
                def _(pe):
                    pe.wait_ge(q["w_in"], 144)
                    for t in range(TT):
                        for k in range(KD):
                            last = pe.matmul(ps[:, t * 16:t * 16 + 16], g.hT[:, k, t * P:(t + 1) * P], wab[:, k, :], start=k == 0, stop=k == KD - 1)
                    last.then_inc(q["full"], 1)

                @s.body.scalar
                def _(act):
                    ln = s.line(act, "act")
                    ln.link(act.activation(sig[:, 6:8, :], raw[:, 6:8, :], ACT.Sigmoid))
                    ln.tell(q["sig_ready"])
                    act.wait_ge(q["asked"], 1)
                    ln.link(act.activation(beta[:, :, :], ab[:, :, 8:16], ACT.Sigmoid))
                    act.wait_ge(q["asked"], 2)
                    ln.link(act.activation(sp1[:, :, :], sp1[:, :, :], ACT.Exp, scale=-1.0))
                    ln.link(act.activation(rowv[:, 0, :], rowv[:, 0, :], ACT.Exp))
                    ln.link(act.activation(sp1[:, :, :], sp1[:, :, :], ACT.Ln, bias=1.0))
                    ln.tell(q["given"])
                    for n in range(6):
                        act.wait_ge(q["conv_ready"], n + 1)
                        ln.link(act.activation(sig[:, n, :], f[:, n, :], ACT.Sigmoid))
                        ln.tell(q["sig_ready"])

                @s.body.vector
                def _(v):
                    ln = s.line(v, "dve")
                    ln.link(v.memset(pad[:, :, :], 0.0))
                    v.wait_ge(q["w_in"], 144)
                    v.wait_ge(q["full"], 1)
                    ln.link(v.tensor_copy(ab[:, :, :], ps[:, 0:TT * 16].rearrange("p (t n) -> p t n", n=16)))
                    ln.tell(q["asked"])
                    dt = rowv[:, 1, :].unsqueeze(1).broadcast_to([P, TT, 8])
                    ln.link(v.tensor_tensor(sp0[:, :, :], ab[:, :, 0:8], dt, ALU.add))
                    ln.link(v.scalar_tensor_tensor(sp1[:, :, :], sp0[:, :, :], -1.0, sp0[:, :, :], ALU.mult, ALU.max))
                    ln.tell(q["asked"])
                    ln.link(v.tensor_copy(pad[:, :, PADG:PADG + CTX], raw[:, 0:6, 0:CTX]))
                    ln.link(v.tensor_copy(pad[:, :, 2 * PADG + CTX:2 * PADG + T], raw[:, 0:6, CTX:T]))
                    for n in range(6):
                        conv(v, ln, acc[:, :], pad[:, n, :], lambda k: taps[:, n, k:k + 1], CONV_G, None, PADG)
                        ln.link(v.tensor_copy(f[:, n, 0:CTX], acc[:, 0:CTX]))
                        ln.link(v.tensor_copy(f[:, n, CTX:T], acc[:, CTX + PADG:CTX + PADG + SEQ]))
                        ln.tell(q["conv_ready"])
                    v.wait_ge(q["given"], 1)
                    ln.link(v.scalar_tensor_tensor(sp0[:, :, :], sp0[:, :, :], 0.0, sp1[:, :, :], ALU.max, ALU.add))
                    ln.link(v.scalar_tensor_tensor(gd[:, :, :], sp0[:, :, :], -1.0,
                                                   rowv[:, 0, :].unsqueeze(1).broadcast_to([P, TT, 8]), ALU.mult, ALU.mult))
                    v.wait_ge(q["sig_ready"], 7)
                    ln.link(v.tensor_tensor(zs[:, :, :], raw[:, 6:8, :], sig[:, 6:8, :], ALU.mult))
                    ln.link(v.tensor_tensor(f[:, :, :], f[:, :, :], sig[:, 0:6, :], ALU.mult))
            normalize(nc, g, f"gdn{l}", f[:, 0:4, :], BLK, 1.0)
            with Stage(nc, f"gdf{l}", "ready stored") as s:
                q = s.sem

                @s.body.vector
                def _(v):
                    ln = s.line(v, "dve")
                    ln.link(v.tensor_scalar(f[:, 0:WT, :], f[:, 0:WT, :], HD ** -0.5, None, ALU.mult))
                    ln.tell(q["ready"])

                @s.body.sync
                def _(sp):
                    sp.wait_ge(q["ready"], 1)
                    sp.dma_start(g.gd_feat.rearrange("n p t -> p n t"), f[:, :, :]).then_inc(q["stored"], 16)
                    sp.wait_ge(q["stored"], 16)
        y = keep("gd_y", [P, 2 * WT, T])
        recurrence(nc, g, f"gdr{l}", y, "gdn", gd, beta)
        with Stage(nc, f"gds{l}") as s:
            @s.body.vector
            def _(v):
                ln = s.line(v, "dve")
                ln.link(v.tensor_tensor(y[:, 0:WT, :], y[:, 0:WT, :], y[:, WT:2 * WT, :], ALU.add))
        normalize(nc, g, f"gdy{l}", y[:, 0:WT, :], BLK, 1.0 / HD)
        with ExitStack() as mem, Stage(nc, f"gdo{l}", "vec_in") as s:
            ng = mem.enter_context(sbuf(nc, "gd_ng", [P, 1]))

            @s.body.sync
            def _(sp):
                with nc.allow_non_contiguous_dma(reason="a vector onto partitions"):
                    for hf in range(2):
                        sp.dma_start(ng[hf * HD:(hf + 1) * HD, :], g.gdn_norm_g[l].rearrange("(p a) -> p a", a=1)).then_inc(s.sem["vec_in"], 16)

            @s.body.vector
            def _(v):
                ln = s.line(v, "dve")
                v.wait_ge(s.sem["vec_in"], 32)
                for n in range(WT):
                    ln.link(v.scalar_tensor_tensor(g.oT[:, 1, n, :], y[:, n, :], ng[:, 0:1], zs[:, n, :], ALU.mult, ALU.mult))


def recurrence(nc, g, name, y, kind, gd=None, beta=None):
    rk = kind == "rwkv"
    ROUNDS = TT
    NF = 10 if rk else 6
    with ExitStack() as mem, Stage(nc, name, "feat_in feat_free front_ready rows_ready gb_ready exp_ready v_ready ops_ready "
                                   "tok_ready diff_ready gamma_ready gammas turned moved mats1 mats1_read mats2 lt_ready mats_done "
                                   "levels x_init t_full t_moved p_full x_ready rhs_full rhs_moved u_full u_moved o_full o_moved "
                                   "s_full s_ready act_end dve_end") as s:
        def sb(n, shape):
            return mem.enter_context(sbuf(nc, n, shape))

        q = s.sem
        ft = sb("ft", [P, 2, NF, P])
        kkt, rt = sb("kkt", [P, 4, P]), sb("rt", [P, 4, P])
        vt, kt = sb("vt", [P, 2, W]), sb("kt", [P, 2, W])
        lt, x, xt, tt = (sb(n, [P, 8, P]) for n in ("lt", "x", "xt", "tt"))
        lk = sb("lk", [P, LEVELS, 8, P])
        mo = sb("mo", [P, 8, P])
        st = sb("st", [P, 2, 4, HD])
        dec = sb("dec", [P, 2, 4])
        rs, us = sb("rs_", [P, W]), sb("us", [P, W])
        if rk:
            lw = sb("lw_", [P, 2, W])
            e_in, e_ex, e_ng = (sb(n, [P, 2, 2, P]) for n in ("e_in", "e_ex", "e_ng"))
            kht, bht = sb("kht", [P, 4, P]), sb("bht", [P, 4, P])
            bt = sb("bt", [P, 2, W])
            ak, mv = sb("ak", [P, 8, P]), sb("mv", [P, 8, P])
        else:
            gs, be = sb("gs_", [P, 2, 4]), sb("be", [P, 2, 4])
            gb = sb("gb", [P, 8, P])
            eg, gcs = sb("eg", [P, 32]), sb("gcs", [P, 8])
            kb, kbe, qe = (sb(n, [P, 8, HD]) for n in ("kb", "kbe", "qe"))
            kbt = sb("kbt", [P, 4, P])
            gam, gam_s = sb("gam", [P, 8, P]), sb("gam_s", [P, 8, P])
        B = [mem.enter_context(psum(nc, f"b{i}", [P, 512])) for i in range(8)]

        def by_head(bank):
            return bank[:, :].rearrange("p (h t) -> p h t", h=H)

        def both(col, stride):
            return g.c(col, 2 * stride).rearrange("p (d s) -> p d s", d=2)[:, :, 0:P].unsqueeze(2).broadcast_to([P, 2, 2, P])

        def quad(a):
            return a.rearrange("p (d w) t -> p d w t", d=2)

        INCL, STRICT, MINUS = both(MASKS, 2 * P), both(MASKS + P, 2 * P), both(NMI, P)

        def incl(d):
            return MASKS + d * 2 * P

        def strict(d):
            return incl(d) + P

        def z_of(d, h):
            pair = d * 2 + h // 2
            return h % 2 * 4 + pair, slice(h % 2 * HD, (h % 2 + 1) * HD), pair

        ZS = [(d, h) for d in range(2) for h in range(H)]

        def tiles(i):
            return i, (7 - i) % TT

        @s.body.sync
        def _(sp):
            ln = s.line(sp, "sp")
            with sp.Fori(0, ROUNDS) as i:
                ln.hold(q["feat_free"], i + 1)
                for d, t in enumerate(tiles(i)):
                    at = bass.ds(t * P, P)
                    f = (g.rk_feat if rk else g.gd_feat).rearrange("n p t -> p n t")
                    sp.dma_start(ft[:, d, 0:6, :], f[:, 0:6, at]).then_inc(q["feat_in"], 16)
                    if rk:
                        sp.dma_start(ft[:, d, 6:8, :], f[:, 6 + 2 * d:8 + 2 * d, at]).then_inc(q["feat_in"], 16)
                        sp.dma_start(ft[:, d, 8:10, :], f[:, 10 + 2 * d:12 + 2 * d, at]).then_inc(q["feat_in"], 16)
                        sp.dma_start(lw[:, d, :], g.rk_logw[at, d * W:(d + 1) * W]).then_inc(q["feat_in"], 16)

        loads = (8 if rk else 2) * 16

        @s.body.tensor
        def _(pe):
            ln = s.line(pe, "pe")

            def turn(bank, src):
                for n in range(4):
                    last = pe.transpose(bank[:, n * P:(n + 1) * P], src(n), g.c(IDENT))
                return last

            def pairs(banks, lhs, rhs):
                for d, h in ZS:
                    z, part, pair = z_of(d, h)
                    last = pe.matmul(by_head(banks[h % 2])[:, pair, :], lhs(part, d, h, pair, z), rhs(part, d, h, pair, z), start=True, stop=True)
                return last

            with pe.Fori(0, ROUNDS) as i:
                ln.hold(q["act_end"], i + 1)
                ln.hold(q["dve_end"], i + 1)
                ln.hold(q["feat_in"], i * loads + loads)
                if rk:
                    turn(B[2], lambda n: ft[:, n // 2, 2 + n % 2, :])
                    for d in range(2):
                        for hp in range(2):
                            last = pe.matmul(B[d][:, hp * 2 * P:(hp + 1) * 2 * P], lw[:, d, hp * P:(hp + 1) * P],
                                             g.c(incl(d), 2 * P), start=True, stop=True)
                    last.then_inc(q["front_ready"], 1)
                    ln.hold(q["v_ready"], i + 1)
                    ln.hold(q["ops_ready"], i + 1)
                    turn(B[3], lambda n: kht[:, n, :])
                    turn(B[4], lambda n: bht[:, n, :]).then_inc(q["turned"], 1)
                    pairs((B[5], B[6]), lambda p, d, h, w, z: bht[p, w, :], lambda p, d, h, w, z: kkt[p, w, :])
                    pairs((B[7], B[0]), lambda p, d, h, w, z: kht[p, w, :], lambda p, d, h, w, z: kkt[p, w, :]).then_inc(q["mats1"], 1)
                    ln.hold(q["moved"], i + 1)
                    pairs((B[1], B[2]), lambda p, d, h, w, z: kht[p, w, :], lambda p, d, h, w, z: rt[p, w, :])
                    pairs((B[3], B[4]), lambda p, d, h, w, z: bht[p, w, :], lambda p, d, h, w, z: rt[p, w, :]).then_inc(q["mats2"], 1)
                else:
                    for n, at in enumerate((0, 2, 4)):
                        turn(B[n], lambda m: ft[:, m // 2, at + m % 2, :])
                    ln.hold(q["gb_ready"], i + 1)
                    for d in range(2):
                        pe.matmul(B[3][:, d * 4:d * 4 + 4], g.c(incl(d)), gs[:, d, :], start=True, stop=True)
                        pe.matmul(B[3][:, 8 + d * 4:12 + d * 4], g.c(strict(1 - d)), gs[:, d, :], start=True, stop=True)
                    for c in range(2):
                        last = pe.matmul(B[3][:, 16 + 8 * c:24 + 8 * c], g.c(CHUNK + c * P), gs[:, :, :].rearrange("p d h -> p (d h)"),
                                         start=True, stop=True)
                    last.then_inc(q["front_ready"], 1)
                    pairs((B[4], B[5]), lambda p, d, h, w, z: gb[:, d * H + h, :], lambda p, d, h, w, z: g.c(incl(d))).then_inc(q["rows_ready"], 1)
                    ln.hold(q["tok_ready"], i + 1)
                    for bank, src in ((B[6], kb), (B[7], kbe), (B[0], qe)):
                        last = turn(bank, lambda n: src[:, 2 * n:2 * n + 2, :].rearrange("p h e -> p (h e)"))
                    last.then_inc(q["turned"], 1)
                    ln.hold(q["moved"], i + 1)
                    ln.hold(q["diff_ready"], i + 1)
                    pairs((B[1], B[2]), lambda p, d, h, w, z: ft[p, d, 2 + h // 2, :], lambda p, d, h, w, z: kbt[p, w, :])
                    pairs((B[3], B[4]), lambda p, d, h, w, z: ft[p, d, 2 + h // 2, :], lambda p, d, h, w, z: ft[p, d, h // 2, :]).then_inc(q["mats1"], 1)
                ln.hold(q["mats_done"], i + 1)
                ln.hold(q["x_init"], i + 1)
                for k in range(LEVELS):
                    ln.hold(q["levels"], i * LEVELS + k + 1)
                    if k:
                        ln.hold(q["x_ready"], i * LEVELS + k)
                    pairs((B[5], B[6]), lambda p, d, h, w, z: lk[:, k, z, :], lambda p, d, h, w, z: x[:, z, :]).then_inc(q["t_full"], 1)
                    ln.hold(q["t_moved"], i * LEVELS + k + 1)
                    if k < LEVELS - 1:
                        pairs((B[7], B[0]), lambda p, d, h, w, z: xt[:, z, :], lambda p, d, h, w, z: tt[:, z, :])
                    pairs((B[1], B[2]), lambda p, d, h, w, z: tt[:, z, :], lambda p, d, h, w, z: xt[:, z, :]).then_inc(q["p_full"], 1)
                ln.hold(q["x_ready"], i * LEVELS + LEVELS)
                for r in range(2):
                    ln.hold(q["s_ready"], i * 2 + r + 1)
                    for d, h in ZS:
                        z, part, pair = z_of(d, h)
                        c = r if d == 0 else 1 - r
                        ch = slice(c * C, (c + 1) * C)
                        o = B[3][ch, h * HD:(h + 1) * HD]
                        hv = slice(h * HD, (h + 1) * HD)
                        pe.matmul(o, kkt[:, pair, ch], st[:, h % 2, pair, :], start=True, stop=False)
                        last = pe.matmul(o, ak[:, z, ch] if rk else g.c(IDENT)[:, ch], vt[:, d, hv], start=False, stop=True)
                    last.then_inc(q["rhs_full"], 1)
                    ln.hold(q["rhs_moved"], i * 2 + r + 1)
                    for d, h in ZS:
                        z, part, pair = z_of(d, h)
                        c = r if d == 0 else 1 - r
                        ch = slice(c * C, (c + 1) * C)
                        last = pe.matmul(B[4][ch, h * HD:(h + 1) * HD], xt[:, z, ch], rs[:, h * HD:(h + 1) * HD], start=True, stop=True)
                    last.then_inc(q["u_full"], 1)
                    ln.hold(q["u_moved"], i * 2 + r + 1)
                    ln.hold(q["o_moved"], i * 2 + r + 1)
                    for d, h in ZS:
                        z, part, pair = z_of(d, h)
                        c = r if d == 0 else 1 - r
                        ch = slice(c * C, (c + 1) * C)
                        hv = slice(h * HD, (h + 1) * HD)
                        o = B[5][part, pair * C:(pair + 1) * C]
                        pe.matmul(o, st[:, h % 2, pair, :], rt[:, pair, ch], start=True, stop=False)
                        if rk:
                            pe.matmul(o, vt[:, d, hv], mv[:, z, ch], start=False, stop=False)
                        last = pe.matmul(o, us[:, hv], mo[:, z, ch], start=False, stop=True)
                    last.then_inc(q["o_full"], 1)
                    for d, h in ZS:
                        z, part, pair = z_of(d, h)
                        c = r if d == 0 else 1 - r
                        ch = slice(c * C, (c + 1) * C)
                        hv = slice(h * HD, (h + 1) * HD)
                        o = B[6 + d][part, h // 2 * HD:(h // 2 + 1) * HD]
                        if rk:
                            pe.matmul(o, kt[ch, d, hv], vt[ch, d, hv], start=True, stop=False)
                        last = pe.matmul(o, (bt if rk else kt)[ch, d, hv], us[ch, hv], start=not rk, stop=True)
                    last.then_inc(q["s_full"], 1)

        @s.body.scalar
        def _(act):
            ln = s.line(act, "act")
            ln.credit(q["act_end"], q["o_moved"])
            with act.Fori(0, ROUNDS) as i:
                ln.hold(q["act_end"], i + 1)
                ln.hold(q["dve_end"], i + 1)
                ln.hold(q["front_ready"], i + 1)
                if rk:
                    for d in range(2):
                        c = B[d][:, :].rearrange("p (h e t) -> p h e t", h=2, e=2)
                        ln.link(act.activation(e_in[:, d, :, :], c[:, :, 0, :], ACT.Exp, scale=-DECAY))
                        ln.link(act.activation(e_ng[:, d, :, :], c[:, :, 0, :], ACT.Exp, scale=DECAY))
                        ln.link(act.activation(e_ex[:, d, :, :], c[:, :, 1, :], ACT.Exp, scale=-DECAY))
                    ln.tell(q["exp_ready"])
                    ln.link(act.activation(vt[:, :, :], B[2][:, :].rearrange("p (d v) -> p d v", d=2), ACT.Copy))
                    ln.tell(q["v_ready"])
                    ln.hold(q["turned"], i + 1)
                    ln.link(act.activation(kt[:, :, :], B[3][:, :].rearrange("p (d v) -> p d v", d=2), ACT.Copy))
                    ln.link(act.activation(bt[:, :, :], B[4][:, :].rearrange("p (d v) -> p d v", d=2), ACT.Copy, scale=-1.0))
                    ln.tell(q["moved"])
                else:
                    ln.link(act.activation(eg[:, :], B[3][:, 0:32], ACT.Exp))
                    ln.tell(q["exp_ready"])
                    ln.hold(q["turned"], i + 1)
                    for bank, dst in ((B[6], kbt), (B[7], kkt), (B[0], rt)):
                        ln.link(act.activation(dst[:, :, :], by_head(bank), ACT.Copy))
                    ln.tell(q["moved"])
                    ln.hold(q["diff_ready"], i + 1)
                    ln.link(act.activation(gam[:, :, :], gam[:, :, :], ACT.Exp))
                    ln.tell(q["gamma_ready"])
                for k in range(LEVELS):
                    ln.hold(q["t_full"], i * LEVELS + k + 1)
                    for e in range(2):
                        ln.link(act.activation(tt[:, e * 4:e * 4 + 4, :], by_head(B[5 + e]), ACT.Copy))
                    ln.tell(q["t_moved"])
                for r in range(2):
                    ln.hold(q["rhs_full"], i * 2 + r + 1)
                    ln.link(act.activation(rs[:, :], B[3][:, 0:W], ACT.Copy))
                    ln.tell(q["rhs_moved"])
                    ln.hold(q["o_full"], i * 2 + r + 1)
                    for d, t in enumerate(tiles(i)):
                        c = r if d == 0 else 1 - r
                        ln.link(act.activation(y[:, d * 2:d * 2 + 2, bass.ds(t * P + c * C, C)],
                                               B[5][:, d * 2 * C:(d + 1) * 2 * C].rearrange("p (h t) -> p h t", h=2), ACT.Copy))
                    ln.tell(q["o_moved"])
                ln.tell(q["act_end"])
                ln.restart()

        @s.body.gpsimd
        def _(pool):
            ln = s.line(pool, "pool")
            with pool.Fori(0, ROUNDS) as i:
                ln.hold(q["act_end"], i + 1)
                ln.hold(q["dve_end"], i + 1)
                ln.hold(q["lt_ready"], i + 1)
                for k in range(LEVELS):
                    for e in range(2):
                        cut = slice(e * 4, e * 4 + 4)
                        ln.link(pool.tensor_tensor(quad(lk[:, k, cut, :]), quad(lt[:, cut, :]), both(LEVEL + 2 * k * P, P), ALU.mult))
                    ln.tell(q["levels"])
                ln.restart()

        @s.body.vector
        def _(v):
            ln = s.line(v, "dve")
            ln.credit(q["dve_end"], q["feat_free"])
            ln.link(v.memset(st[:, :, :, :], 0.0))
            ln.tell(q["s_ready"])
            ln.restart()
            with v.Fori(0, ROUNDS) as i:
                ln.hold(q["act_end"], i + 1)
                ln.hold(q["dve_end"], i + 1)
                for m in (x, xt):
                    ln.link(v.tensor_copy(m[:, :, :], g.c(IDENT).unsqueeze(1).broadcast_to([P, 8, P])))
                ln.tell(q["x_init"])
                if rk:
                    ln.hold(q["feat_in"], i * loads + loads)
                    ln.hold(q["exp_ready"], i + 1)
                    for d in range(2):
                        cut = slice(2 * d, 2 * d + 2)
                        for o, e, at in ((bht, e_ng, 8), (kkt, e_ex, 4), (kht, e_ng, 6), (rt, e_in, 0)):
                            ln.link(v.tensor_tensor(o[:, cut, :], e[:, d, :, :], ft[:, d, at:at + 2, :], ALU.mult))
                        for c in range(2):
                            end = c * C + (C - 1 if d == 0 else 0)
                            ln.link(v.tensor_copy(dec[:, c, cut], e_in[:, d, :, end]))
                    ln.tell(q["ops_ready"])
                    ln.tell(q["feat_free"])
                    ln.hold(q["mats1"], i + 1)
                    for e in range(2):
                        cut = slice(e * 4, e * 4 + 4)
                        ln.link(v.tensor_tensor(quad(lt[:, cut, :]), quad(by_head(B[5 + e])), STRICT, ALU.mult))
                    ln.tell(q["lt_ready"])
                    for e, bank in enumerate((B[7], B[0])):
                        cut = slice(e * 4, e * 4 + 4)
                        ln.link(v.tensor_tensor(quad(ak[:, cut, :]), quad(by_head(bank)), STRICT, ALU.mult))
                    ln.hold(q["mats2"], i + 1)
                    for e in range(2):
                        cut = slice(e * 4, e * 4 + 4)
                        ln.link(v.tensor_tensor(quad(mv[:, cut, :]), quad(by_head(B[1 + e])), INCL, ALU.mult))
                        ln.link(v.tensor_tensor(quad(mo[:, cut, :]), quad(by_head(B[3 + e])), MINUS, ALU.mult))
                    ln.tell(q["mats_done"])
                else:
                    for d, t in enumerate(tiles(i)):
                        ln.link(v.tensor_copy(gs[:, d, :].unsqueeze(1), gd[:, bass.ds(t, 1), d * H:(d + 1) * H]))
                        ln.link(v.tensor_copy(be[:, d, :].unsqueeze(1), beta[:, bass.ds(t, 1), d * H:(d + 1) * H]))
                    flat = gs[:, :, :].rearrange("p d h -> p (d h)")
                    ln.link(v.tensor_copy(gb[:, :, :], flat.unsqueeze(2).broadcast_to([P, 8, P])))
                    ln.tell(q["gb_ready"])
                    ln.hold(q["exp_ready"], i + 1)
                    ln.link(v.tensor_copy(gcs[:, :], B[3][:, 0:8]))

                    def heads(bank):
                        return bank[:, :].rearrange("p (z e) -> p z e", z=8)

                    def wide(a):
                        return a.unsqueeze(2).broadcast_to([P, 8, HD])

                    bz = wide(be[:, :, :].rearrange("p d h -> p (d h)"))
                    v8, k8 = (m[:, :, :].rearrange("p d (h e) -> p (d h) e", e=HD) for m in (vt, kt))
                    ln.link(v.tensor_tensor(kb[:, :, :], heads(B[1]), bz, ALU.mult))
                    ln.link(v.scalar_tensor_tensor(kbe[:, :, :], kb[:, :, :], -1.0, wide(eg[:, 0:8]), ALU.mult, ALU.mult))
                    ln.link(v.tensor_tensor(qe[:, :, :], heads(B[0]), wide(eg[:, 0:8]), ALU.mult))
                    ln.link(v.tensor_tensor(k8, heads(B[1]), wide(eg[:, 8:16]), ALU.mult))
                    ln.link(v.tensor_tensor(v8, heads(B[2]), bz, ALU.mult))
                    ln.tell(q["tok_ready"])
                    ends = eg[:, 16:32].rearrange("p (c w h) -> p c w h", c=2, h=2)
                    for hf in range(2):
                        part = slice(hf * HD, (hf + 1) * HD)
                        ln.link(v.tensor_copy(dec[part, :, :], ends[part, :, :, hf]))
                    ln.hold(q["rows_ready"], i + 1)
                    for d, h in ZS:
                        z, _, pair = z_of(d, h)
                        m = d * H + h
                        ln.link(v.tensor_scalar(gam[:, z, :], by_head(B[4 + h % 2])[:, pair, :], gcs[:, m:m + 1], 0.0, ALU.subtract, ALU.min))
                    ln.tell(q["diff_ready"])
                    ln.hold(q["gamma_ready"], i + 1)
                    halves = [slice(e * 4, e * 4 + 4) for e in range(2)]
                    for cut in halves:
                        ln.link(v.tensor_tensor(quad(gam_s[:, cut, :]), quad(gam[:, cut, :]), STRICT, ALU.mult))
                    ln.hold(q["mats1"], i + 1)
                    ln.tell(q["feat_free"])
                    for e, cut in enumerate(halves):
                        ln.link(v.tensor_tensor(lt[:, cut, :], by_head(B[1 + e]), gam_s[:, cut, :], ALU.mult))
                    ln.tell(q["lt_ready"])
                    for e, cut in enumerate(halves):
                        ln.link(v.tensor_tensor(quad(gam[:, cut, :]), quad(gam[:, cut, :]), INCL, ALU.mult))
                        ln.link(v.tensor_tensor(mo[:, cut, :], by_head(B[3 + e]), gam[:, cut, :], ALU.mult))
                    ln.tell(q["mats_done"])
                for k in range(LEVELS):
                    ln.hold(q["p_full"], i * LEVELS + k + 1)
                    for m, banks in ((x, (B[7], B[0])), (xt, (B[1], B[2])))[0 if k < LEVELS - 1 else 1:]:
                        for e in range(2):
                            cut = slice(e * 4, e * 4 + 4)
                            ln.link(v.tensor_tensor(m[:, cut, :], m[:, cut, :], by_head(banks[e]), ALU.subtract))
                    ln.tell(q["x_ready"])
                for r in range(2):
                    ln.hold(q["u_full"], i * 2 + r + 1)
                    ln.link(v.tensor_copy(us[:, :], B[4][:, 0:W]))
                    ln.tell(q["u_moved"])
                    ln.hold(q["s_full"], i * 2 + r + 1)
                    for d in range(2):
                        c = r if d == 0 else 1 - r
                        cut = slice(2 * d, 2 * d + 2)
                        for e in range(2):
                            part = slice(e * HD, (e + 1) * HD)
                            grown = B[6 + d][part, 0:2 * HD].rearrange("p (w e) -> p w e", w=2)
                            dd = dec[part, c, cut].unsqueeze(2).broadcast_to([HD, 2, HD])
                            sd = st[part, e, cut, :]
                            for by, op in ((grown, ALU.add), (dd, ALU.mult)) if rk else ((dd, ALU.mult), (grown, ALU.add)):
                                ln.link(v.tensor_tensor(sd, sd, by, op))
                    ln.tell(q["s_ready"])
                ln.tell(q["dve_end"])
                ln.restart()


def peer_pick(nc, g, l, t0, t1, qT, idx, gates):
    M = 2 * HEADS
    with ExitStack() as mem, Stage(nc, f"pick{l}", "keys_in k_turned k_moved q_in q_used scored copied sc_free exp_asked exp_done") as s:
        def sb(n, shape, dt=F32):
            return mem.enter_context(sbuf(nc, n, shape, dt))

        keys, keysT = sb("keys", [P, M, P]), sb("keysT", [P, M, P])
        qs, sc, wk = sb("qs", [P, M, P]), sb("sc", [P, M, NKEYS]), sb("wk", [P, NKEYS])
        top, best = sb("top", [P, M, TOPK]), sb("best", [P, HEADS, TOPK])
        at, pos, ab = sb("at", [P, M, TOPK], U32), sb("pos", [P, PICKS], U32), sb("ab", [P, PICKS], U32)
        atf, abf = sb("atf", [P, M, TOPK]), sb("abf", [P, PICKS])
        cand, eq = sb("cand", [P, HEADS, TOPK * TOPK]), sb("eq", [P, PICKS, TOPK])
        wk2, sel = sb("wk2", [P, TOPK * TOPK]), sb("sel", [P, 2, PICKS])
        ex, den = sb("ex", [P, HEADS, TOPK]), sb("den", [P, HEADS])
        B = [mem.enter_context(psum(nc, "pb", [P, 512])) for _ in range(4)]
        q = s.sem
        N = t1 - t0

        @s.body.sync
        def _(sp):
            ln = s.line(sp, "sp")
            sp.dma_start(keys[:, :, :], g.peer_keys[l].rearrange("h s k d -> k (h s) d")).then_inc(q["keys_in"], 16)
            with sp.Fori(0, N) as i:
                ln.hold(q["q_used"], i + 1)
                sp.dma_start(qs[:, :, :], qT[:, :, bass.ds(i * P + t0 * P, P)]).then_inc(q["q_in"], 16)

        @s.body.tensor
        def _(pe):
            ln = s.line(pe, "pe")
            ln.credit(q["q_used"])
            pe.wait_ge(q["keys_in"], 16)
            for n in range(4):
                for m in range(4):
                    last = pe.transpose(B[n][:, m * P:(m + 1) * P], keys[:, 4 * n + m, :], g.c(IDENT))
            last.then_inc(q["k_turned"], 1)
            pe.wait_ge(q["k_moved"], 1)
            with pe.Fori(0, N) as i:
                ln.hold(q["q_in"], i * 16 + 16)
                ln.hold(q["copied"], i + 1)
                for n in range(M):
                    last = pe.matmul(B[n // 4][:, n % 4 * P:(n % 4 + 1) * P], qs[:, n, :], keysT[:, n, :], start=True, stop=True)
                last.then_inc(q["scored"], 1)
                ln.hold(q["scored"], i + 1)
                ln.tell(q["q_used"])

        @s.body.scalar
        def _(act):
            ln = s.line(act, "act")
            ln.credit(q["copied"])
            act.wait_ge(q["k_turned"], 1)
            for n in range(4):
                ln.link(act.activation(keysT[:, 4 * n:4 * n + 4, :], B[n][:, :].rearrange("p (m k) -> p m k", m=4), ACT.Copy))
            ln.tell(q["k_moved"])
            ln.restart()
            with act.Fori(0, N) as i:
                ln.hold(q["scored"], i + 1)
                ln.hold(q["sc_free"], i + 1)
                for n in range(4):
                    ln.link(act.activation(sc[:, 4 * n:4 * n + 4, :], B[n][:, :].rearrange("p (m k) -> p m k", m=4), ACT.Copy))
                ln.tell(q["copied"])
                ln.hold(q["exp_asked"], i + 1)
                ln.link(act.activation(ex[:, :, :], ex[:, :, :], ACT.Exp))
                ln.tell(q["exp_done"])
                ln.restart()

        @s.body.vector
        def _(v):
            ln = s.line(v, "dve")
            ln.credit(q["sc_free"])

            def top16(values, work, out, where):
                ln.link(v.max(out[:, 0:8], values))
                ln.link(v.max_index(where[:, 0:8], out[:, 0:8], values))
                ln.link(v.match_replace(work, out[:, 0:8], values, NEG))
                ln.link(v.max(out[:, 8:16], work))
                ln.link(v.max_index(where[:, 8:16], out[:, 8:16], work))

            with v.Fori(0, N) as i:
                tile = bass.ds(i + t0, 1)
                ln.hold(q["copied"], i + 2)
                for m in range(M):
                    top16(sc[:, m, :], wk[:, :], top[:, m, :], at[:, m, :])
                ln.tell(q["sc_free"])
                ln.link(v.tensor_copy(atf[:, :, :], at[:, :, :]))
                tv = top[:, :, :].rearrange("p (h s) k -> p h s k", s=2)
                fv = atf[:, :, :].rearrange("p (h s) k -> p h s k", s=2)
                ln.link(v.tensor_tensor(cand[:, :, :].rearrange("p h (a b) -> p h a b", a=TOPK),
                                        tv[:, :, 0, :].unsqueeze(3).broadcast_to([P, HEADS, TOPK, TOPK]),
                                        tv[:, :, 1, :].unsqueeze(2).broadcast_to([P, HEADS, TOPK, TOPK]), ALU.add))
                for h in range(HEADS):
                    top16(cand[:, h, :], wk2[:, :], best[:, h, :], pos[:, h * TOPK:(h + 1) * TOPK])
                ln.link(v.tensor_tensor(ex[:, :, :], best[:, :, :], best[:, :, 0:1].broadcast_to([P, HEADS, TOPK]), ALU.subtract))
                ln.tell(q["exp_asked"])
                iota = g.c(IOTA, TOPK).unsqueeze(1).broadcast_to([P, PICKS, TOPK])
                for n, (op, by) in enumerate(((ALU.logical_shift_right, 4), (ALU.bitwise_and, TOPK - 1))):
                    ln.link(v.tensor_scalar(ab[:, :], pos[:, :], by, None, op))
                    ln.link(v.tensor_copy(abf[:, :], ab[:, :]))
                    ln.link(v.tensor_tensor(eq[:, :, :], abf[:, :].unsqueeze(2).broadcast_to([P, PICKS, TOPK]), iota, ALU.is_equal))
                    e4 = eq[:, :, :].rearrange("p (h k) a -> p h k a", h=HEADS)
                    ln.link(v.tensor_tensor(e4, e4, fv[:, :, n, :].unsqueeze(2).broadcast_to([P, HEADS, TOPK, TOPK]), ALU.mult))
                    ln.link(v.tensor_reduce(sel[:, n, :], eq[:, :, :], AX_X, ALU.add))
                ln.link(v.tensor_scalar(sel[:, 0, :], sel[:, 0, :], float(NKEYS), float(l * EXPERTS), ALU.mult, ALU.add))
                ln.link(v.tensor_tensor(idx[:, tile, :], sel[:, 0:1, :], sel[:, 1:2, :], ALU.add))
                ln.hold(q["exp_done"], i + 1)
                ln.link(v.tensor_reduce(den[:, :], ex[:, :, :], AX_X, ALU.add))
                ln.link(v.reciprocal(den[:, :], den[:, :]))
                ln.link(v.tensor_tensor(gates[:, tile, :].rearrange("p a (h k) -> p (a h) k", h=HEADS), ex[:, :, :],
                                        den[:, :].unsqueeze(2).broadcast_to([P, HEADS, TOPK]), ALU.mult))
                ln.restart()


def peer_apply(nc, g, l, t0, t1, cond, idx, gates):
    HALF = RING // 2
    ROUNDS = PICKS // RING
    before = g.rows_landed * 16
    g.rows_landed += (t1 - t0) * 2 * ROUNDS
    with ExitStack() as mem, Stage(nc, f"apply{l}_{t0}", "rows_used h_in h_used h_turned h_moved dots_done gelu_done f_ready f_turned f_moved") as s:
        def sb(n, shape, dt=F32):
            return mem.enter_context(sbuf(nc, n, shape, dt))

        hs, ht, junk, acc = sb("hs", [P, KD, P]), sb("ht", [P, D]), sb("junk", [P, D]), sb("acc", [P, D])
        ring = sb("ring", [P, RING, D])
        idxc = sb("idxc", [P, RING], U32)
        dots, dot16, coef, coef16 = sb("dots", [P, PICKS]), sb("dot16", [P, RING]), sb("coef", [P, PICKS]), sb("coef16", [P, RING])
        B = [mem.enter_context(psum(nc, "ab", [P, 512])) for _ in range(4)]
        q = s.sem
        N = t1 - t0

        @s.body.sync
        def _(sp):
            ln = s.line(sp, "sp")
            with sp.Fori(0, N) as i:
                ln.hold(q["h_used"], i + 1)
                sp.dma_start(hs[:, :, :], g.hT[:, :, bass.ds(i * P + t0 * P, P)]).then_inc(q["h_in"], 16)

        @s.body.gpsimd
        def _(pool):
            ln = s.line(pool, "pool")
            tables = [a.rearrange("l e d -> (l e) d") for a in (g.peer_u, g.peer_v)]
            with pool.Fori(0, N) as i:
                for n, table in enumerate(tables):
                    with pool.Fori(0, ROUNDS) as r:
                        for hf in range(2):
                            ln.hold(q["rows_used"], (i * (2 * ROUNDS) + r + n * ROUNDS) * RING + (hf + 1) * HALF)
                            cut = slice(hf * HALF, (hf + 1) * HALF)
                            ln.link(pool.tensor_copy(idxc[:, cut].unsqueeze(1), idx[:, bass.ds(i + t0, 1), bass.ds(r * RING + hf * HALF, HALF)]))
                            for j in range(hf * HALF, (hf + 1) * HALF):
                                pool.indirect_dma_start(ring[:, j, :], None, table, bass.IndirectOffsetOnAxis(ap=idxc[:, j:j + 1], axis=0)).then_inc(g.row_in[j], 16)
                        ln.restart()

        @s.body.tensor
        def _(pe):
            ln = s.line(pe, "pe")
            ln.credit(q["h_used"])
            with pe.Fori(0, N) as i:
                ln.hold(q["h_in"], i * 16 + 16)
                ln.hold(q["h_moved"], i + 1)
                for k in range(KD):
                    last = pe.transpose(B[k // 4][:, k % 4 * P:(k % 4 + 1) * P], hs[:, k, :], g.c(IDENT))
                last.then_inc(q["h_turned"], 1)
                ln.hold(q["h_turned"], i + 1)
                ln.tell(q["h_used"])
                ln.hold(q["f_ready"], i + 1)
                ln.hold(q["f_moved"], i + 1)
                for k in range(KD):
                    last = pe.transpose(B[2 + k // 4][:, k % 4 * P:(k % 4 + 1) * P], acc[:, k * P:(k + 1) * P], g.c(IDENT))
                last.then_inc(q["f_turned"], 1)

        @s.body.scalar
        def _(act):
            ln = s.line(act, "act")
            with act.Fori(0, N) as i:
                ln.hold(q["dots_done"], i + 1)
                ln.link(act.activation(dots[:, :], dots[:, :], ACT.Gelu_apprx_tanh))
                ln.tell(q["gelu_done"])
                ln.restart()

        @s.body.vector
        def _(v):
            ln = s.line(v, "dve")
            ln.credit(q["h_moved"], q["f_moved"])
            ln.tell(q["rows_used"], RING)
            with v.Fori(0, N) as i:
                ln.hold(q["h_turned"], i + 1)
                for n in range(2):
                    ln.link(v.tensor_copy(ht[:, n * 512:(n + 1) * 512], B[n][:, :]))
                ln.tell(q["h_moved"])
                ln.restart()
                with v.Fori(0, ROUNDS) as r:
                    for j in range(RING):
                        ln.hold(g.row_in[j], (i * (2 * ROUNDS) + r) * 16 + before + 16)
                        ln.link(v.tensor_tensor_reduce(junk[:, :], ring[:, j, :], ht[:, :], 1.0, 0.0, ALU.mult, ALU.add, dot16[:, j:j + 1]))
                        ln.tell(q["rows_used"])
                    ln.link(v.tensor_copy(dots[:, bass.ds(r * RING, RING)], dot16[:, :]))
                    ln.restart()
                ln.tell(q["dots_done"])
                ln.hold(q["gelu_done"], i + 1)
                ln.link(v.tensor_tensor(coef[:, :].unsqueeze(1), dots[:, :].unsqueeze(1), gates[:, bass.ds(i + t0, 1), :], ALU.mult))
                ln.link(v.memset(acc[:, :], 0.0))
                ln.restart()
                with v.Fori(0, ROUNDS) as r:
                    ln.link(v.tensor_copy(coef16[:, :], coef[:, bass.ds(r * RING, RING)]))
                    for j in range(RING):
                        ln.hold(g.row_in[j], (i * (2 * ROUNDS) + r + ROUNDS) * 16 + before + 16)
                        ln.link(v.scalar_tensor_tensor(acc[:, :], ring[:, j, :], coef16[:, j:j + 1], acc[:, :], ALU.mult, ALU.add))
                        ln.tell(q["rows_used"])
                    ln.restart()
                ln.tell(q["f_ready"])
                ln.hold(q["f_turned"], i + 1)
                tok = bass.ds(i * P + t0 * P, P)
                for k in range(KD):
                    ln.link(v.scalar_tensor_tensor(g.xT[:, k, tok], B[2 + k // 4][:, k % 4 * P:(k % 4 + 1) * P],
                                                   g.mods[:, 5 * KD + k, cond:cond + 1], g.xT[:, k, tok], ALU.mult, ALU.add))
                ln.tell(q["f_moved"])
                ln.restart()


def peer(nc, g, l, segs):
    t0 = segs[0][0] // P
    with ExitStack() as mem:
        idx = mem.enter_context(sbuf(nc, "idx", [P, TT, PICKS], U32))
        gates = mem.enter_context(sbuf(nc, "gates", [P, TT, PICKS]))
        with ExitStack() as front:
            qT = front.enter_context(sbuf(nc, "qT", [P, 2 * HEADS, T]))
            project(nc, g, f"q{l}", g.peer_w_q[l], 2 * HEADS, g.hT, segs, out=qT)
            peer_pick(nc, g, l, t0, TT, qT, idx, gates)
        for a, b, cond in segs:
            peer_apply(nc, g, l, a // P, b // P, cond, idx, gates)


def store_tokens(nc, g):
    with ExitStack() as mem, Stage(nc, "store", "turned moved stored") as s:
        rows = mem.enter_context(sbuf(nc, "orows", [P, TT - CT, D], F32))
        ps = [mem.enter_context(psum(nc, f"st{i}", [P, 4 * P], F32)) for i in range(2)]
        q = s.sem
        N = (TT - CT) * 2

        @s.body.tensor
        def _(pe):
            for n in range(N):
                if n >= 2:
                    pe.wait_ge(q["moved"], n - 1)
                for j in range(4):
                    t0 = CTX + n // 2 * P
                    last = pe.transpose(ps[n % 2][:, j * P:(j + 1) * P], g.hT[:, n % 2 * 4 + j, t0:t0 + P], g.c(IDENT))
                last.then_inc(q["turned"], 1)

        @s.body.vector
        def _(v):
            for n in range(N):
                v.wait_ge(q["turned"], n + 1)
                v.tensor_copy(rows[:, n // 2, n % 2 * 512:n % 2 * 512 + 512], ps[n % 2][:, :]).then_inc(q["moved"], 1)

        @s.body.sync
        def _(sp):
            sp.wait_ge(q["moved"], N)
            sp.dma_start(g.out[0].rearrange("(t p) d -> p t d", p=P), rows[:, :, :]).then_inc(q["stored"], 16)
            sp.wait_ge(q["stored"], 16)


def program(nc, args, consts, out):
    with ExitStack() as mem:
        def sb(name, shape, dt=F32):
            return mem.enter_context(sbuf(nc, name, shape, dt))

        g = Program()
        g.x, g.cvec, g.ctx, g.c_ctx, g.w_ada, g.b_ada = (args[n] for n in NAMES[0:6])
        g.norm1_g, g.norm2_g, g.w_in, g.rwkv_mu, g.rwkv_w0, g.rwkv_w2 = (args[n] for n in NAMES[6:12])
        g.rwkv_a0, g.rwkv_a2, g.rwkv_g2, g.rwkv_k_k, g.rwkv_k_a, g.rwkv_r_k = (args[n] for n in NAMES[12:18])
        g.rwkv_gn_g, g.rwkv_gn_b, g.gdn_conv_w, g.gdn_a_log, g.gdn_dt_bias, g.gdn_norm_g = (args[n] for n in NAMES[18:24])
        g.sgu_ln_g, g.sgu_ln_b, g.sgu_w_s, g.sgu_b_s, g.conf_dw_w, g.conf_dw_b = (args[n] for n in NAMES[24:30])
        g.conf_ln_g, g.conf_ln_b, g.w_branch, g.w_out, g.peer_w_q, g.peer_keys = (args[n] for n in NAMES[30:36])
        g.peer_u, g.peer_v, g.final_g = (args[n] for n in NAMES[36:39])
        g.out, g.consts = out, consts
        g.xT = sb("xT", [P, KD, T])
        g.hT = sb("hT", [P, KD, T])
        g.cst = sb("cst", [P, NCONST])
        g.cond = sb("cond", [P, KD, 2])
        g.cond_sig = sb("cond_sig", [P, KD, 2])
        g.mods = sb("mods", [P, 6 * KD, 2])
        g.gs = sb("gs", [P, 2, KD, 2])
        g.c = lambda col, n=P: g.cst[:, col:col + n]
        g.rk_feat = nc.dram_tensor("rk_feat", [14, P, T], F32, kind="Internal").ap()
        g.rk_logw = nc.dram_tensor("rk_logw", [T, 2 * W], F32, kind="Internal").ap()
        g.gd_feat = nc.dram_tensor("gd_feat", [6, P, T], F32, kind="Internal").ap()
        g.row_in = [mem.enter_context(nc.semaphore(f"row_in{j}")) for j in range(RING)]
        g.rows_landed = 0
        load_tokens(nc, g)
        for l in range(DEPTH):
            segs = SEG_ALL if l < DEPTH - 1 else SEG_X
            ada(nc, g, l)
            norm(nc, g, f"norm1_{l}", SEG_ALL, 0)
            with ExitStack() as mix:
                g.oT = mix.enter_context(sbuf(nc, "oT", [P, 4, WT, T]))
                rwkv(nc, g, l)
                gdn(nc, g, l)
                conformer(nc, g, l)
                sgu(nc, g, l)
                g.mT = mix.enter_context(sbuf(nc, "mT", [P, KD, T]))
                merge(nc, g, l, segs)
                project(nc, g, f"out{l}", g.w_out[l], KD, g.mT, segs, residual=2)
            norm(nc, g, f"norm2_{l}", segs, 1)
            peer(nc, g, l, segs)
        norm(nc, g, "final", SEG_X, 0, g.final_g)
        store_tokens(nc, g)


NAMES = ("x cvec ctx c_ctx w_ada b_ada norm1_g norm2_g w_in rwkv_mu rwkv_w0 rwkv_w2 rwkv_a0 rwkv_a2 rwkv_g2 rwkv_k_k "
         "rwkv_k_a rwkv_r_k rwkv_gn_g rwkv_gn_b gdn_conv_w gdn_a_log gdn_dt_bias gdn_norm_g sgu_ln_g sgu_ln_b sgu_w_s "
         "sgu_b_s conf_dw_w conf_dw_b conf_ln_g conf_ln_b w_branch w_out peer_w_q peer_keys peer_u peer_v final_g").split()


def kernel(**inputs):
    import concourse.bacc as bacc
    from concourse.bass_utils import run_bass_kernel_spmd as run

    nc = bacc.Bacc("TRN2", target_bir_lowering=False, num_devices=1)
    arrays, args = {}, {}
    for name in NAMES:
        a = np.ascontiguousarray(inputs["c" if name == "cvec" else name])
        arrays[f"in_{name}"] = a
        args[name] = nc.dram_tensor(f"in_{name}", a.shape, mybir.dt.from_np(a.dtype), kind="ExternalInput").ap()
    arrays["in_consts"] = constants()
    consts = nc.dram_tensor("in_consts", (P, NCONST), F32, kind="ExternalInput").ap()
    out = nc.dram_tensor("out_0", (1, SEQ, D), F32, kind="ExternalOutput").ap()
    program(nc, args, consts, out)
    return run(nc, [arrays], core_ids=[0]).results[0]["out_0"]
```

```python
from contextlib import ExitStack

import numpy as np
import concourse.bass as bass
from concourse import mybir

ALU = mybir.AluOpType
ACT = mybir.ActivationFunctionType
F32 = mybir.dt.float32
U32 = mybir.dt.uint32
AX_X = mybir.AxisListType.X

P = 128
D = 1024
KD = D // P
W = 256
WT = W // P
H = 4
HD = W // H
CTX, SEQ = 256, 512
T = CTX + SEQ
TT = T // P
CT = CTX // P
GW = 64
GR = SEQ // GW
C = 64
LEVELS = 6
EPS = 1e-6
DECAY = float(np.exp(-0.5))
DEPTH = 2

RWKV0, GDN0 = 0, 1024
AB0, SGU0, CONF0, GATE0 = 2048, 2064, 2576, 3088

HEADS = 8
NKEYS = 128
EXPERTS = NKEYS * NKEYS
TOPK = 16
PICKS = HEADS * TOPK
RING = 16
NEG = -3.0e38

CONV_G, CONV_C = 5, 31

IDENT, ONES, BLK = 0, 128, 256
MASKS = 384
CHUNK = MASKS + 4 * P
CINCL = CHUNK + 2 * P
CSTRICT = CINCL + 2 * C
CMINUS = CSTRICT + 2 * C
CEYE = CMINUS + 2 * C
CLEVEL = CEYE + C
QUAD = CLEVEL + 2 * LEVELS * C
IOTA = QUAD + 4
NCONST = IOTA + TOPK



class Program:
    pass


def constants():
    s, t = np.arange(P)[:, None], np.arange(P)[None, :]
    same = s // C == t // C
    cols = [s == t, np.ones((P, P)), s // HD == t // HD]
    for later, strictly in ((s <= t, s < t), (s >= t, s > t)):
        cols += [same & later, same & strictly]
    cols += [(s // C == c) & (t >= 0) for c in range(2)]
    u, w = s % C, np.arange(C)[None, :]
    cols += [u <= w, u >= w, u < w, u > w, -1.0 * (u <= w), -1.0 * (u >= w), u == w]
    for k in range(LEVELS):
        b = 1 << k
        near = u // (2 * b) == w // (2 * b)
        cols += [near & (u // b % 2 == 0) & (w // b % 2 == 1), near & (u // b % 2 == 1) & (w // b % 2 == 0)]
    cols += [s % 4 == np.arange(4)[None, :], np.broadcast_to(np.arange(TOPK)[None, :], (P, TOPK))]
    out = np.concatenate([np.asarray(c, np.float32) for c in cols], 1)
    assert out.shape == (P, NCONST)
    return out


def sbuf(nc, name, shape, dt=F32):
    return nc.sbuf_tensor(f"{name}_{nc.next_id()}", shape, dt)


def psum(nc, name, shape, dt=F32):
    return nc.psum_tensor(f"{name}_{nc.next_id()}", shape, dt)


class Line:

    def __init__(self, eng, chain, pace):
        self.eng, self.chain, self.pace, self.n = eng, chain, pace, 0

    def link(self, ins):
        self.n += 1
        ins.then_inc(self.chain, 1)
        self.eng.wait_ge(self.chain, self.n)

    def restart(self):
        if self.n:
            self.eng.sem_inc(self.chain, -self.n)
            self.n = 0

    def hold(self, sem, value):
        self.eng.wait_ge(sem, value)
        if not isinstance(value, int):
            self.eng.sem_inc(self.pace, 1)

    def tell(self, sem, n=1):
        self.eng.sem_inc(sem, n)

    def credit(self, *sems):
        for sem in sems:
            self.eng.sem_inc(sem, 1)


ENGINES = ("pe", "act", "dve", "pool", "sp")


class Stage:

    def __init__(self, nc, name, sems=""):
        self.nc, self.name, self.names = nc, name, sems.split()

    def __enter__(self):
        self.ctx = ExitStack()
        made = {n: self.ctx.enter_context(self.nc.semaphore(f"{self.name}_{n}"))
                for n in self.names + [f"chain_{e}" for e in ENGINES] + [f"pace_{e}" for e in ENGINES]}
        self.sem = made
        self.block = self.nc.Block()
        self.body = self.block.__enter__()
        return self

    def line(self, eng, name):
        return Line(eng, self.sem[f"chain_{name}"], self.sem[f"pace_{name}"])

    def __exit__(self, *e):
        self.block.__exit__(*e)
        if e[0] is None:
            with self.nc.Block() as clear:
                @clear.gpsimd
                def _(pool):
                    for s in self.sem.values():
                        pool.sem_clear(s)
        self.ctx.close()


SEG_ALL = ((0, CTX, 1), (CTX, T, 0))
SEG_X = ((CTX, T, 0),)


def load_tokens(nc, g):
    with ExitStack() as mem, Stage(nc, "load", "rows_in turned moved consts_in") as s:
        rows = mem.enter_context(sbuf(nc, "rows", [P, TT, D], F32))
        ps = [mem.enter_context(psum(nc, f"ld{i}", [P, 4, P], F32)) for i in range(2)]
        q = s.sem

        @s.body.sync
        def _(sp):
            sp.dma_start(g.cst[:, :], g.consts).then_inc(q["consts_in"], 16)
            sp.dma_start(rows[:, 0:CT, :], g.ctx[0].rearrange("(t p) d -> p t d", p=P)).then_inc(q["rows_in"], 16)
            sp.dma_start(rows[:, CT:TT, :], g.x[0].rearrange("(t p) d -> p t d", p=P)).then_inc(q["rows_in"], 16)

        @s.body.tensor
        def _(pe):
            pe.wait_ge(q["consts_in"], 16)
            pe.wait_ge(q["rows_in"], 32)
            for n in range(TT * 2):
                if n >= 2:
                    pe.wait_ge(q["moved"], n - 1)
                for j in range(4):
                    k = n % 2 * 4 + j
                    last = pe.transpose(ps[n % 2][:, j, :], rows[:, n // 2, k * P:(k + 1) * P], g.c(IDENT))
                last.then_inc(q["turned"], 1)

        @s.body.vector
        def _(v):
            for n in range(TT * 2):
                v.wait_ge(q["turned"], n + 1)
                v.tensor_copy(g.xT[:, n % 2 * 4:n % 2 * 4 + 4, n // 2 * P:(n // 2 + 1) * P],
                              ps[n % 2][:, :, :]).then_inc(q["moved"], 1)

    with Stage(nc, "cond", "cond_in sig_ready") as s:
        q = s.sem

        @s.body.sync
        def _(sp):
            with nc.allow_non_contiguous_dma(reason="2048 numbers, once"):
                sp.dma_start(g.cond[:, :, 0], g.cvec.rearrange("a (k p) -> p (a k)", p=P)).then_inc(q["cond_in"], 16)
                sp.dma_start(g.cond[:, :, 1], g.c_ctx.rearrange("(k p) -> p k", p=P)).then_inc(q["cond_in"], 16)

        @s.body.scalar
        def _(act):
            act.wait_ge(q["cond_in"], 32)
            act.activation(g.cond_sig[:, :, :], g.cond[:, :, :], ACT.Sigmoid).then_inc(q["sig_ready"], 1)

        @s.body.vector
        def _(v):
            v.wait_ge(q["sig_ready"], 1)
            ln = s.line(v, "dve")
            ln.link(v.tensor_tensor(g.cond[:, :, :], g.cond[:, :, :], g.cond_sig[:, :, :], ALU.mult))


def ada(nc, g, l):
    SLAB = 4 * P
    with ExitStack() as mem, Stage(nc, f"ada{l}", "w0_in w1_in w0_used w1_used full0 full1 free0 free1 vec_in") as s:
        wt = [mem.enter_context(sbuf(nc, f"ada_w{i}", [P, KD, SLAB], F32)) for i in range(2)]
        bias = mem.enter_context(sbuf(nc, "ada_b", [P, 6 * KD], F32))
        gain = mem.enter_context(sbuf(nc, "ada_g", [P, 2, KD], F32))
        ps = [mem.enter_context(psum(nc, f"ada_p{i}", [P, 512], F32)) for i in range(2)]
        q = s.sem
        w_in, w_used, full, free = [q["w0_in"], q["w1_in"]], [q["w0_used"], q["w1_used"]], [q["full0"], q["full1"]], [q["free0"], q["free1"]]
        rounds = 6 * D // SLAB // 2

        @s.body.sync
        def _(sp):
            ln = s.line(sp, "sp")
            with nc.allow_non_contiguous_dma(reason="vectors onto partitions"):
                sp.dma_start(bias[:, :], g.b_ada[l].rearrange("(j p) -> p j", p=P)).then_inc(q["vec_in"], 16)
                sp.dma_start(gain[:, 0, :], g.norm1_g[l].rearrange("(j p) -> p j", p=P)).then_inc(q["vec_in"], 16)
                sp.dma_start(gain[:, 1, :], g.norm2_g[l].rearrange("(j p) -> p j", p=P)).then_inc(q["vec_in"], 16)
            w = g.w_ada[l].rearrange("(k p) n -> p k n", p=P)
            with sp.Fori(0, rounds) as i:
                for j in range(2):
                    ln.hold(w_used[j], i + 1)
                    sp.dma_start(wt[j][:, :, :], w[:, :, bass.ds(i * (2 * SLAB) + j * SLAB, SLAB)]).then_inc(w_in[j], 16)

        @s.body.tensor
        def _(pe):
            ln = s.line(pe, "pe")
            ln.credit(*w_used)
            with pe.Fori(0, rounds) as i:
                for j in range(2):
                    ln.hold(w_in[j], i * 16 + 16)
                    ln.hold(free[j], i + 1)
                    for m in range(4):
                        for k in range(KD):
                            last = pe.matmul(ps[j][:, 2 * m:2 * m + 2], wt[j][:, k, m * P:(m + 1) * P],
                                             g.cond[:, k, :], start=k == 0, stop=k == KD - 1)
                    last.then_inc(full[j], 1)
                    ln.hold(full[j], i + 1)
                    ln.tell(w_used[j])

        @s.body.vector
        def _(v):
            ln = s.line(v, "dve")
            ln.credit(*free)
            v.wait_ge(q["vec_in"], 48)
            with v.Fori(0, rounds) as i:
                for j in range(2):
                    ln.hold(full[j], i + 1)
                    at = bass.ds(i * 8 + j * 4, 4)
                    ln.link(v.tensor_tensor(g.mods[:, at, :], ps[j][:, 0:8].rearrange("p (m v) -> p m v", v=2),
                                            bias[:, at].unsqueeze(2).broadcast_to([P, 4, 2]), ALU.add))
                    ln.tell(free[j])
                ln.restart()
            for n in range(2):
                sc = g.mods[:, (3 * n + 1) * KD:(3 * n + 2) * KD, :]
                ln.link(v.tensor_scalar(g.gs[:, n, :, :], sc, 1.0, None, ALU.add))
                ln.link(v.tensor_tensor(g.gs[:, n, :, :], g.gs[:, n, :, :],
                                        gain[:, n, :].unsqueeze(2).broadcast_to([P, KD, 2]), ALU.mult))


def norm(nc, g, name, segs, which, gain=None):
    with ExitStack() as mem, Stage(nc, name, "sq_ready sq_used mean_ready rstd_ready scaled gain_in") as s:
        sq = [mem.enter_context(sbuf(nc, f"sq{i}", [P, T], F32)) for i in range(2)]
        rs = mem.enter_context(sbuf(nc, "rs", [P, T], F32))
        fg = mem.enter_context(sbuf(nc, "fg", [P, KD], F32))
        ps = [mem.enter_context(psum(nc, f"np{i}", [P, 512], F32)) for i in range(len(segs))]
        q = s.sem
        lo, hi = segs[0][0], segs[-1][1]

        @s.body.sync
        def _(sp):
            if gain is not None:
                with nc.allow_non_contiguous_dma(reason="a vector onto partitions"):
                    sp.dma_start(fg[:, :], gain.rearrange("(j p) -> p j", p=P)).then_inc(q["gain_in"], 16)

        @s.body.scalar
        def _(act):
            ln = s.line(act, "act")
            for k in range(KD):
                if k >= 2:
                    act.wait_ge(q["sq_used"], k - 1)
                ln.link(act.activation(sq[k % 2][:, lo:hi], g.xT[:, k, lo:hi], ACT.Square))
                ln.tell(q["sq_ready"])
            act.wait_ge(q["mean_ready"], 1)
            ln.link(act.activation(rs[:, lo:hi], rs[:, lo:hi], ACT.Sqrt))
            ln.tell(q["rstd_ready"])
            if gain is not None:
                act.wait_ge(q["gain_in"], 16)
            for k in range(KD):
                act.wait_ge(q["scaled"], k + 1)
                for a, b, v in segs:
                    if gain is None:
                        ln.link(act.activation(g.hT[:, k, a:b], g.hT[:, k, a:b], ACT.Identity,
                                               scale=g.gs[:, which, k, v:v + 1],
                                               bias=g.mods[:, 3 * which * KD + k, v:v + 1]))
                    else:
                        ln.link(act.activation(g.hT[:, k, a:b], g.hT[:, k, a:b], ACT.Copy, scale=fg[:, k:k + 1]))

        @s.body.tensor
        def _(pe):
            for k in range(KD):
                pe.wait_ge(q["sq_ready"], k + 1)
                for n, (a, b, v) in enumerate(segs):
                    last = pe.matmul(ps[n][:, 0:b - a], g.c(ONES), sq[k % 2][:, a:b], start=k == 0, stop=k == KD - 1)
                last.then_inc(q["sq_used"], 1)

        @s.body.vector
        def _(v):
            ln = s.line(v, "dve")
            v.wait_ge(q["sq_used"], KD)
            for n, (a, b, _) in enumerate(segs):
                ln.link(v.tensor_scalar(rs[:, a:b], ps[n][:, 0:b - a], 1.0 / D, EPS, ALU.mult, ALU.add))
            ln.link(v.reciprocal(rs[:, lo:hi], rs[:, lo:hi]))
            ln.tell(q["mean_ready"])
            v.wait_ge(q["rstd_ready"], 1)
            for k in range(KD):
                ln.link(v.tensor_tensor(g.hT[:, k, lo:hi], g.xT[:, k, lo:hi], rs[:, lo:hi], ALU.mult))
                ln.tell(q["scaled"])


def project(nc, g, name, w, tiles, rhs, segs, out=None, residual=None):
    with ExitStack() as mem, Stage(nc, name, "w0_in w1_in w0_used w1_used full0 full1 full2 full3 a0 a1 a2 a3 v0 v1 v2 v3") as s:
        wt = [mem.enter_context(sbuf(nc, f"w{i}", [P, KD, 2 * P], F32)) for i in range(2)]
        ps = [mem.enter_context(psum(nc, f"pp{i}", [P, 512], F32)) for i in range(8)]
        q = s.sem
        w_in, w_used = [q["w0_in"], q["w1_in"]], [q["w0_used"], q["w1_used"]]
        full, a_free, v_free = [q["full0"], q["full1"], q["full2"], q["full3"]], [q["a0"], q["a1"], q["a2"], q["a3"]], [q["v0"], q["v1"], q["v2"], q["v3"]]
        rounds = tiles // 4
        both = len(segs) == 2 and residual is None

        @s.body.sync
        def _(sp):
            ln = s.line(sp, "sp")
            wv = w.rearrange("(k p) n -> p k n", p=P)
            with sp.Fori(0, rounds) as i:
                for j in range(2):
                    ln.hold(w_used[j], i + 1)
                    sp.dma_start(wt[j][:, :, :], wv[:, :, bass.ds(i * (4 * P) + j * 2 * P, 2 * P)]).then_inc(w_in[j], 16)

        @s.body.tensor
        def _(pe):
            ln = s.line(pe, "pe")
            ln.credit(*w_used)
            with pe.Fori(0, rounds) as i:
                for j in range(4):
                    if j % 2 == 0:
                        ln.hold(w_in[j // 2], i * 16 + 16)
                    if both:
                        ln.hold(a_free[j], i + 1)
                    ln.hold(v_free[j], i + 1)
                    for n, (a, b, _) in enumerate(segs):
                        for k in range(KD):
                            last = pe.matmul(ps[2 * j + n][:, 0:b - a], wt[j // 2][:, k, j % 2 * P:(j % 2 + 1) * P],
                                             rhs[:, k, a:b], start=k == 0, stop=k == KD - 1)
                    last.then_inc(full[j], 1)
                    if j % 2:
                        ln.hold(full[j], i + 1)
                        ln.tell(w_used[j // 2])

        if both:
            @s.body.scalar
            def _(act):
                ln = s.line(act, "act")
                ln.credit(*a_free)
                with act.Fori(0, rounds) as i:
                    for j in range(4):
                        a, b, _ = segs[0]
                        ln.hold(full[j], i + 1)
                        ln.link(act.activation(out[:, bass.ds(i * 4 + j, 1), a:b], ps[2 * j][:, 0:b - a].unsqueeze(1), ACT.Copy))
                        ln.tell(a_free[j])
                    ln.restart()

        @s.body.vector
        def _(v):
            ln = s.line(v, "dve")
            ln.credit(*v_free)
            with v.Fori(0, rounds) as i:
                for j in range(4):
                    ln.hold(full[j], i + 1)
                    for n, (a, b, c) in enumerate(segs):
                        tile = bass.ds(i * 4 + j, 1)
                        if residual is not None:
                            ln.link(v.scalar_tensor_tensor(
                                g.xT[:, tile, a:b], ps[2 * j + n][:, 0:b - a].unsqueeze(1),
                                g.mods[:, bass.ds(i * 4 + j + residual * KD, 1), c:c + 1],
                                g.xT[:, tile, a:b], ALU.mult, ALU.add))
                        elif n or not both:
                            ln.link(v.tensor_copy(out[:, tile, a:b], ps[2 * j + n][:, 0:b - a].unsqueeze(1)))
                    ln.tell(v_free[j])
                ln.restart()


def normalize(nc, g, name, x, const, factor, center=False, pooled=False):
    G = x.shape[1]
    per = 2 if pooled else 1
    units = G // per
    HALF = T // 2
    with ExitStack() as mem, Stage(nc, name, "asked summed used sums_read root_asked root_done") as s:
        sq = mem.enter_context(sbuf(nc, "nsq", [P, 2, per, T]))
        rs = mem.enter_context(sbuf(nc, "nrs", [P, 2, T]))
        ps = [[mem.enter_context(psum(nc, "nps", [P, 512])) for _ in range(2)] for _ in range(2)]
        q = s.sem
        passes = 2 if center else 1

        @s.body.tensor
        def _(pe):
            n = 0
            for ps_no in range(passes):
                for u in range(units):
                    pe.wait_ge(q["asked"], n + 1)
                    if n >= 2:
                        pe.wait_ge(q["sums_read"], n - 1)
                    for half in range(2):
                        for j in range(per):
                            src = x[:, u * per + j, :] if center and ps_no == 0 else sq[:, u % 2, j, :]
                            last = pe.matmul(ps[n % 2][half][:, 0:HALF], g.c(const), src[:, half * HALF:(half + 1) * HALF],
                                             start=j == 0, stop=j == per - 1)
                    last.then_inc(q["summed"], 1)
                    n += 1

        @s.body.vector
        def _(v):
            ln = s.line(v, "dve")
            n = 0
            if center:
                ln.tell(q["asked"], units)
                for u in range(units):
                    v.wait_ge(q["summed"], n + 1)
                    for half in range(2):
                        cut = slice(half * HALF, (half + 1) * HALF)
                        for j in range(per):
                            xs = x[:, u * per + j, cut]
                            ln.link(v.scalar_tensor_tensor(xs, ps[n % 2][half][:, 0:HALF], -factor, xs, ALU.mult, ALU.add))
                    ln.tell(q["sums_read"])
                    n += 1

            def square(u):
                for j in range(per):
                    ln.link(v.tensor_tensor(sq[:, u % 2, j, :], x[:, u * per + j, :], x[:, u * per + j, :], ALU.mult))
                ln.tell(q["asked"])

            def scale(u):
                v.wait_ge(q["root_done"], u + 1)
                for j in range(per):
                    ln.link(v.tensor_tensor(x[:, u * per + j, :], x[:, u * per + j, :], rs[:, u % 2, :], ALU.mult))

            square(0)
            for u in range(units):
                v.wait_ge(q["summed"], n + 1)
                for half in range(2):
                    ln.link(v.tensor_scalar(rs[:, u % 2, half * HALF:(half + 1) * HALF], ps[n % 2][half][:, 0:HALF],
                                            factor, EPS, ALU.mult, ALU.add))
                ln.tell(q["sums_read"])
                n += 1
                ln.link(v.reciprocal(rs[:, u % 2, :], rs[:, u % 2, :]))
                ln.tell(q["root_asked"])
                if u + 1 < units:
                    square(u + 1)
                if u >= 1:
                    scale(u - 1)
            scale(units - 1)

        @s.body.scalar
        def _(act):
            ln = s.line(act, "act")
            for u in range(units):
                act.wait_ge(q["root_asked"], u + 1)
                ln.link(act.activation(rs[:, u % 2, :], rs[:, u % 2, :], ACT.Sqrt))
                ln.tell(q["root_done"])


PADC = CONV_C // 2
LONG = PADC + CTX + PADC + SEQ + PADC
X_AT = CTX + PADC


def conv(v, ln, out, padded, tap, taps, bias, pad):
    n = CTX + pad + SEQ
    order = [taps // 2] + [k for k in range(taps) if k != taps // 2]
    for k in order:
        src = padded[:, k:k + n]
        if k == taps // 2:
            if bias is None:
                ln.link(v.tensor_scalar(out[:, 0:n], src, tap(k), None, ALU.mult))
            else:
                ln.link(v.tensor_scalar(out[:, 0:n], src, tap(k), bias, ALU.mult, ALU.add))
        else:
            ln.link(v.scalar_tensor_tensor(out[:, 0:n], src, tap(k), out[:, 0:n], ALU.mult, ALU.add))


def conformer(nc, g, l):
    with ExitStack() as top:
        pc = top.enter_context(sbuf(nc, "conf_p", [P, 4, T]))
        y = top.enter_context(sbuf(nc, "conf_y", [P, WT, T]))
        vec = top.enter_context(sbuf(nc, "conf_v", [P, 3, WT]))
        project(nc, g, f"confp{l}", g.w_in[l][:, CONF0:CONF0 + 2 * W], 4, g.hT, SEG_ALL, out=pc)
        with ExitStack() as mem, Stage(nc, f"conf{l}", "vec_in sig_ready") as s:
            pad = mem.enter_context(sbuf(nc, "conf_pad", [P, WT, LONG]))
            acc = mem.enter_context(sbuf(nc, "conf_acc", [P, WT, LONG]))
            taps = mem.enter_context(sbuf(nc, "conf_w", [P, WT, CONV_C]))
            q = s.sem

            @s.body.sync
            def _(sp):
                with nc.allow_non_contiguous_dma(reason="small weights onto partitions"):
                    for n, a in enumerate((g.conf_dw_b, g.conf_ln_g, g.conf_ln_b)):
                        sp.dma_start(vec[:, n, :], a[l].rearrange("(t p) -> p t", p=P)).then_inc(q["vec_in"], 16)
                    for n in range(WT):
                        sp.dma_start(taps[:, n, :], g.conf_dw_w[l][:, n * P:(n + 1) * P].rearrange("k p -> p k")).then_inc(q["vec_in"], 16)

            @s.body.scalar
            def _(act):
                ln = s.line(act, "act")
                ln.link(act.activation(pc[:, 2:4, :], pc[:, 2:4, :], ACT.Sigmoid))
                ln.tell(q["sig_ready"])

            @s.body.vector
            def _(v):
                ln = s.line(v, "dve")
                ln.link(v.memset(pad[:, :, :], 0.0))
                v.wait_ge(q["sig_ready"], 1)
                ln.link(v.tensor_tensor(pad[:, :, PADC:PADC + CTX], pc[:, 0:2, 0:CTX], pc[:, 2:4, 0:CTX], ALU.mult))
                ln.link(v.tensor_tensor(pad[:, :, PADC + X_AT:PADC + X_AT + SEQ], pc[:, 0:2, CTX:T], pc[:, 2:4, CTX:T], ALU.mult))
                v.wait_ge(q["vec_in"], 80)
                for n in range(WT):
                    conv(v, ln, acc[:, n, :], pad[:, n, :], lambda k: taps[:, n, k:k + 1], CONV_C, vec[:, 0, n:n + 1], PADC)
                ln.link(v.tensor_copy(y[:, :, 0:CTX], acc[:, :, 0:CTX]))
                ln.link(v.tensor_copy(y[:, :, CTX:T], acc[:, :, X_AT:X_AT + SEQ]))
        normalize(nc, g, f"confn{l}", y[:, :, :], ONES, 1.0 / W, center=True, pooled=True)
        with ExitStack() as mem, Stage(nc, f"confo{l}", "lin_ready sig_ready") as s:
            sig = mem.enter_context(sbuf(nc, "conf_s", [P, WT, T]))
            q = s.sem

            @s.body.vector
            def _(v):
                ln = s.line(v, "dve")
                for n in range(WT):
                    ln.link(v.tensor_scalar(y[:, n, :], y[:, n, :], vec[:, 1, n:n + 1], vec[:, 2, n:n + 1], ALU.mult, ALU.add))
                    ln.tell(q["lin_ready"])
                for n in range(WT):
                    v.wait_ge(q["sig_ready"], n + 1)
                    ln.link(v.tensor_tensor(g.oT[:, 3, n, :], y[:, n, :], sig[:, n, :], ALU.mult))

            @s.body.scalar
            def _(act):
                ln = s.line(act, "act")
                for n in range(WT):
                    act.wait_ge(q["lin_ready"], n + 1)
                    ln.link(act.activation(sig[:, n, :], y[:, n, :], ACT.Sigmoid))
                    ln.tell(q["sig_ready"])


def sgu(nc, g, l):
    with ExitStack() as top:
        pc = top.enter_context(sbuf(nc, "sgu_p", [P, 4, T]))
        project(nc, g, f"sgup{l}", g.w_in[l][:, SGU0:SGU0 + 2 * W], 4, g.hT, SEG_ALL, out=pc)
        with Stage(nc, f"sgug{l}", "") as s:
            @s.body.scalar
            def _(act):
                ln = s.line(act, "act")
                ln.link(act.activation(pc[:, :, :], pc[:, :, :], ACT.Gelu_apprx_tanh))
        normalize(nc, g, f"sgun{l}", pc[:, 2:4, :], ONES, 1.0 / W, center=True, pooled=True)
        with ExitStack() as mem, Stage(nc, f"sgu{l}", "w_in turned moved mixed read lin_ready") as s:
            vec = mem.enter_context(sbuf(nc, "sgu_v", [P, 2, WT]))
            ws = mem.enter_context(sbuf(nc, "sgu_w", [P, H, P]))
            wsT = mem.enter_context(sbuf(nc, "sgu_wT", [P, H, P]))
            bs = mem.enter_context(sbuf(nc, "sgu_b", [1, H * P]))
            vt = mem.enter_context(sbuf(nc, "sgu_vt", [P, TT, W]))
            ps = [mem.enter_context(psum(nc, "sgu_ps", [P, 512])) for _ in range(4)]
            q = s.sem

            @s.body.sync
            def _(sp):
                with nc.allow_non_contiguous_dma(reason="small weights onto partitions"):
                    sp.dma_start(vec[:, 0, :], g.sgu_ln_g[l].rearrange("(t p) -> p t", p=P)).then_inc(q["w_in"], 16)
                    sp.dma_start(vec[:, 1, :], g.sgu_ln_b[l].rearrange("(t p) -> p t", p=P)).then_inc(q["w_in"], 16)
                sp.dma_start(ws[:, :, :], g.sgu_w_s[l].rearrange("g p s -> p g s")).then_inc(q["w_in"], 16)
                sp.dma_start(bs[:, :], g.sgu_b_s[l:l + 1].rearrange("a g p -> a (g p)")).then_inc(q["w_in"], 16)

            @s.body.tensor
            def _(pe):
                pe.wait_ge(q["w_in"], 64)
                for h in range(H):
                    last = pe.transpose(ps[0][:, h * P:(h + 1) * P], ws[:, h, :], g.c(IDENT))
                last.then_inc(q["turned"], 1)
                pe.wait_ge(q["lin_ready"], WT)
                for t in range(TT):
                    if t >= 1:
                        pe.wait_ge(q["moved"], t)
                    for n in range(WT):
                        last = pe.transpose(ps[(t + 1) % 2][:, n * P:(n + 1) * P], pc[:, 2 + n, t * P:(t + 1) * P], g.c(IDENT))
                    last.then_inc(q["turned"], 1)
                pe.wait_ge(q["moved"], TT + 1)
                for t in range(TT):
                    if t >= 2:
                        pe.wait_ge(q["read"], t - 1)
                    for h in range(H):
                        o = ps[2 + t % 2][h % 2 * HD:(h % 2 + 1) * HD, h // 2 * P:(h // 2 + 1) * P]
                        pe.matmul(o, vt[:, t, h * HD:(h + 1) * HD], wsT[:, h, :], start=True, stop=False)
                        last = pe.matmul(o, g.c(ONES)[0:1, 0:HD], bs[0:1, h * P:(h + 1) * P], start=False, stop=True)
                    last.then_inc(q["mixed"], 1)

            @s.body.vector
            def _(v):
                ln = s.line(v, "dve")
                v.wait_ge(q["w_in"], 64)
                for n in range(WT):
                    ln.link(v.tensor_scalar(pc[:, 2 + n, :], pc[:, 2 + n, :], vec[:, 0, n:n + 1], vec[:, 1, n:n + 1], ALU.mult, ALU.add))
                    ln.tell(q["lin_ready"])
                v.wait_ge(q["turned"], 1)
                ln.link(v.tensor_copy(wsT[:, :, :], ps[0][:, :].rearrange("p (h s) -> p h s", h=H)))
                ln.tell(q["moved"])
                for t in range(TT):
                    v.wait_ge(q["turned"], t + 2)
                    ln.link(v.tensor_copy(vt[:, t, :], ps[(t + 1) % 2][:, 0:W]))
                    ln.tell(q["moved"])
                for t in range(TT):
                    v.wait_ge(q["mixed"], t + 1)
                    ln.link(v.tensor_tensor(g.oT[:, 2, :, t * P:(t + 1) * P], pc[:, 0:2, t * P:(t + 1) * P],
                                            ps[2 + t % 2][:, 0:2 * P].rearrange("p (n t) -> p n t", n=2), ALU.mult))
                    ln.tell(q["read"])


def merge(nc, g, l, segs):
    with ExitStack() as mem, Stage(nc, f"merge{l}", "g0_in g1_in b0_in b1_in w0_used w1_used gate0 gate1 val0 val1 sig0 sig1 free0 free1") as s:
        wg = [mem.enter_context(sbuf(nc, "wg", [P, KD, 4, P])) for _ in range(2)]
        wb = [mem.enter_context(sbuf(nc, "wb", [P, 4, WT, P])) for _ in range(2)]
        sg = [mem.enter_context(sbuf(nc, "sg", [P, T])) for _ in range(2)]
        tmp = mem.enter_context(sbuf(nc, "tmp", [P, T]))
        pg = [[mem.enter_context(psum(nc, "pg", [P, 512])) for _ in segs] for _ in range(2)]
        pv = [[mem.enter_context(psum(nc, "pv", [P, 512])) for _ in segs] for _ in range(2)]
        q = s.sem
        g_in, b_in, used = [q["g0_in"], q["g1_in"]], [q["b0_in"], q["b1_in"]], [q["w0_used"], q["w1_used"]]
        gate, val, sig, free = [q["gate0"], q["gate1"]], [q["val0"], q["val1"]], [q["sig0"], q["sig1"]], [q["free0"], q["free1"]]
        lo, hi = segs[0][0], segs[-1][1]

        @s.body.sync
        def _(sp):
            ln = s.line(sp, "sp")
            gw = g.w_in[l][:, GATE0:].rearrange("(k p) (b n) -> p k b n", p=P, b=4)
            bw = g.w_branch[l].rearrange("b (k p) n -> p b k n", p=P)
            with sp.Fori(0, KD // 2) as i:
                for j in range(2):
                    ln.hold(used[j], i + 1)
                    at = bass.ds(i * (2 * P) + j * P, P)
                    for b in range(4):
                        sp.dma_start(wg[j][:, :, b, :], gw[:, :, b, at]).then_inc(g_in[j], 16)
                        sp.dma_start(wb[j][:, b, :, :], bw[:, b, :, at]).then_inc(b_in[j], 16)

        @s.body.tensor
        def _(pe):
            ln = s.line(pe, "pe")
            ln.credit(*used)
            with pe.Fori(0, KD // 2) as i:
                for j in range(2):
                    ln.hold(g_in[j], i * 64 + 64)
                    ln.hold(b_in[j], i * 64 + 64)
                    for b in range(4):
                        u = b % 2
                        ln.hold(free[u], i * 4 + j * 2 + b // 2 + 1)
                        for n, (a, e, _) in enumerate(segs):
                            for k in range(KD):
                                last = pe.matmul(pg[u][n][:, 0:e - a], wg[j][:, k, b, :], g.hT[:, k, a:e], start=k == 0, stop=k == KD - 1)
                        last.then_inc(gate[u], 1)
                        for n, (a, e, _) in enumerate(segs):
                            for k in range(WT):
                                last = pe.matmul(pv[u][n][:, 0:e - a], wb[j][:, b, k, :], g.oT[:, b, k, a:e], start=k == 0, stop=k == WT - 1)
                        last.then_inc(val[u], 1)
                    ln.hold(val[1], i * 4 + j * 2 + 2)
                    ln.tell(used[j])

        @s.body.scalar
        def _(act):
            ln = s.line(act, "act")
            with act.Fori(0, KD // 2) as i:
                for j in range(2):
                    for b in range(4):
                        u, n_done = b % 2, i * 4 + j * 2 + b // 2
                        ln.hold(gate[u], n_done + 1)
                        ln.hold(free[u], n_done + 1)
                        for n, (a, e, _) in enumerate(segs):
                            ln.link(act.activation(sg[u][:, a:e], pg[u][n][:, 0:e - a], ACT.Sigmoid))
                        ln.tell(sig[u])
                ln.restart()

        @s.body.vector
        def _(v):
            ln = s.line(v, "dve")
            ln.credit(*free)
            with v.Fori(0, KD // 2) as i:
                for j in range(2):
                    m = g.mT[:, bass.ds(i * 2 + j, 1), lo:hi]
                    for b in range(4):
                        u, n_done = b % 2, i * 4 + j * 2 + b // 2
                        ln.hold(sig[u], n_done + 1)
                        ln.hold(val[u], n_done + 1)
                        for n, (a, e, _) in enumerate(segs):
                            o = m[:, :, a - lo:e - lo] if b == 0 else tmp[:, a:e].unsqueeze(1)
                            ln.link(v.tensor_tensor(o, sg[u][:, a:e].unsqueeze(1), pv[u][n][:, 0:e - a].unsqueeze(1), ALU.mult))
                        ln.tell(free[u])
                        if b:
                            ln.link(v.tensor_tensor(m, m, tmp[:, lo:hi].unsqueeze(1), ALU.add))
                ln.restart()


def shift_tiles(v, ln, src, out, mmu, omu):
    for t in range(src.shape[1]):
        ln.link(v.tensor_scalar(out[:, t, :], src[:, t, :], omu[:, t:t + 1], None, ALU.mult))

        def add(o, i, kind):
            ln.link(v.scalar_tensor_tensor(o, i, mmu[:, t, kind:kind + 1], o, ALU.mult, ALU.add))

        add(out[:, t, 1:CTX], src[:, t, 0:CTX - 1], 0)
        add(out[:, t, 0:CTX - 1], src[:, t, 1:CTX], 1)
        og = out[:, t, CTX:T].rearrange("p (r w) -> p r w", w=GW)
        sg = src[:, t, CTX:T].rearrange("p (r w) -> p r w", w=GW)
        add(og[:, :, 1:GW], sg[:, :, 0:GW - 1], 0)
        add(og[:, :, 0:GW - 1], sg[:, :, 1:GW], 1)
        add(og[:, 1:GR, :], sg[:, 0:GR - 1, :], 2)
        add(og[:, 0:GR - 1, :], sg[:, 1:GR, :], 3)


def rwkv_front(nc, g, l, vec):
    HALF = T // 2
    with ExitStack() as prep:
        def tmp(name, shape):
            return prep.enter_context(sbuf(nc, name, shape))

        gate, bonus = tmp("rk_gate", [P, WT, T]), tmp("rk_bonus", [P, WT, T])
        pq = tmp("rk_q", [P, 8, T])
        with ExitStack() as first:
            raw = first.enter_context(sbuf(nc, "rk_p", [P, 8, T]))
            project(nc, g, f"rkp{l}", g.w_in[l][:, RWKV0:RWKV0 + 8 * P], 8, g.hT, SEG_ALL, out=raw)
            with ExitStack() as mem, Stage(nc, f"rks{l}", "vec_in") as s:
                mu = mem.enter_context(sbuf(nc, "mu", [P, 2, 8]))
                mmu = mem.enter_context(sbuf(nc, "mmu", [P, 8, 4]))
                q = s.sem

                @s.body.sync
                def _(sp):
                    with nc.allow_non_contiguous_dma(reason="vectors onto partitions"):
                        sp.dma_start(mu[:, 0, :], g.rwkv_mu[l].rearrange("(t p) -> p t", p=P)).then_inc(q["vec_in"], 16)
                        for n, a in enumerate((g.rwkv_k_k[l], g.rwkv_k_a[l], g.rwkv_r_k[l].rearrange("h n -> (h n)"),
                                               g.rwkv_gn_g[l].rearrange("h n -> (h n)"), g.rwkv_gn_b[l].rearrange("h n -> (h n)"))):
                            sp.dma_start(vec[:, n, :], a.rearrange("(t p) -> p t", p=P)).then_inc(q["vec_in"], 16)

                @s.body.vector
                def _(v):
                    ln = s.line(v, "dve")
                    v.wait_ge(q["vec_in"], 96)
                    ln.link(v.tensor_scalar(mu[:, 1, :], mu[:, 0, :], -1.0, 1.0, ALU.mult, ALU.add))
                    ln.link(v.tensor_tensor(mmu[:, :, :], mu[:, 0, :].unsqueeze(2).broadcast_to([P, 8, 4]),
                                            g.c(QUAD, 4).unsqueeze(1).broadcast_to([P, 8, 4]), ALU.mult))
                    shift_tiles(v, ln, raw, pq, mmu, mu[:, 1, :])

        aT, kd = tmp("rk_a", [P, 2 * WT, T]), tmp("rk_kd", [P, 2 * WT, T])
        kk, lw = tmp("rk_kk", [P, WT, T]), tmp("rk_lw", [P, TT, 2 * W])
        with ExitStack() as mem, Stage(nc, f"rkl{l}", "w_in act_ready full read") as s:
            g2 = mem.enter_context(sbuf(nc, "g2", [P, W]))
            wa = mem.enter_context(sbuf(nc, "w2a2", [P, 2, W]))
            w0 = mem.enter_context(sbuf(nc, "w0", [1, 2 * W]))
            a0 = mem.enter_context(sbuf(nc, "a0", [P, 2, WT]))
            ps = [mem.enter_context(psum(nc, "lps", [P, 512])) for _ in range(8)]
            q = s.sem
            jobs = [("gate", 0, n) for n in range(WT)] + [("a", d, n) for d in range(2) for n in range(WT)]
            jobs += [("w", t, 0) for t in range(TT)]

            @s.body.sync
            def _(sp):
                sp.dma_start(g2[:, :], g.rwkv_g2[l]).then_inc(q["w_in"], 16)
                sp.dma_start(wa[0:HD, :, :], g.rwkv_w2[l].rearrange("d r w -> r d w")).then_inc(q["w_in"], 16)
                sp.dma_start(wa[HD:P, :, :], g.rwkv_a2[l].rearrange("d r w -> r d w")).then_inc(q["w_in"], 16)
                sp.dma_start(w0[:, :], g.rwkv_w0[l:l + 1].rearrange("a d w -> a (d w)")).then_inc(q["w_in"], 16)
                with nc.allow_non_contiguous_dma(reason="vectors onto partitions"):
                    for d in range(2):
                        sp.dma_start(a0[:, d, :], g.rwkv_a0[l, d].rearrange("(t p) -> p t", p=P)).then_inc(q["w_in"], 16)

            @s.body.tensor
            def _(pe):
                pe.wait_ge(q["w_in"], 96)
                pe.wait_ge(q["act_ready"], 1)
                for n, (kind, d, j) in enumerate(jobs):
                    if n >= 4:
                        pe.wait_ge(q["read"], n - 3)
                    b = n % 4 * 2
                    if kind == "w":
                        pe.matmul(ps[b][:, :], pq[0:HD, 6, d * P:(d + 1) * P], wa[0:HD, :, :].rearrange("r d w -> r (d w)"),
                                  start=True, stop=False)
                        last = pe.matmul(ps[b][:, :], g.c(ONES)[0:1, :], w0[0:1, :], start=False, stop=True)
                    for half in range(2 if kind != "w" else 0):
                        cut = slice(half * HALF, (half + 1) * HALF)
                        lhs, rhs = ((g2[:, j * P:(j + 1) * P], pq[:, 7, cut]) if kind == "gate" else
                                    (wa[HD:P, d, j * P:(j + 1) * P], pq[HD:P, 6, cut]))
                        last = pe.matmul(ps[b + half][:, 0:HALF], lhs, rhs, start=True, stop=True)
                    last.then_inc(q["full"], 1)

            @s.body.scalar
            def _(act):
                ln = s.line(act, "act")
                ln.link(act.activation(pq[0:HD, 6, :], pq[0:HD, 6, :], ACT.Tanh))
                ln.link(act.activation(pq[:, 7, :], pq[:, 7, :], ACT.Sigmoid))
                ln.tell(q["act_ready"])
                act.wait_ge(q["w_in"], 96)
                for n, (kind, d, j) in enumerate(jobs):
                    act.wait_ge(q["full"], n + 1)
                    b = n % 4 * 2
                    if kind == "w":
                        ln.link(act.activation(lw[:, d, :], ps[b][:, :], ACT.Sigmoid))
                    for half in range(2 if kind != "w" else 0):
                        cut = slice(half * HALF, (half + 1) * HALF)
                        if kind == "gate":
                            ln.link(act.activation(gate[:, j, cut], ps[b + half][:, 0:HALF], ACT.Copy))
                        else:
                            ln.link(act.activation(aT[:, d * WT + j, cut], ps[b + half][:, 0:HALF], ACT.Sigmoid, bias=a0[:, d, j:j + 1]))
                    ln.tell(q["read"])

            @s.body.vector
            def _(v):
                ln = s.line(v, "dve")
                for n in range(WT):
                    ln.link(v.tensor_scalar(kk[:, n, :], pq[:, 2 + n, :], vec[:, 0, n:n + 1], None, ALU.mult))
        normalize(nc, g, f"rkn{l}", kk[:, :, :], BLK, 1.0)
        with ExitStack() as mem, Stage(nc, f"rkb{l}", "prod_ready summed ready bonus_ready stored") as s:
            one_ka = mem.enter_context(sbuf(nc, "one_ka", [P, WT]))
            t = mem.enter_context(sbuf(nc, "rk_t", [P, WT, T]))
            ps = [mem.enter_context(psum(nc, "bps", [P, 512])) for _ in range(4)]
            q = s.sem

            @s.body.vector
            def _(v):
                ln = s.line(v, "dve")
                ln.link(v.tensor_scalar(one_ka[:, :], vec[:, 1, :], -1.0, 1.0, ALU.mult, ALU.add))
                for d in range(2):
                    for n in range(WT):
                        m = d * WT + n
                        ln.link(v.tensor_scalar(kd[:, m, :], aT[:, m, :], vec[:, 1, n:n + 1], one_ka[:, n:n + 1], ALU.mult, ALU.add))
                        ln.link(v.tensor_tensor(kd[:, m, :], kd[:, m, :], pq[:, 2 + n, :], ALU.mult))
                        ln.link(v.tensor_tensor(aT[:, m, :], aT[:, m, :], kk[:, n, :], ALU.mult))
                ln.tell(q["ready"])
                ln.link(v.tensor_tensor(t[:, :, :], kd[:, 0:WT, :], kd[:, WT:2 * WT, :], ALU.add))
                for n in range(WT):
                    ln.link(v.scalar_tensor_tensor(t[:, n, :], t[:, n, :], vec[:, 2, n:n + 1], pq[:, n, :], ALU.mult, ALU.mult))
                ln.tell(q["prod_ready"])
                v.wait_ge(q["summed"], 1)
                for n in range(WT):
                    for half in range(2):
                        cut = slice(half * HALF, (half + 1) * HALF)
                        ln.link(v.tensor_tensor(bonus[:, n, cut], pq[:, 4 + n, cut], ps[2 * n + half][:, 0:HALF], ALU.mult))
                ln.tell(q["bonus_ready"])

            @s.body.tensor
            def _(pe):
                pe.wait_ge(q["prod_ready"], 1)
                for n in range(WT):
                    for half in range(2):
                        last = pe.matmul(ps[2 * n + half][:, 0:HALF], g.c(BLK), t[:, n, half * HALF:(half + 1) * HALF], start=True, stop=True)
                last.then_inc(q["summed"], 1)

            @s.body.sync
            def _(sp):
                f = g.rk_feat.rearrange("n p t -> p n t")
                sp.dma_start(f[:, 0:2, :], pq[:, 0:2, :]).then_inc(q["stored"], 16)
                sp.dma_start(f[:, 2:4, :], pq[:, 4:6, :]).then_inc(q["stored"], 16)
                sp.dma_start(f[:, 4:6, :], kk[:, :, :]).then_inc(q["stored"], 16)
                sp.dma_start(g.rk_logw.rearrange("(t p) n -> p t n", p=P), lw[:, :, :]).then_inc(q["stored"], 16)
                sp.wait_ge(q["ready"], 1)
                sp.dma_start(f[:, 6:10, :], kd[:, :, :]).then_inc(q["stored"], 16)
                sp.dma_start(f[:, 10:14, :], aT[:, :, :]).then_inc(q["stored"], 16)
                sp.dma_start(f[:, 14:16, :], gate[:, :, :]).then_inc(q["stored"], 16)
                sp.wait_ge(q["bonus_ready"], 1)
                sp.dma_start(f[:, 16:18, :], bonus[:, :, :]).then_inc(q["stored"], 16)
                sp.wait_ge(q["stored"], 128)


def rwkv_end(nc, g, l, y, vec):
    normalize(nc, g, f"rky{l}", y[:, :, :], BLK, 1.0 / HD, center=True)
    with ExitStack() as mem, Stage(nc, f"rko{l}", "back_in") as s:
        gb = mem.enter_context(sbuf(nc, "rk_gb", [P, 2 * WT, T]))

        @s.body.sync
        def _(sp):
            sp.dma_start(gb[:, :, :], g.rk_feat[14:18].rearrange("n p t -> p n t")).then_inc(s.sem["back_in"], 16)

        @s.body.vector
        def _(v):
            ln = s.line(v, "dve")
            for m in range(2 * WT):
                n = m % WT
                ln.link(v.tensor_scalar(y[:, m, :], y[:, m, :], vec[:, 3, n:n + 1], vec[:, 4, n:n + 1], ALU.mult, ALU.add))
            ln.link(v.tensor_tensor(y[:, 0:WT, :], y[:, 0:WT, :], y[:, WT:2 * WT, :], ALU.add))
            v.wait_ge(s.sem["back_in"], 16)
            ln.link(v.tensor_tensor(y[:, 0:WT, :], y[:, 0:WT, :], gb[:, WT:2 * WT, :], ALU.add))
            ln.link(v.tensor_tensor(g.oT[:, 0, :, :], y[:, 0:WT, :], gb[:, 0:WT, :], ALU.mult))


def gdn_front(nc, g, l, zs, gd, beta):
    PADG = CONV_G // 2
    LONGG = PADG + CTX + PADG + SEQ + PADG
    with ExitStack() as prep:
        raw = prep.enter_context(sbuf(nc, "gd_p", [P, 8, T]))
        f = prep.enter_context(sbuf(nc, "gd_f", [P, 6, T]))
        project(nc, g, f"gdp{l}", g.w_in[l][:, GDN0:GDN0 + 8 * P], 8, g.hT, SEG_ALL, out=raw)
        with ExitStack() as mem, Stage(nc, f"gdc{l}", "w_in full conv_ready sig_ready asked given") as s:
            pad = mem.enter_context(sbuf(nc, "gd_pad", [P, 6, LONGG]))
            acc = mem.enter_context(sbuf(nc, "gd_acc", [P, LONGG]))
            taps = mem.enter_context(sbuf(nc, "gd_taps", [P, 6, CONV_G]))
            wab = mem.enter_context(sbuf(nc, "gd_wab", [P, KD, 16]))
            rowv = mem.enter_context(sbuf(nc, "gd_rowv", [P, 2, 8]))
            sp0 = mem.enter_context(sbuf(nc, "gd_sp0", [P, TT, 8]))
            sp1 = mem.enter_context(sbuf(nc, "gd_sp1", [P, TT, 8]))
            sig = mem.enter_context(sbuf(nc, "gd_sig", [P, 8, T]))
            ps = mem.enter_context(psum(nc, "gab", [P, 512]))
            q = s.sem
            ab = mem.enter_context(sbuf(nc, "gd_ab", [P, TT, 16]))

            @s.body.sync
            def _(sp):
                with nc.allow_non_contiguous_dma(reason="small weights onto partitions"):
                    for n in range(6):
                        sp.dma_start(taps[:, n, :], g.gdn_conv_w[l][:, n * P:(n + 1) * P].rearrange("k p -> p k")).then_inc(q["w_in"], 16)
                    sp.dma_start(wab[:, :, :], g.w_in[l][:, AB0:AB0 + 16].rearrange("(k p) n -> p k n", p=P)).then_inc(q["w_in"], 16)
                    for n, a in enumerate((g.gdn_a_log, g.gdn_dt_bias)):
                        sp.dma_start(rowv[:, n, :], a[l].rearrange("d h -> (d h)").partition_broadcast(P)).then_inc(q["w_in"], 16)

            @s.body.tensor
            def _(pe):
                pe.wait_ge(q["w_in"], 144)
                for t in range(TT):
                    for k in range(KD):
                        last = pe.matmul(ps[:, t * 16:t * 16 + 16], g.hT[:, k, t * P:(t + 1) * P], wab[:, k, :], start=k == 0, stop=k == KD - 1)
                last.then_inc(q["full"], 1)

            @s.body.scalar
            def _(act):
                ln = s.line(act, "act")
                ln.link(act.activation(sig[:, 6:8, :], raw[:, 6:8, :], ACT.Sigmoid))
                ln.tell(q["sig_ready"])
                act.wait_ge(q["asked"], 1)
                ln.link(act.activation(beta[:, :, :], ab[:, :, 8:16], ACT.Sigmoid))
                act.wait_ge(q["asked"], 2)
                ln.link(act.activation(sp1[:, :, :], sp1[:, :, :], ACT.Exp, scale=-1.0))
                ln.link(act.activation(rowv[:, 0, :], rowv[:, 0, :], ACT.Exp))
                ln.link(act.activation(sp1[:, :, :], sp1[:, :, :], ACT.Ln, bias=1.0))
                ln.tell(q["given"])
                for n in range(6):
                    act.wait_ge(q["conv_ready"], n + 1)
                    ln.link(act.activation(sig[:, n, :], f[:, n, :], ACT.Sigmoid))
                    ln.tell(q["sig_ready"])

            @s.body.vector
            def _(v):
                ln = s.line(v, "dve")
                ln.link(v.memset(pad[:, :, :], 0.0))
                v.wait_ge(q["w_in"], 144)
                v.wait_ge(q["full"], 1)
                ln.link(v.tensor_copy(ab[:, :, :], ps[:, 0:TT * 16].rearrange("p (t n) -> p t n", n=16)))
                ln.tell(q["asked"])
                dt = rowv[:, 1, :].unsqueeze(1).broadcast_to([P, TT, 8])
                ln.link(v.tensor_tensor(sp0[:, :, :], ab[:, :, 0:8], dt, ALU.add))
                ln.link(v.scalar_tensor_tensor(sp1[:, :, :], sp0[:, :, :], -1.0, sp0[:, :, :], ALU.mult, ALU.max))
                ln.tell(q["asked"])
                ln.link(v.tensor_copy(pad[:, :, PADG:PADG + CTX], raw[:, 0:6, 0:CTX]))
                ln.link(v.tensor_copy(pad[:, :, 2 * PADG + CTX:2 * PADG + T], raw[:, 0:6, CTX:T]))
                for n in range(6):
                    conv(v, ln, acc[:, :], pad[:, n, :], lambda k: taps[:, n, k:k + 1], CONV_G, None, PADG)
                    ln.link(v.tensor_copy(f[:, n, 0:CTX], acc[:, 0:CTX]))
                    ln.link(v.tensor_copy(f[:, n, CTX:T], acc[:, CTX + PADG:CTX + PADG + SEQ]))
                    ln.tell(q["conv_ready"])
                v.wait_ge(q["given"], 1)
                ln.link(v.scalar_tensor_tensor(sp0[:, :, :], sp0[:, :, :], 0.0, sp1[:, :, :], ALU.max, ALU.add))
                ln.link(v.scalar_tensor_tensor(gd[:, :, :], sp0[:, :, :], -1.0,
                                               rowv[:, 0, :].unsqueeze(1).broadcast_to([P, TT, 8]), ALU.mult, ALU.mult))
                v.wait_ge(q["sig_ready"], 7)
                ln.link(v.tensor_tensor(zs[:, :, :], raw[:, 6:8, :], sig[:, 6:8, :], ALU.mult))
                ln.link(v.tensor_tensor(f[:, :, :], f[:, :, :], sig[:, 0:6, :], ALU.mult))
        normalize(nc, g, f"gdn{l}", f[:, 0:4, :], BLK, 1.0)
        with Stage(nc, f"gdf{l}", "ready stored") as s:
            q = s.sem

            @s.body.vector
            def _(v):
                ln = s.line(v, "dve")
                ln.link(v.tensor_scalar(f[:, 0:WT, :], f[:, 0:WT, :], HD ** -0.5, None, ALU.mult))
                ln.tell(q["ready"])

            @s.body.sync
            def _(sp):
                sp.wait_ge(q["ready"], 1)
                sp.dma_start(g.gd_feat.rearrange("n p t -> p n t"), f[:, :, :]).then_inc(q["stored"], 16)
                sp.wait_ge(q["stored"], 16)


def gdn_end(nc, g, l, y, zs):
    with Stage(nc, f"gds{l}") as s:
        @s.body.vector
        def _(v):
            ln = s.line(v, "dve")
            ln.link(v.tensor_tensor(y[:, 0:WT, :], y[:, 0:WT, :], y[:, WT:2 * WT, :], ALU.add))
    normalize(nc, g, f"gdy{l}", y[:, 0:WT, :], BLK, 1.0 / HD)
    with ExitStack() as mem, Stage(nc, f"gdo{l}", "vec_in") as s:
        ng = mem.enter_context(sbuf(nc, "gd_ng", [P, 1]))

        @s.body.sync
        def _(sp):
            with nc.allow_non_contiguous_dma(reason="a vector onto partitions"):
                for hf in range(2):
                    sp.dma_start(ng[hf * HD:(hf + 1) * HD, :], g.gdn_norm_g[l].rearrange("(p a) -> p a", a=1)).then_inc(s.sem["vec_in"], 16)

        @s.body.vector
        def _(v):
            ln = s.line(v, "dve")
            v.wait_ge(s.sem["vec_in"], 32)
            for n in range(WT):
                ln.link(v.scalar_tensor_tensor(g.oT[:, 1, n, :], y[:, n, :], ng[:, 0:1], zs[:, n, :], ALU.mult, ALU.mult))


def mixers(nc, g, l):
    with ExitStack() as mem:
        def keep(name, shape):
            return mem.enter_context(sbuf(nc, name, shape))

        vec = keep("rk_vec", [P, 5, WT])
        zs = keep("gd_z", [P, WT, T])
        gd = keep("gd_g", [P, TT, 8])
        beta = keep("gd_beta", [P, TT, 8])
        rwkv_front(nc, g, l, vec)
        gdn_front(nc, g, l, zs, gd, beta)
        y_rk, y_gd = (g.oT[:, 2 * n:2 * n + 2, :, :].rearrange("p b n t -> p (b n) t") for n in range(2))
        recurrence(nc, g, f"rec{l}", y_rk, y_gd, gd, beta)
        rwkv_end(nc, g, l, y_rk, vec)
        gdn_end(nc, g, l, y_gd, zs)


def recurrence(nc, g, name, y_rk, y_gd, gd, beta):
    ROUNDS = TT
    RK, GD = "rk", "gd"
    KINDS = (RK, GD)
    both_kinds = ("feat_in feat_free front_ready exp_ready turned moved lt_full lt_ready mo_full mats_done levels t_full "
                  "t_moved p_full x_ready rhs_full rhs_moved u_full u_moved o_full o_moved s_full s_ready act_end dve_end").split()
    sems = [f"{k}_{n}" for k in KINDS for n in both_kinds]
    sems += "rk_v_ready rk_ops_ready rk_ak_full rk_ak_read rk_mv_full gd_gb_ready gd_tok_ready gd_rows_ready gd_diff_ready gd_gamma_ready".split()
    with ExitStack() as mem, Stage(nc, name, " ".join(sems)) as s:
        q = s.sem

        def sb(n, shape):
            return mem.enter_context(sbuf(nc, n, shape))

        def each(n, shape):
            return {k: sb(f"{k}_{n}", shape) for k in KINDS}

        NF = {RK: 10, GD: 6}
        ft = {k: sb(f"{k}_ft", [P, 2, NF[k], P]) for k in KINDS}
        kkt, rt = each("kkt", [P, 4, P]), each("rt", [P, 4, P])
        vt, kt = each("vt", [P, 2, W]), each("kt", [P, 2, W])
        lt, x, xt, tt, mo = (each(n, [P, 8, C]) for n in ("lt", "x", "xt", "tt", "mo"))
        lk = each("lk", [P, LEVELS, 8, C])
        st = each("st", [P, 2, 4, HD])
        dec = each("dec", [P, 2, 4])
        rs, us = each("rs", [P, W]), each("us", [P, W])
        lw = sb("lw", [P, 2, W])
        e_in, e_ex, e_ng = (sb(n, [P, 2, 2, P]) for n in ("e_in", "e_ex", "e_ng"))
        kht, bht = sb("kht", [P, 4, P]), sb("bht", [P, 4, P])
        bt = sb("bt", [P, 2, W])
        ak, mv = sb("ak", [P, 8, C]), sb("mv", [P, 8, C])
        gs, be = sb("gs", [P, 2, 4]), sb("be", [P, 2, 4])
        gb = sb("gb", [P, 8, C])
        eg, gcs = sb("eg", [P, 32]), sb("gcs", [P, 8])
        kb, kbe, qe = (sb(n, [P, 8, HD]) for n in ("kb", "kbe", "qe"))
        kbt = sb("kbt", [P, 4, P])
        gam, gam_s = sb("gam", [P, 8, C]), sb("gam_s", [P, 8, C])
        BANKS = {k: [mem.enter_context(psum(nc, f"{k}_b{i}", [P, 512])) for i in range(4)] for k in KINDS}
        Y = {RK: y_rk, GD: y_gd}

        def half(bank):
            return bank[:, 0:4 * C].rearrange("p (z t) -> p z t", z=4)

        def whole(bank):
            return bank[:, :].rearrange("p (z t) -> p z t", z=8)

        def both(col, stride):
            return g.c(col, 2 * stride).rearrange("p (d s) -> p d s", d=2)[:, :, 0:C].unsqueeze(2).broadcast_to([P, 2, 2, C])

        def quad(a):
            return a.rearrange("p (d w) t -> p d w t", d=2)

        INCL, STRICT, MINUS = both(CINCL, C), both(CSTRICT, C), both(CMINUS, C)
        EYE = g.c(CEYE, C)
        EYES = EYE.unsqueeze(1).broadcast_to([P, 8, C])

        def z_of(d, h):
            pair = d * 2 + h // 2
            return h % 2 * 4 + pair, slice(h % 2 * HD, (h % 2 + 1) * HD), pair

        ZS = [(d, h) for h in range(H) for d in range(2)]
        CH = [slice(c * C, (c + 1) * C) for c in range(2)]

        def chunk(d, r):
            return CH[r if d == 0 else 1 - r]

        def tiles(i):
            return i, (7 - i) % TT

        loads = {RK: 8 * 16, GD: 2 * 16}

        @s.body.sync
        def _(sp):
            ln = s.line(sp, "sp")
            with sp.Fori(0, ROUNDS) as i:
                for k in KINDS:
                    ln.hold(q[f"{k}_feat_free"], i + 1)
                    f = (g.rk_feat if k == RK else g.gd_feat).rearrange("n p t -> p n t")
                    for d, t in enumerate(tiles(i)):
                        at, landed = bass.ds(t * P, P), q[f"{k}_feat_in"]
                        sp.dma_start(ft[k][:, d, 0:6, :], f[:, 0:6, at]).then_inc(landed, 16)
                        if k == RK:
                            sp.dma_start(ft[k][:, d, 6:8, :], f[:, 6 + 2 * d:8 + 2 * d, at]).then_inc(landed, 16)
                            sp.dma_start(ft[k][:, d, 8:10, :], f[:, 10 + 2 * d:12 + 2 * d, at]).then_inc(landed, 16)
                            sp.dma_start(lw[:, d, :], g.rk_logw[at, d * W:(d + 1) * W]).then_inc(landed, 16)

        @s.body.tensor
        def _(pe):
            ln = s.line(pe, "pe")

            def turn(bank, src):
                for n in range(4):
                    last = pe.transpose(bank[:, n * P:(n + 1) * P], src(n), g.c(IDENT))
                return last

            def grams(banks, lhs, rhs):
                for d, h in ZS:
                    _, part, pair = z_of(d, h)
                    for ch in CH:
                        last = pe.matmul(half(banks[h % 2])[ch, pair, :], lhs(part, d, h, pair, ch), rhs(part, d, h, pair, ch), start=True, stop=True)
                return last

            def squares(bank, lhs, rhs):
                for d, h in ZS:
                    z, _, _ = z_of(d, h)
                    for ch in CH:
                        last = pe.matmul(whole(bank)[ch, z, :], lhs[ch, z, :], rhs(z, ch), start=True, stop=True)
                return last

            with pe.Fori(0, ROUNDS) as i:
                for k in KINDS:
                    B, f = BANKS[k], ft[k]
                    ln.hold(q[f"{k}_act_end"], i + 1)
                    ln.hold(q[f"{k}_dve_end"], i + 1)
                    ln.hold(q[f"{k}_feat_in"], i * loads[k] + loads[k])
                    if k == RK:
                        turn(B[2], lambda n: f[:, n // 2, 2 + n % 2, :])
                        for d in range(2):
                            for hp in range(2):
                                last = pe.matmul(B[d][:, hp * 2 * P:(hp + 1) * 2 * P], lw[:, d, hp * P:(hp + 1) * P],
                                                 g.c(MASKS + d * 2 * P, 2 * P), start=True, stop=True)
                    else:
                        for n, at in enumerate((0, 2, 4)):
                            turn(B[n], lambda m: f[:, m // 2, at + m % 2, :])
                        ln.hold(q["gd_gb_ready"], i + 1)
                        for d in range(2):
                            pe.matmul(B[3][:, d * 4:d * 4 + 4], g.c(MASKS + d * 2 * P), gs[:, d, :], start=True, stop=True)
                            pe.matmul(B[3][:, 8 + d * 4:12 + d * 4], g.c(MASKS + (1 - d) * 2 * P + P), gs[:, d, :], start=True, stop=True)
                        for c in range(2):
                            last = pe.matmul(B[3][:, 16 + 8 * c:24 + 8 * c], g.c(CHUNK + c * P), gs[:, :, :].rearrange("p d h -> p (d h)"),
                                             start=True, stop=True)
                    last.then_inc(q[f"{k}_front_ready"], 1)
                B = BANKS[RK]
                ln.hold(q["rk_v_ready"], i + 1)
                ln.hold(q["rk_ops_ready"], i + 1)
                grams(B[0:2], lambda p, d, h, w, ch: bht[p, w, ch], lambda p, d, h, w, ch: kkt[RK][p, w, ch]).then_inc(q["rk_lt_full"], 1)
                turn(B[3], lambda n: kht[:, n, :])
                turn(B[2], lambda n: bht[:, n, :]).then_inc(q["rk_turned"], 1)
                B = BANKS[GD]
                ln.hold(q["gd_tok_ready"], i + 1)
                for n, src in enumerate((kb, kbe, qe)):
                    last = turn(B[n], lambda m: src[:, 2 * m:2 * m + 2, :].rearrange("p h e -> p (h e)"))
                last.then_inc(q["gd_turned"], 1)
                for d, h in ZS:
                    z, _, _ = z_of(d, h)
                    for ch in CH:
                        last = pe.matmul(whole(B[3])[ch, z, :], gb[ch, d * H + h, :], g.c(CINCL + d * C, C)[ch, :], start=True, stop=True)
                last.then_inc(q["gd_rows_ready"], 1)
                B = BANKS[RK]
                ln.hold(q["rk_moved"], i + 1)
                grams(B[2:4], lambda p, d, h, w, ch: kht[p, w, ch], lambda p, d, h, w, ch: kkt[RK][p, w, ch]).then_inc(q["rk_ak_full"], 1)
                ln.hold(q["rk_lt_ready"], i + 1)
                grams(B[0:2], lambda p, d, h, w, ch: kht[p, w, ch], lambda p, d, h, w, ch: rt[RK][p, w, ch]).then_inc(q["rk_mv_full"], 1)
                B, f = BANKS[GD], ft[GD]
                ln.hold(q["gd_moved"], i + 1)
                grams(B[0:2], lambda p, d, h, w, ch: f[p, d, 2 + h // 2, ch], lambda p, d, h, w, ch: kbt[p, w, ch]).then_inc(q["gd_lt_full"], 1)
                ln.hold(q["rk_ak_read"], i + 1)
                grams(BANKS[RK][2:4], lambda p, d, h, w, ch: bht[p, w, ch], lambda p, d, h, w, ch: rt[RK][p, w, ch]).then_inc(q["rk_mo_full"], 1)
                ln.hold(q["gd_diff_ready"], i + 1)
                grams(B[2:4], lambda p, d, h, w, ch: f[p, d, 2 + h // 2, ch], lambda p, d, h, w, ch: f[p, d, h // 2, ch]).then_inc(q["gd_mo_full"], 1)
                for n in range(LEVELS):
                    for k in KINDS:
                        if n == 0:
                            ln.hold(q[f"{k}_mats_done"], i + 1)
                        else:
                            ln.hold(q[f"{k}_x_ready"], i * LEVELS + n)
                        ln.hold(q[f"{k}_levels"], i * LEVELS + n + 1)
                        squares(BANKS[k][0], lk[k][:, n, :, :], (lambda z, ch: EYE[ch, :]) if n == 0 else
                                (lambda z, ch: x[k][ch, z, :])).then_inc(q[f"{k}_t_full"], 1)
                    for k in KINDS if n else ():
                        ln.hold(q[f"{k}_t_moved"], i * (LEVELS - 1) + n)
                        if n < LEVELS - 1:
                            squares(BANKS[k][1], xt[k], lambda z, ch: tt[k][ch, z, :])
                        squares(BANKS[k][2], tt[k], lambda z, ch: xt[k][ch, z, :]).then_inc(q[f"{k}_p_full"], 1)
                for r in range(2):
                    for k in KINDS:
                        B = BANKS[k]
                        if r == 0:
                            ln.hold(q[f"{k}_x_ready"], i * LEVELS + LEVELS)
                        ln.hold(q[f"{k}_s_ready"], i * 2 + r + 1)
                        for d, h in ZS:
                            z, part, pair = z_of(d, h)
                            ch, hv = chunk(d, r), slice(h * HD, (h + 1) * HD)
                            pe.matmul(B[0][ch, hv], kkt[k][:, pair, ch], st[k][:, h % 2, pair, :], start=True, stop=False)
                            last = pe.matmul(B[0][ch, hv], ak[ch, z, :] if k == RK else EYE[ch, :], vt[k][ch, d, hv], start=False, stop=True)
                        last.then_inc(q[f"{k}_rhs_full"], 1)
                    for k in KINDS:
                        ln.hold(q[f"{k}_rhs_moved"], i * 2 + r + 1)
                        for d, h in ZS:
                            z, _, _ = z_of(d, h)
                            ch, hv = chunk(d, r), slice(h * HD, (h + 1) * HD)
                            last = pe.matmul(BANKS[k][1][ch, hv], xt[k][ch, z, :], rs[k][ch, hv], start=True, stop=True)
                        last.then_inc(q[f"{k}_u_full"], 1)
                    for k in KINDS:
                        B = BANKS[k]
                        ln.hold(q[f"{k}_u_moved"], i * 2 + r + 1)
                        for d, h in ZS:
                            _, part, pair = z_of(d, h)
                            ch, hv = chunk(d, r), slice(h * HD, (h + 1) * HD)
                            o = B[d][part, h // 2 * HD:(h // 2 + 1) * HD]
                            if k == RK:
                                pe.matmul(o, kt[k][ch, d, hv], vt[k][ch, d, hv], start=True, stop=False)
                            last = pe.matmul(o, (bt if k == RK else kt[k])[ch, d, hv], us[k][ch, hv], start=k != RK, stop=True)
                        last.then_inc(q[f"{k}_s_full"], 1)
                        ln.hold(q[f"{k}_o_moved"], i * 2 + r + 1)
                        for d, h in ZS:
                            z, part, pair = z_of(d, h)
                            ch, hv = chunk(d, r), slice(h * HD, (h + 1) * HD)
                            o = B[2 + d][part, h // 2 * C:(h // 2 + 1) * C]
                            pe.matmul(o, st[k][:, h % 2, pair, :], rt[k][:, pair, ch], start=True, stop=False)
                            if k == RK:
                                pe.matmul(o, vt[k][ch, d, hv], mv[ch, z, :], start=False, stop=False)
                            last = pe.matmul(o, us[k][ch, hv], mo[k][ch, z, :], start=False, stop=True)
                        last.then_inc(q[f"{k}_o_full"], 1)

        @s.body.scalar
        def _(act):
            ln = s.line(act, "act")
            for k in KINDS:
                ln.credit(q[f"{k}_act_end"], q[f"{k}_o_moved"])
            with act.Fori(0, ROUNDS) as i:
                for k in KINDS:
                    ln.hold(q[f"{k}_act_end"], i + 1)
                    ln.hold(q[f"{k}_dve_end"], i + 1)
                B = BANKS[RK]
                ln.hold(q["rk_front_ready"], i + 1)
                for d in range(2):
                    c = B[d][:, :].rearrange("p (h e t) -> p h e t", h=2, e=2)
                    ln.link(act.activation(e_in[:, d, :, :], c[:, :, 0, :], ACT.Exp, scale=-DECAY))
                    ln.link(act.activation(e_ng[:, d, :, :], c[:, :, 0, :], ACT.Exp, scale=DECAY))
                    ln.link(act.activation(e_ex[:, d, :, :], c[:, :, 1, :], ACT.Exp, scale=-DECAY))
                ln.tell(q["rk_exp_ready"])
                ln.hold(q["gd_front_ready"], i + 1)
                ln.link(act.activation(eg[:, :], BANKS[GD][3][:, 0:32], ACT.Exp))
                ln.tell(q["gd_exp_ready"])
                ln.link(act.activation(vt[RK][:, :, :], B[2][:, :].rearrange("p (d v) -> p d v", d=2), ACT.Copy))
                ln.tell(q["rk_v_ready"])
                ln.hold(q["rk_turned"], i + 1)
                ln.link(act.activation(kt[RK][:, :, :], B[3][:, :].rearrange("p (d v) -> p d v", d=2), ACT.Copy))
                ln.link(act.activation(bt[:, :, :], B[2][:, :].rearrange("p (d v) -> p d v", d=2), ACT.Copy, scale=-1.0))
                ln.tell(q["rk_moved"])
                ln.hold(q["gd_turned"], i + 1)
                for bank, dst in zip(BANKS[GD], (kbt, kkt[GD], rt[GD])):
                    ln.link(act.activation(dst[:, :, :], bank[:, :].rearrange("p (w t) -> p w t", w=4), ACT.Copy))
                ln.tell(q["gd_moved"])
                ln.hold(q["gd_diff_ready"], i + 1)
                ln.link(act.activation(gam[:, :, :], gam[:, :, :], ACT.Exp))
                ln.tell(q["gd_gamma_ready"])
                for n in range(1, LEVELS):
                    for k in KINDS:
                        ln.hold(q[f"{k}_t_full"], i * LEVELS + n + 1)
                        ln.link(act.activation(tt[k][:, :, :], whole(BANKS[k][0]), ACT.Copy))
                        ln.tell(q[f"{k}_t_moved"])
                for r in range(2):
                    for k in KINDS:
                        ln.hold(q[f"{k}_rhs_full"], i * 2 + r + 1)
                        ln.link(act.activation(rs[k][:, :], BANKS[k][0][:, 0:W], ACT.Copy))
                        ln.tell(q[f"{k}_rhs_moved"])
                    for k in KINDS:
                        ln.hold(q[f"{k}_o_full"], i * 2 + r + 1)
                        for d, t in enumerate(tiles(i)):
                            c = r if d == 0 else 1 - r
                            ln.link(act.activation(Y[k][:, d * 2:d * 2 + 2, bass.ds(t * P + c * C, C)],
                                                   BANKS[k][2 + d][:, 0:2 * C].rearrange("p (h t) -> p h t", h=2), ACT.Copy))
                        ln.tell(q[f"{k}_o_moved"])
                for k in KINDS:
                    ln.tell(q[f"{k}_act_end"])
                ln.restart()

        @s.body.gpsimd
        def _(pool):
            ln = s.line(pool, "pool")
            with pool.Fori(0, ROUNDS) as i:
                for k in KINDS:
                    ln.hold(q[f"{k}_act_end"], i + 1)
                    ln.hold(q[f"{k}_dve_end"], i + 1)
                    ln.hold(q[f"{k}_lt_ready"], i + 1)
                    for n in range(LEVELS):
                        for e in range(2):
                            cut = slice(e * 4, e * 4 + 4)
                            ln.link(pool.tensor_tensor(quad(lk[k][:, n, cut, :]), quad(lt[k][:, cut, :]), both(CLEVEL + 2 * n * C, C), ALU.mult))
                        ln.tell(q[f"{k}_levels"])
                ln.restart()

        @s.body.vector
        def _(v):
            ln = s.line(v, "dve")
            for k in KINDS:
                ln.link(v.memset(st[k][:, :, :, :], 0.0))
                ln.credit(q[f"{k}_dve_end"], q[f"{k}_feat_free"], q[f"{k}_s_ready"])
            ln.restart()
            halves = [slice(e * 4, e * 4 + 4) for e in range(2)]

            def masked(out, banks, m):
                for cut, bank in zip(halves, banks):
                    ln.link(v.tensor_tensor(quad(out[:, cut, :]), quad(half(bank)), m, ALU.mult))

            with v.Fori(0, ROUNDS) as i:
                for k in KINDS:
                    ln.hold(q[f"{k}_act_end"], i + 1)
                    ln.hold(q[f"{k}_dve_end"], i + 1)
                for d, t in enumerate(tiles(i)):
                    ln.link(v.tensor_copy(gs[:, d, :].unsqueeze(1), gd[:, bass.ds(t, 1), d * H:(d + 1) * H]))
                    ln.link(v.tensor_copy(be[:, d, :].unsqueeze(1), beta[:, bass.ds(t, 1), d * H:(d + 1) * H]))
                ln.link(v.tensor_copy(gb[:, :, :], gs[:, :, :].rearrange("p d h -> p (d h)").unsqueeze(2).broadcast_to([P, 8, C])))
                ln.tell(q["gd_gb_ready"])

                ln.hold(q["rk_feat_in"], i * loads[RK] + loads[RK])
                ln.hold(q["rk_exp_ready"], i + 1)
                for d in range(2):
                    cut = slice(2 * d, 2 * d + 2)
                    for o, e, at in ((bht, e_ng, 8), (kkt[RK], e_ex, 4), (kht, e_ng, 6), (rt[RK], e_in, 0)):
                        ln.link(v.tensor_tensor(o[:, cut, :], e[:, d, :, :], ft[RK][:, d, at:at + 2, :], ALU.mult))
                ln.tell(q["rk_ops_ready"])
                ln.tell(q["rk_feat_free"])
                for d in range(2):
                    for c in range(2):
                        end = c * C + (C - 1 if d == 0 else 0)
                        ln.link(v.tensor_copy(dec[RK][:, c, 2 * d:2 * d + 2], e_in[:, d, :, end]))

                ln.hold(q["gd_exp_ready"], i + 1)
                B = BANKS[GD]
                ln.link(v.tensor_copy(gcs[:, :], B[3][:, 0:8]))

                def heads(bank):
                    return bank[:, :].rearrange("p (z e) -> p z e", z=8)

                def wide(a):
                    return a.unsqueeze(2).broadcast_to([P, 8, HD])

                bz = wide(be[:, :, :].rearrange("p d h -> p (d h)"))
                v8, k8 = (m[:, :, :].rearrange("p d (h e) -> p (d h) e", e=HD) for m in (vt[GD], kt[GD]))
                ln.link(v.tensor_tensor(kb[:, :, :], heads(B[1]), bz, ALU.mult))
                ln.link(v.scalar_tensor_tensor(kbe[:, :, :], kb[:, :, :], -1.0, wide(eg[:, 0:8]), ALU.mult, ALU.mult))
                ln.link(v.tensor_tensor(qe[:, :, :], heads(B[0]), wide(eg[:, 0:8]), ALU.mult))
                ln.link(v.tensor_tensor(k8, heads(B[1]), wide(eg[:, 8:16]), ALU.mult))
                ln.link(v.tensor_tensor(v8, heads(B[2]), bz, ALU.mult))
                ln.tell(q["gd_tok_ready"])
                ends = eg[:, 16:32].rearrange("p (c w h) -> p c w h", c=2, h=2)
                for hf in range(2):
                    part = slice(hf * HD, (hf + 1) * HD)
                    ln.link(v.tensor_copy(dec[GD][part, :, :], ends[part, :, :, hf]))

                ln.hold(q["rk_lt_full"], i + 1)
                masked(lt[RK], BANKS[RK][0:2], STRICT)
                ln.tell(q["rk_lt_ready"])
                ln.hold(q["gd_rows_ready"], i + 1)
                for d, h in ZS:
                    z, m = z_of(d, h)[0], d * H + h
                    ln.link(v.tensor_scalar(gam[:, z, :], whole(B[3])[:, z, :], gcs[:, m:m + 1], 0.0, ALU.subtract, ALU.min))
                ln.tell(q["gd_diff_ready"])
                ln.hold(q["rk_ak_full"], i + 1)
                masked(ak, BANKS[RK][2:4], STRICT)
                ln.tell(q["rk_ak_read"])
                ln.hold(q["gd_gamma_ready"], i + 1)
                for cut in halves:
                    ln.link(v.tensor_tensor(quad(gam_s[:, cut, :]), quad(gam[:, cut, :]), STRICT, ALU.mult))
                ln.hold(q["gd_lt_full"], i + 1)
                for cut, bank in zip(halves, B[0:2]):
                    ln.link(v.tensor_tensor(lt[GD][:, cut, :], half(bank), gam_s[:, cut, :], ALU.mult))
                ln.tell(q["gd_lt_ready"])
                ln.hold(q["rk_mv_full"], i + 1)
                masked(mv, BANKS[RK][0:2], INCL)
                ln.hold(q["rk_mo_full"], i + 1)
                masked(mo[RK], BANKS[RK][2:4], MINUS)
                ln.tell(q["rk_mats_done"])
                for cut in halves:
                    ln.link(v.tensor_tensor(quad(gam[:, cut, :]), quad(gam[:, cut, :]), INCL, ALU.mult))
                ln.hold(q["gd_mo_full"], i + 1)
                ln.tell(q["gd_feat_free"])
                for cut, bank in zip(halves, B[2:4]):
                    ln.link(v.tensor_tensor(mo[GD][:, cut, :], half(bank), gam[:, cut, :], ALU.mult))
                ln.tell(q["gd_mats_done"])

                for n in range(LEVELS):
                    for k in KINDS:
                        if n == 0:
                            ln.hold(q[f"{k}_levels"], i * LEVELS + 1)
                            ln.link(v.tensor_tensor(xt[k][:, :, :], EYES, lk[k][:, 0, :, :], ALU.subtract))
                            ln.hold(q[f"{k}_t_full"], i * LEVELS + 1)
                            ln.link(v.tensor_tensor(x[k][:, :, :], EYES, whole(BANKS[k][0]), ALU.subtract))
                        else:
                            ln.hold(q[f"{k}_p_full"], i * (LEVELS - 1) + n)
                            if n < LEVELS - 1:
                                ln.link(v.tensor_tensor(x[k][:, :, :], x[k][:, :, :], whole(BANKS[k][1]), ALU.subtract))
                            ln.link(v.tensor_tensor(xt[k][:, :, :], xt[k][:, :, :], whole(BANKS[k][2]), ALU.subtract))
                        ln.tell(q[f"{k}_x_ready"])
                for r in range(2):
                    for k in KINDS:
                        ln.hold(q[f"{k}_u_full"], i * 2 + r + 1)
                        ln.link(v.tensor_copy(us[k][:, :], BANKS[k][1][:, 0:W]))
                        ln.tell(q[f"{k}_u_moved"])
                    for k in KINDS:
                        ln.hold(q[f"{k}_o_full"], i * 2 + r + 1)
                        for d in range(2):
                            c = r if d == 0 else 1 - r
                            cut = slice(2 * d, 2 * d + 2)
                            for e in range(2):
                                part = slice(e * HD, (e + 1) * HD)
                                grown = BANKS[k][d][part, 0:2 * HD].rearrange("p (w e) -> p w e", w=2)
                                dd = dec[k][part, c, cut].unsqueeze(2).broadcast_to([HD, 2, HD])
                                sd = st[k][part, e, cut, :]
                                for by, op in ((grown, ALU.add), (dd, ALU.mult)) if k == RK else ((dd, ALU.mult), (grown, ALU.add)):
                                    ln.link(v.tensor_tensor(sd, sd, by, op))
                        ln.tell(q[f"{k}_s_ready"])
                for k in KINDS:
                    ln.tell(q[f"{k}_dve_end"])
                ln.restart()


def peer_pick(nc, g, l, t0, t1, qT, idx, gates):
    M = 2 * HEADS
    with ExitStack() as mem, Stage(nc, f"pick{l}", "keys_in k_turned k_moved q_in q_used scored copied sc_free exp_asked exp_done") as s:
        def sb(n, shape, dt=F32):
            return mem.enter_context(sbuf(nc, n, shape, dt))

        keys, keysT = sb("keys", [P, M, P]), sb("keysT", [P, M, P])
        qs, sc, wk = sb("qs", [P, M, P]), sb("sc", [P, M, NKEYS]), sb("wk", [P, NKEYS])
        top, best = sb("top", [P, M, TOPK]), sb("best", [P, HEADS, TOPK])
        at, pos, ab = sb("at", [P, M, TOPK], U32), sb("pos", [P, PICKS], U32), sb("ab", [P, PICKS], U32)
        atf, abf = sb("atf", [P, M, TOPK]), sb("abf", [P, PICKS])
        cand, eq = sb("cand", [P, HEADS, TOPK * TOPK]), sb("eq", [P, PICKS, TOPK])
        wk2, sel = sb("wk2", [P, TOPK * TOPK]), sb("sel", [P, 2, PICKS])
        ex, den = sb("ex", [P, HEADS, TOPK]), sb("den", [P, HEADS])
        B = [mem.enter_context(psum(nc, "pb", [P, 512])) for _ in range(4)]
        q = s.sem
        N = t1 - t0

        @s.body.sync
        def _(sp):
            ln = s.line(sp, "sp")
            sp.dma_start(keys[:, :, :], g.peer_keys[l].rearrange("h s k d -> k (h s) d")).then_inc(q["keys_in"], 16)
            with sp.Fori(0, N) as i:
                ln.hold(q["q_used"], i + 1)
                sp.dma_start(qs[:, :, :], qT[:, :, bass.ds(i * P + t0 * P, P)]).then_inc(q["q_in"], 16)

        @s.body.tensor
        def _(pe):
            ln = s.line(pe, "pe")
            ln.credit(q["q_used"])
            pe.wait_ge(q["keys_in"], 16)
            for n in range(4):
                for m in range(4):
                    last = pe.transpose(B[n][:, m * P:(m + 1) * P], keys[:, 4 * n + m, :], g.c(IDENT))
            last.then_inc(q["k_turned"], 1)
            pe.wait_ge(q["k_moved"], 1)
            with pe.Fori(0, N) as i:
                ln.hold(q["q_in"], i * 16 + 16)
                ln.hold(q["copied"], i + 1)
                for n in range(M):
                    last = pe.matmul(B[n // 4][:, n % 4 * P:(n % 4 + 1) * P], qs[:, n, :], keysT[:, n, :], start=True, stop=True)
                last.then_inc(q["scored"], 1)
                ln.hold(q["scored"], i + 1)
                ln.tell(q["q_used"])

        @s.body.scalar
        def _(act):
            ln = s.line(act, "act")
            ln.credit(q["copied"])
            act.wait_ge(q["k_turned"], 1)
            for n in range(4):
                ln.link(act.activation(keysT[:, 4 * n:4 * n + 4, :], B[n][:, :].rearrange("p (m k) -> p m k", m=4), ACT.Copy))
            ln.tell(q["k_moved"])
            ln.restart()
            with act.Fori(0, N) as i:
                ln.hold(q["scored"], i + 1)
                ln.hold(q["sc_free"], i + 1)
                for n in range(4):
                    ln.link(act.activation(sc[:, 4 * n:4 * n + 4, :], B[n][:, :].rearrange("p (m k) -> p m k", m=4), ACT.Copy))
                ln.tell(q["copied"])
                ln.hold(q["exp_asked"], i + 1)
                ln.link(act.activation(ex[:, :, :], ex[:, :, :], ACT.Exp))
                ln.tell(q["exp_done"])
                ln.restart()

        @s.body.vector
        def _(v):
            ln = s.line(v, "dve")
            ln.credit(q["sc_free"])

            def top16(values, work, out, where):
                ln.link(v.max(out[:, 0:8], values))
                ln.link(v.max_index(where[:, 0:8], out[:, 0:8], values))
                ln.link(v.match_replace(work, out[:, 0:8], values, NEG))
                ln.link(v.max(out[:, 8:16], work))
                ln.link(v.max_index(where[:, 8:16], out[:, 8:16], work))

            with v.Fori(0, N) as i:
                tile = bass.ds(i + t0, 1)
                ln.hold(q["copied"], i + 2)
                for m in range(M):
                    top16(sc[:, m, :], wk[:, :], top[:, m, :], at[:, m, :])
                ln.tell(q["sc_free"])
                ln.link(v.tensor_copy(atf[:, :, :], at[:, :, :]))
                tv = top[:, :, :].rearrange("p (h s) k -> p h s k", s=2)
                fv = atf[:, :, :].rearrange("p (h s) k -> p h s k", s=2)
                ln.link(v.tensor_tensor(cand[:, :, :].rearrange("p h (a b) -> p h a b", a=TOPK),
                                        tv[:, :, 0, :].unsqueeze(3).broadcast_to([P, HEADS, TOPK, TOPK]),
                                        tv[:, :, 1, :].unsqueeze(2).broadcast_to([P, HEADS, TOPK, TOPK]), ALU.add))
                for h in range(HEADS):
                    top16(cand[:, h, :], wk2[:, :], best[:, h, :], pos[:, h * TOPK:(h + 1) * TOPK])
                ln.link(v.tensor_tensor(ex[:, :, :], best[:, :, :], best[:, :, 0:1].broadcast_to([P, HEADS, TOPK]), ALU.subtract))
                ln.tell(q["exp_asked"])
                iota = g.c(IOTA, TOPK).unsqueeze(1).broadcast_to([P, PICKS, TOPK])
                for n, (op, by) in enumerate(((ALU.logical_shift_right, 4), (ALU.bitwise_and, TOPK - 1))):
                    ln.link(v.tensor_scalar(ab[:, :], pos[:, :], by, None, op))
                    ln.link(v.tensor_copy(abf[:, :], ab[:, :]))
                    ln.link(v.tensor_tensor(eq[:, :, :], abf[:, :].unsqueeze(2).broadcast_to([P, PICKS, TOPK]), iota, ALU.is_equal))
                    e4 = eq[:, :, :].rearrange("p (h k) a -> p h k a", h=HEADS)
                    ln.link(v.tensor_tensor(e4, e4, fv[:, :, n, :].unsqueeze(2).broadcast_to([P, HEADS, TOPK, TOPK]), ALU.mult))
                    ln.link(v.tensor_reduce(sel[:, n, :], eq[:, :, :], AX_X, ALU.add))
                ln.link(v.tensor_scalar(sel[:, 0, :], sel[:, 0, :], float(NKEYS), float(l * EXPERTS), ALU.mult, ALU.add))
                ln.link(v.tensor_tensor(idx[:, tile, :], sel[:, 0:1, :], sel[:, 1:2, :], ALU.add))
                ln.hold(q["exp_done"], i + 1)
                ln.link(v.tensor_reduce(den[:, :], ex[:, :, :], AX_X, ALU.add))
                ln.link(v.reciprocal(den[:, :], den[:, :]))
                ln.link(v.tensor_tensor(gates[:, tile, :].rearrange("p a (h k) -> p (a h) k", h=HEADS), ex[:, :, :],
                                        den[:, :].unsqueeze(2).broadcast_to([P, HEADS, TOPK]), ALU.mult))
                ln.restart()


def peer_apply(nc, g, l, t0, t1, cond, idx, gates):
    HALF = RING // 2
    ROUNDS = PICKS // RING
    before = g.rows_landed * 16
    g.rows_landed += (t1 - t0) * 2 * ROUNDS
    with ExitStack() as mem, Stage(nc, f"apply{l}_{t0}", "rows_used h_in h_used h_turned h_moved dots_done gelu_done f_ready f_turned f_moved") as s:
        def sb(n, shape, dt=F32):
            return mem.enter_context(sbuf(nc, n, shape, dt))

        hs, ht, junk, acc = sb("hs", [P, KD, P]), sb("ht", [P, D]), sb("junk", [P, D]), sb("acc", [P, D])
        ring = sb("ring", [P, RING, D])
        idxc = sb("idxc", [P, RING], U32)
        dots, dot16, coef, coef16 = sb("dots", [P, PICKS]), sb("dot16", [P, RING]), sb("coef", [P, PICKS]), sb("coef16", [P, RING])
        B = [mem.enter_context(psum(nc, "ab", [P, 512])) for _ in range(4)]
        q = s.sem
        N = t1 - t0

        @s.body.sync
        def _(sp):
            ln = s.line(sp, "sp")
            with sp.Fori(0, N) as i:
                ln.hold(q["h_used"], i + 1)
                sp.dma_start(hs[:, :, :], g.hT[:, :, bass.ds(i * P + t0 * P, P)]).then_inc(q["h_in"], 16)

        @s.body.gpsimd
        def _(pool):
            ln = s.line(pool, "pool")
            tables = [a.rearrange("l e d -> (l e) d") for a in (g.peer_u, g.peer_v)]
            with pool.Fori(0, N) as i:
                for n, table in enumerate(tables):
                    with pool.Fori(0, ROUNDS) as r:
                        for hf in range(2):
                            ln.hold(q["rows_used"], (i * (2 * ROUNDS) + r + n * ROUNDS) * RING + (hf + 1) * HALF)
                            cut = slice(hf * HALF, (hf + 1) * HALF)
                            ln.link(pool.tensor_copy(idxc[:, cut].unsqueeze(1), idx[:, bass.ds(i + t0, 1), bass.ds(r * RING + hf * HALF, HALF)]))
                            for j in range(hf * HALF, (hf + 1) * HALF):
                                pool.indirect_dma_start(ring[:, j, :], None, table, bass.IndirectOffsetOnAxis(ap=idxc[:, j:j + 1], axis=0)).then_inc(g.row_in[j], 16)
                        ln.restart()

        @s.body.tensor
        def _(pe):
            ln = s.line(pe, "pe")
            ln.credit(q["h_used"])
            with pe.Fori(0, N) as i:
                ln.hold(q["h_in"], i * 16 + 16)
                ln.hold(q["h_moved"], i + 1)
                for k in range(KD):
                    last = pe.transpose(B[k // 4][:, k % 4 * P:(k % 4 + 1) * P], hs[:, k, :], g.c(IDENT))
                last.then_inc(q["h_turned"], 1)
                ln.hold(q["h_turned"], i + 1)
                ln.tell(q["h_used"])
                ln.hold(q["f_ready"], i + 1)
                ln.hold(q["f_moved"], i + 1)
                for k in range(KD):
                    last = pe.transpose(B[2 + k // 4][:, k % 4 * P:(k % 4 + 1) * P], acc[:, k * P:(k + 1) * P], g.c(IDENT))
                last.then_inc(q["f_turned"], 1)

        @s.body.scalar
        def _(act):
            ln = s.line(act, "act")
            with act.Fori(0, N) as i:
                ln.hold(q["dots_done"], i + 1)
                ln.link(act.activation(dots[:, :], dots[:, :], ACT.Gelu_apprx_tanh))
                ln.tell(q["gelu_done"])
                ln.restart()

        @s.body.vector
        def _(v):
            ln = s.line(v, "dve")
            ln.credit(q["h_moved"], q["f_moved"])
            ln.tell(q["rows_used"], RING)
            with v.Fori(0, N) as i:
                ln.hold(q["h_turned"], i + 1)
                for n in range(2):
                    ln.link(v.tensor_copy(ht[:, n * 512:(n + 1) * 512], B[n][:, :]))
                ln.tell(q["h_moved"])
                ln.restart()
                with v.Fori(0, ROUNDS) as r:
                    for j in range(RING):
                        ln.hold(g.row_in[j], (i * (2 * ROUNDS) + r) * 16 + before + 16)
                        ln.link(v.tensor_tensor_reduce(junk[:, :], ring[:, j, :], ht[:, :], 1.0, 0.0, ALU.mult, ALU.add, dot16[:, j:j + 1]))
                        ln.tell(q["rows_used"])
                    ln.link(v.tensor_copy(dots[:, bass.ds(r * RING, RING)], dot16[:, :]))
                    ln.restart()
                ln.tell(q["dots_done"])
                ln.hold(q["gelu_done"], i + 1)
                ln.link(v.tensor_tensor(coef[:, :].unsqueeze(1), dots[:, :].unsqueeze(1), gates[:, bass.ds(i + t0, 1), :], ALU.mult))
                ln.link(v.memset(acc[:, :], 0.0))
                ln.restart()
                with v.Fori(0, ROUNDS) as r:
                    ln.link(v.tensor_copy(coef16[:, :], coef[:, bass.ds(r * RING, RING)]))
                    for j in range(RING):
                        ln.hold(g.row_in[j], (i * (2 * ROUNDS) + r + ROUNDS) * 16 + before + 16)
                        ln.link(v.scalar_tensor_tensor(acc[:, :], ring[:, j, :], coef16[:, j:j + 1], acc[:, :], ALU.mult, ALU.add))
                        ln.tell(q["rows_used"])
                    ln.restart()
                ln.tell(q["f_ready"])
                ln.hold(q["f_turned"], i + 1)
                tok = bass.ds(i * P + t0 * P, P)
                for k in range(KD):
                    ln.link(v.scalar_tensor_tensor(g.xT[:, k, tok], B[2 + k // 4][:, k % 4 * P:(k % 4 + 1) * P],
                                                   g.mods[:, 5 * KD + k, cond:cond + 1], g.xT[:, k, tok], ALU.mult, ALU.add))
                ln.tell(q["f_moved"])
                ln.restart()


def peer(nc, g, l, segs):
    t0 = segs[0][0] // P
    with ExitStack() as mem:
        idx = mem.enter_context(sbuf(nc, "idx", [P, TT, PICKS], U32))
        gates = mem.enter_context(sbuf(nc, "gates", [P, TT, PICKS]))
        with ExitStack() as front:
            qT = front.enter_context(sbuf(nc, "qT", [P, 2 * HEADS, T]))
            project(nc, g, f"q{l}", g.peer_w_q[l], 2 * HEADS, g.hT, segs, out=qT)
            peer_pick(nc, g, l, t0, TT, qT, idx, gates)
        for a, b, cond in segs:
            peer_apply(nc, g, l, a // P, b // P, cond, idx, gates)


def store_tokens(nc, g):
    with ExitStack() as mem, Stage(nc, "store", "turned moved stored") as s:
        rows = mem.enter_context(sbuf(nc, "orows", [P, TT - CT, D], F32))
        ps = [mem.enter_context(psum(nc, f"st{i}", [P, 4 * P], F32)) for i in range(2)]
        q = s.sem
        N = (TT - CT) * 2

        @s.body.tensor
        def _(pe):
            for n in range(N):
                if n >= 2:
                    pe.wait_ge(q["moved"], n - 1)
                for j in range(4):
                    t0 = CTX + n // 2 * P
                    last = pe.transpose(ps[n % 2][:, j * P:(j + 1) * P], g.hT[:, n % 2 * 4 + j, t0:t0 + P], g.c(IDENT))
                last.then_inc(q["turned"], 1)

        @s.body.vector
        def _(v):
            for n in range(N):
                v.wait_ge(q["turned"], n + 1)
                v.tensor_copy(rows[:, n // 2, n % 2 * 512:n % 2 * 512 + 512], ps[n % 2][:, :]).then_inc(q["moved"], 1)

        @s.body.sync
        def _(sp):
            sp.wait_ge(q["moved"], N)
            sp.dma_start(g.out[0].rearrange("(t p) d -> p t d", p=P), rows[:, :, :]).then_inc(q["stored"], 16)
            sp.wait_ge(q["stored"], 16)


def program(nc, args, consts, out):
    with ExitStack() as mem:
        def sb(name, shape, dt=F32):
            return mem.enter_context(sbuf(nc, name, shape, dt))

        g = Program()
        g.x, g.cvec, g.ctx, g.c_ctx, g.w_ada, g.b_ada = (args[n] for n in NAMES[0:6])
        g.norm1_g, g.norm2_g, g.w_in, g.rwkv_mu, g.rwkv_w0, g.rwkv_w2 = (args[n] for n in NAMES[6:12])
        g.rwkv_a0, g.rwkv_a2, g.rwkv_g2, g.rwkv_k_k, g.rwkv_k_a, g.rwkv_r_k = (args[n] for n in NAMES[12:18])
        g.rwkv_gn_g, g.rwkv_gn_b, g.gdn_conv_w, g.gdn_a_log, g.gdn_dt_bias, g.gdn_norm_g = (args[n] for n in NAMES[18:24])
        g.sgu_ln_g, g.sgu_ln_b, g.sgu_w_s, g.sgu_b_s, g.conf_dw_w, g.conf_dw_b = (args[n] for n in NAMES[24:30])
        g.conf_ln_g, g.conf_ln_b, g.w_branch, g.w_out, g.peer_w_q, g.peer_keys = (args[n] for n in NAMES[30:36])
        g.peer_u, g.peer_v, g.final_g = (args[n] for n in NAMES[36:39])
        g.out, g.consts = out, consts
        g.xT = sb("xT", [P, KD, T])
        g.hT = sb("hT", [P, KD, T])
        g.cst = sb("cst", [P, NCONST])
        g.cond = sb("cond", [P, KD, 2])
        g.cond_sig = sb("cond_sig", [P, KD, 2])
        g.mods = sb("mods", [P, 6 * KD, 2])
        g.gs = sb("gs", [P, 2, KD, 2])
        g.c = lambda col, n=P: g.cst[:, col:col + n]
        g.rk_feat = nc.dram_tensor("rk_feat", [18, P, T], F32, kind="Internal").ap()
        g.rk_logw = nc.dram_tensor("rk_logw", [T, 2 * W], F32, kind="Internal").ap()
        g.gd_feat = nc.dram_tensor("gd_feat", [6, P, T], F32, kind="Internal").ap()
        g.row_in = [mem.enter_context(nc.semaphore(f"row_in{j}")) for j in range(RING)]
        g.rows_landed = 0
        load_tokens(nc, g)
        for l in range(DEPTH):
            segs = SEG_ALL if l < DEPTH - 1 else SEG_X
            ada(nc, g, l)
            norm(nc, g, f"norm1_{l}", SEG_ALL, 0)
            with ExitStack() as mix:
                g.oT = mix.enter_context(sbuf(nc, "oT", [P, 4, WT, T]))
                mixers(nc, g, l)
                conformer(nc, g, l)
                sgu(nc, g, l)
                g.mT = mix.enter_context(sbuf(nc, "mT", [P, KD, T]))
                merge(nc, g, l, segs)
                project(nc, g, f"out{l}", g.w_out[l], KD, g.mT, segs, residual=2)
            norm(nc, g, f"norm2_{l}", segs, 1)
            peer(nc, g, l, segs)
        norm(nc, g, "final", SEG_X, 0, g.final_g)
        store_tokens(nc, g)


NAMES = ("x cvec ctx c_ctx w_ada b_ada norm1_g norm2_g w_in rwkv_mu rwkv_w0 rwkv_w2 rwkv_a0 rwkv_a2 rwkv_g2 rwkv_k_k "
         "rwkv_k_a rwkv_r_k rwkv_gn_g rwkv_gn_b gdn_conv_w gdn_a_log gdn_dt_bias gdn_norm_g sgu_ln_g sgu_ln_b sgu_w_s "
         "sgu_b_s conf_dw_w conf_dw_b conf_ln_g conf_ln_b w_branch w_out peer_w_q peer_keys peer_u peer_v final_g").split()


def kernel(**inputs):
    import concourse.bacc as bacc
    from concourse.bass_utils import run_bass_kernel_spmd as run

    nc = bacc.Bacc("TRN2", target_bir_lowering=False, num_devices=1)
    arrays, args = {}, {}
    for name in NAMES:
        a = np.ascontiguousarray(inputs["c" if name == "cvec" else name])
        arrays[f"in_{name}"] = a
        args[name] = nc.dram_tensor(f"in_{name}", a.shape, mybir.dt.from_np(a.dtype), kind="ExternalInput").ap()
    arrays["in_consts"] = constants()
    consts = nc.dram_tensor("in_consts", (P, NCONST), F32, kind="ExternalInput").ap()
    out = nc.dram_tensor("out_0", (1, SEQ, D), F32, kind="ExternalOutput").ap()
    program(nc, args, consts, out)
    return run(nc, [arrays], core_ids=[0]).results[0]["out_0"]
```

```python
from contextlib import ExitStack

import numpy as np
import concourse.bass as bass
from concourse import mybir

ALU = mybir.AluOpType
ACT = mybir.ActivationFunctionType
F32 = mybir.dt.float32
U32 = mybir.dt.uint32
AX_X = mybir.AxisListType.X

P = 128
D = 1024
KD = D // P
W = 256
WT = W // P
H = 4
HD = W // H
CTX, SEQ = 256, 512
T = CTX + SEQ
TT = T // P
CT = CTX // P
GW = 64
GR = SEQ // GW
C = 64
LEVELS = 6
EPS = 1e-6
DECAY = float(np.exp(-0.5))
DEPTH = 2

RWKV0, GDN0 = 0, 1024
AB0, SGU0, CONF0, GATE0 = 2048, 2064, 2576, 3088

HEADS = 8
NKEYS = 128
EXPERTS = NKEYS * NKEYS
TOPK = 16
PICKS = HEADS * TOPK
RING = 16
EXP_ROUND = 5
NEG = -3.0e38

CONV_G, CONV_C = 5, 31

IDENT, ONES, BLK = 0, 128, 256
MASKS = 384
CHUNK = MASKS + 4 * P
CINCL = CHUNK + 2 * P
CSTRICT = CINCL + 2 * C
CMINUS = CSTRICT + 2 * C
CEYE = CMINUS + 2 * C
CLEVEL = CEYE + C
QUAD = CLEVEL + 2 * LEVELS * C
IOTA = QUAD + 4
NCONST = IOTA + TOPK


class Program:
    pass


def constants():
    s, t = np.arange(P)[:, None], np.arange(P)[None, :]
    same = s // C == t // C
    cols = [s == t, np.ones((P, P)), s // HD == t // HD]
    for later, strictly in ((s <= t, s < t), (s >= t, s > t)):
        cols += [same & later, same & strictly]
    cols += [(s // C == c) & (t >= 0) for c in range(2)]
    u, w = s % C, np.arange(C)[None, :]
    cols += [u <= w, u >= w, u < w, u > w, -1.0 * (u <= w), -1.0 * (u >= w), u == w]
    for k in range(LEVELS):
        b = 1 << k
        near = u // (2 * b) == w // (2 * b)
        cols += [near & (u // b % 2 == 0) & (w // b % 2 == 1), near & (u // b % 2 == 1) & (w // b % 2 == 0)]
    cols += [s % 4 == np.arange(4)[None, :], np.broadcast_to(np.arange(TOPK)[None, :], (P, TOPK))]
    out = np.concatenate([np.asarray(c, np.float32) for c in cols], 1)
    assert out.shape == (P, NCONST)
    return out


def sbuf(nc, name, shape, dt=F32):
    return nc.sbuf_tensor(f"{name}_{nc.next_id()}", shape, dt)


def psum(nc, name, shape, dt=F32):
    return nc.psum_tensor(f"{name}_{nc.next_id()}", shape, dt)


class Line:

    def __init__(self, eng, chain, pace):
        self.eng, self.chain, self.pace, self.n = eng, chain, pace, 0

    def link(self, ins):
        self.n += 1
        ins.then_inc(self.chain, 1)
        self.eng.wait_ge(self.chain, self.n)

    def restart(self):
        if self.n:
            self.eng.sem_inc(self.chain, -self.n)
            self.n = 0

    def hold(self, sem, value):
        self.eng.wait_ge(sem, value)
        if not isinstance(value, int):
            self.eng.sem_inc(self.pace, 1)

    def tell(self, sem, n=1):
        self.eng.sem_inc(sem, n)

    def credit(self, *sems):
        for sem in sems:
            self.eng.sem_inc(sem, 1)


ENGINES = ("pe", "act", "dve", "pool", "sp")


class Stage:

    def __init__(self, nc, name, sems=""):
        self.nc, self.name, self.names = nc, name, sems.split()

    def __enter__(self):
        self.ctx = ExitStack()
        made = {n: self.ctx.enter_context(self.nc.semaphore(f"{self.name}_{n}"))
                for n in self.names + [f"chain_{e}" for e in ENGINES] + [f"pace_{e}" for e in ENGINES]}
        self.sem = made
        self.block = self.nc.Block()
        self.body = self.block.__enter__()
        return self

    def line(self, eng, name):
        return Line(eng, self.sem[f"chain_{name}"], self.sem[f"pace_{name}"])

    def __exit__(self, *e):
        self.block.__exit__(*e)
        if e[0] is None:
            with self.nc.Block() as clear:
                @clear.gpsimd
                def _(pool):
                    for s in self.sem.values():
                        pool.sem_clear(s)
        self.ctx.close()


SEG_ALL = ((0, CTX, 1), (CTX, T, 0))
SEG_X = ((CTX, T, 0),)


def load_tokens(nc, g):
    with ExitStack() as mem, Stage(nc, "load", "rows_in turned moved consts_in") as s:
        rows = mem.enter_context(sbuf(nc, "rows", [P, TT, D], F32))
        ps = [mem.enter_context(psum(nc, f"ld{i}", [P, 4, P], F32)) for i in range(2)]
        q = s.sem

        @s.body.sync
        def _(sp):
            sp.dma_start(g.cst[:, :], g.consts).then_inc(q["consts_in"], 16)
            sp.dma_start(rows[:, 0:CT, :], g.ctx[0].rearrange("(t p) d -> p t d", p=P)).then_inc(q["rows_in"], 16)
            sp.dma_start(rows[:, CT:TT, :], g.x[0].rearrange("(t p) d -> p t d", p=P)).then_inc(q["rows_in"], 16)

        @s.body.tensor
        def _(pe):
            pe.wait_ge(q["consts_in"], 16)
            pe.wait_ge(q["rows_in"], 32)
            for n in range(TT * 2):
                if n >= 2:
                    pe.wait_ge(q["moved"], n - 1)
                for j in range(4):
                    k = n % 2 * 4 + j
                    last = pe.transpose(ps[n % 2][:, j, :], rows[:, n // 2, k * P:(k + 1) * P], g.c(IDENT))
                last.then_inc(q["turned"], 1)

        @s.body.vector
        def _(v):
            for n in range(TT * 2):
                v.wait_ge(q["turned"], n + 1)
                v.tensor_copy(g.xT[:, n % 2 * 4:n % 2 * 4 + 4, n // 2 * P:(n // 2 + 1) * P],
                              ps[n % 2][:, :, :]).then_inc(q["moved"], 1)

    with Stage(nc, "cond", "cond_in sig_ready") as s:
        q = s.sem

        @s.body.sync
        def _(sp):
            with nc.allow_non_contiguous_dma(reason="2048 numbers, once"):
                sp.dma_start(g.cond[:, :, 0], g.cvec.rearrange("a (k p) -> p (a k)", p=P)).then_inc(q["cond_in"], 16)
                sp.dma_start(g.cond[:, :, 1], g.c_ctx.rearrange("(k p) -> p k", p=P)).then_inc(q["cond_in"], 16)

        @s.body.scalar
        def _(act):
            act.wait_ge(q["cond_in"], 32)
            act.activation(g.cond_sig[:, :, :], g.cond[:, :, :], ACT.Sigmoid).then_inc(q["sig_ready"], 1)

        @s.body.vector
        def _(v):
            v.wait_ge(q["sig_ready"], 1)
            ln = s.line(v, "dve")
            ln.link(v.tensor_tensor(g.cond[:, :, :], g.cond[:, :, :], g.cond_sig[:, :, :], ALU.mult))


def ada(nc, g, l):
    SLAB = 4 * P
    with ExitStack() as mem, Stage(nc, f"ada{l}", "w0_in w1_in w0_used w1_used full0 full1 free0 free1 moved0 moved1 "
                                   "turned0 turned1 vec_in") as s:
        wt = [mem.enter_context(sbuf(nc, f"ada_w{i}", [P, KD, SLAB], F32)) for i in range(2)]
        rows = [mem.enter_context(sbuf(nc, f"ada_r{i}", [2, SLAB], F32)) for i in range(2)]
        bias = mem.enter_context(sbuf(nc, "ada_b", [P, 6 * KD], F32))
        gain = mem.enter_context(sbuf(nc, "ada_g", [P, 2, KD], F32))
        ps = [mem.enter_context(psum(nc, f"ada_p{i}", [P, 512], F32)) for i in range(2)]
        pt = [mem.enter_context(psum(nc, f"ada_t{i}", [P, 512], F32)) for i in range(2)]
        q = s.sem
        moved, turned = [q["moved0"], q["moved1"]], [q["turned0"], q["turned1"]]
        w_in, w_used, full, free = [q["w0_in"], q["w1_in"]], [q["w0_used"], q["w1_used"]], [q["full0"], q["full1"]], [q["free0"], q["free1"]]
        rounds = 6 * D // SLAB // 2

        @s.body.sync
        def _(sp):
            ln = s.line(sp, "sp")
            with nc.allow_non_contiguous_dma(reason="vectors onto partitions"):
                sp.dma_start(bias[:, :], g.b_ada[l].rearrange("(j p) -> p j", p=P)).then_inc(q["vec_in"], 16)
                sp.dma_start(gain[:, 0, :], g.norm1_g[l].rearrange("(j p) -> p j", p=P)).then_inc(q["vec_in"], 16)
                sp.dma_start(gain[:, 1, :], g.norm2_g[l].rearrange("(j p) -> p j", p=P)).then_inc(q["vec_in"], 16)
            w = g.w_ada[l].rearrange("(k p) n -> p k n", p=P)
            with sp.Fori(0, rounds) as i:
                for j in range(2):
                    ln.hold(w_used[j], i + 1)
                    sp.dma_start(wt[j][:, :, :], w[:, :, bass.ds(i * (2 * SLAB) + j * SLAB, SLAB)]).then_inc(w_in[j], 16)

        @s.body.tensor
        def _(pe):
            ln = s.line(pe, "pe")
            ln.credit(*w_used)
            with pe.Fori(0, rounds) as i:
                for j in range(2):
                    ln.hold(w_in[j], i * 16 + 16)
                    ln.hold(free[j], i + 1)
                    for k in range(KD):
                        last = pe.matmul(ps[j][0:2, :], g.cond[:, k, :], wt[j][:, k, :], start=k == 0, stop=k == KD - 1)
                    last.then_inc(full[j], 1)
                    ln.hold(full[j], i + 1)
                    ln.tell(w_used[j])
                for j in range(2):
                    ln.hold(moved[j], i + 1)
                    for m in range(4):
                        last = pe.transpose(pt[j][:, 2 * m:2 * m + 2], rows[j][:, m * P:(m + 1) * P], g.c(IDENT)[0:2, 0:2])
                    last.then_inc(turned[j], 1)

        @s.body.vector
        def _(v):
            ln = s.line(v, "dve")
            ln.credit(*free)
            v.wait_ge(q["vec_in"], 48)
            with v.Fori(0, rounds) as i:
                for j in range(2):
                    ln.hold(full[j], i + 1)
                    ln.link(v.tensor_copy(rows[j][:, :], ps[j][0:2, :]))
                    ln.tell(moved[j])
                for j in range(2):
                    ln.hold(turned[j], i + 1)
                    at = bass.ds(i * 8 + j * 4, 4)
                    ln.link(v.tensor_tensor(g.mods[:, at, :], pt[j][:, 0:8].rearrange("p (m v) -> p m v", v=2),
                                            bias[:, at].unsqueeze(2).broadcast_to([P, 4, 2]), ALU.add))
                    ln.tell(free[j])
                ln.restart()
            for n in range(2):
                sc = g.mods[:, (3 * n + 1) * KD:(3 * n + 2) * KD, :]
                ln.link(v.tensor_scalar(g.gs[:, n, :, :], sc, 1.0, None, ALU.add))
                ln.link(v.tensor_tensor(g.gs[:, n, :, :], g.gs[:, n, :, :],
                                        gain[:, n, :].unsqueeze(2).broadcast_to([P, KD, 2]), ALU.mult))


def norm(nc, g, name, segs, which, gain=None):
    with ExitStack() as mem, Stage(nc, name, "sq_ready sq_used mean_ready rstd_ready scaled gain_in") as s:
        sq = [mem.enter_context(sbuf(nc, f"sq{i}", [P, T], F32)) for i in range(2)]
        rs = mem.enter_context(sbuf(nc, "rs", [P, T], F32))
        fg = mem.enter_context(sbuf(nc, "fg", [P, KD], F32))
        ps = [mem.enter_context(psum(nc, f"np{i}", [P, 512], F32)) for i in range(len(segs))]
        q = s.sem
        lo, hi = segs[0][0], segs[-1][1]

        @s.body.sync
        def _(sp):
            if gain is not None:
                with nc.allow_non_contiguous_dma(reason="a vector onto partitions"):
                    sp.dma_start(fg[:, :], gain.rearrange("(j p) -> p j", p=P)).then_inc(q["gain_in"], 16)

        @s.body.scalar
        def _(act):
            ln = s.line(act, "act")
            for k in range(KD):
                if k >= 2:
                    act.wait_ge(q["sq_used"], k - 1)
                ln.link(act.activation(sq[k % 2][:, lo:hi], g.xT[:, k, lo:hi], ACT.Square))
                ln.tell(q["sq_ready"])
            act.wait_ge(q["mean_ready"], 1)
            ln.link(act.activation(rs[:, lo:hi], rs[:, lo:hi], ACT.Sqrt))
            ln.tell(q["rstd_ready"])
            if gain is not None:
                act.wait_ge(q["gain_in"], 16)
            for k in range(KD):
                act.wait_ge(q["scaled"], k + 1)
                for a, b, v in segs:
                    if gain is None:
                        ln.link(act.activation(g.hT[:, k, a:b], g.hT[:, k, a:b], ACT.Identity,
                                               scale=g.gs[:, which, k, v:v + 1],
                                               bias=g.mods[:, 3 * which * KD + k, v:v + 1]))
                    else:
                        ln.link(act.activation(g.hT[:, k, a:b], g.hT[:, k, a:b], ACT.Copy, scale=fg[:, k:k + 1]))

        @s.body.tensor
        def _(pe):
            for k in range(KD):
                pe.wait_ge(q["sq_ready"], k + 1)
                for n, (a, b, v) in enumerate(segs):
                    last = pe.matmul(ps[n][:, 0:b - a], g.c(ONES), sq[k % 2][:, a:b], start=k == 0, stop=k == KD - 1)
                last.then_inc(q["sq_used"], 1)

        @s.body.vector
        def _(v):
            ln = s.line(v, "dve")
            v.wait_ge(q["sq_used"], KD)
            for n, (a, b, _) in enumerate(segs):
                ln.link(v.tensor_scalar(rs[:, a:b], ps[n][:, 0:b - a], 1.0 / D, EPS, ALU.mult, ALU.add))
            ln.link(v.reciprocal(rs[:, lo:hi], rs[:, lo:hi]))
            ln.tell(q["mean_ready"])
            v.wait_ge(q["rstd_ready"], 1)
            for k in range(KD):
                ln.link(v.tensor_tensor(g.hT[:, k, lo:hi], g.xT[:, k, lo:hi], rs[:, lo:hi], ALU.mult))
                ln.tell(q["scaled"])


def project(nc, g, name, w, tiles, rhs, segs, out=None, residual=None, spill=None, func=ACT.Copy, beside=None, sems=""):
    with ExitStack() as mem, Stage(nc, name, sems + " stored w0_in w1_in w0_used w1_used full0 full1 full2 full3 a0 a1 a2 a3 v0 v1 v2 v3") as s:
        wt = [mem.enter_context(sbuf(nc, f"w{i}", [P, KD, 2 * P], F32)) for i in range(2)]
        ps = [mem.enter_context(psum(nc, f"pp{i}", [P, 512], F32)) for i in range(8)]
        q = s.sem
        w_in, w_used = [q["w0_in"], q["w1_in"]], [q["w0_used"], q["w1_used"]]
        full, a_free, v_free = [q["full0"], q["full1"], q["full2"], q["full3"]], [q["a0"], q["a1"], q["a2"], q["a3"]], [q["v0"], q["v1"], q["v2"], q["v3"]]
        rounds = tiles // 4
        both = beside is None and len(segs) == 2 and residual is None
        lo, hi = segs[0][0], segs[-1][1]

        @s.body.sync
        def _(sp):
            ln = s.line(sp, "sp")
            wv = w.rearrange("(k p) n -> p k n", p=P)
            if beside is not None:
                beside["sync"](sp, q)
            with sp.Fori(0, rounds) as i:
                for j in range(2):
                    ln.hold(w_used[j], i + 1)
                    sp.dma_start(wt[j][:, :, :], wv[:, :, bass.ds(i * (4 * P) + j * 2 * P, 2 * P)]).then_inc(w_in[j], 16)

        @s.body.tensor
        def _(pe):
            ln = s.line(pe, "pe")
            ln.credit(*w_used)
            with pe.Fori(0, rounds) as i:
                for j in range(4):
                    if j % 2 == 0:
                        ln.hold(w_in[j // 2], i * 16 + 16)
                    if both or beside is not None:
                        ln.hold(a_free[j], i + 1)
                    if beside is None:
                        ln.hold(v_free[j], i + 1)
                    for n, (a, b, _) in enumerate(segs):
                        for k in range(KD):
                            last = pe.matmul(ps[2 * j + n][:, 0:b - a], wt[j // 2][:, k, j % 2 * P:(j % 2 + 1) * P],
                                             rhs[:, k, a:b], start=k == 0, stop=k == KD - 1)
                    last.then_inc(full[j], 1)
                    if j % 2:
                        ln.hold(full[j], i + 1)
                        ln.tell(w_used[j // 2])

        if both or spill is not None:
            @s.body.scalar
            def _(act):
                ln = s.line(act, "act")
                if both:
                    ln.credit(*a_free)
                with act.Fori(0, rounds) as i:
                    for j in range(4):
                        tile = bass.ds(i * 4 + j, 1)
                        if both:
                            a, b, _ = segs[0]
                            ln.hold(full[j], i + 1)
                            ln.link(act.activation(out[:, tile, a:b], ps[2 * j][:, 0:b - a].unsqueeze(1), ACT.Copy))
                            ln.tell(a_free[j])
                        if spill is not None:
                            ln.hold(v_free[j], i + 2)
                            act.dma_start(spill.rearrange("n p t -> p n t")[:, tile, lo:hi], out[:, tile, lo:hi]).then_inc(q["stored"], 16)
                    if both:
                        ln.restart()
                if spill is not None:
                    act.wait_ge(q["stored"], tiles * 16)

        if beside is not None:
            @s.body.scalar
            def _(act):
                ln = s.line(act, "act")
                ln.credit(*a_free)
                if "scalar" in beside:
                    beside["scalar"](act, ln, q)
                    ln.restart()
                with act.Fori(0, rounds) as i:
                    for j in range(4):
                        ln.hold(full[j], i + 1)
                        for n, (a, b, _) in enumerate(segs):
                            ln.link(act.activation(out[:, bass.ds(i * 4 + j, 1), a:b], ps[2 * j + n][:, 0:b - a].unsqueeze(1), func))
                        ln.tell(a_free[j])
                    ln.restart()

        @s.body.vector
        def _(v):
            ln = s.line(v, "dve")
            if beside is not None:
                beside["vector"](v, ln, q)
                return
            ln.credit(*v_free)
            with v.Fori(0, rounds) as i:
                for j in range(4):
                    ln.hold(full[j], i + 1)
                    for n, (a, b, c) in enumerate(segs):
                        tile = bass.ds(i * 4 + j, 1)
                        if residual is not None:
                            ln.link(v.scalar_tensor_tensor(
                                g.xT[:, tile, a:b], ps[2 * j + n][:, 0:b - a].unsqueeze(1),
                                g.mods[:, bass.ds(i * 4 + j + residual * KD, 1), c:c + 1],
                                g.xT[:, tile, a:b], ALU.mult, ALU.add))
                        elif n or not both:
                            ln.link(v.tensor_copy(out[:, tile, a:b], ps[2 * j + n][:, 0:b - a].unsqueeze(1)))
                    ln.tell(v_free[j])
                ln.restart()


def normalize(nc, g, name, x, const, factor, center=False, pooled=False):
    G = x.shape[1]
    per = 2 if pooled else 1
    units = G // per
    HALF = T // 2
    with ExitStack() as mem, Stage(nc, name, "asked summed used sums_read root_asked root_done") as s:
        sq = mem.enter_context(sbuf(nc, "nsq", [P, 2, per, T]))
        rs = mem.enter_context(sbuf(nc, "nrs", [P, 2, T]))
        ps = [[mem.enter_context(psum(nc, "nps", [P, 512])) for _ in range(2)] for _ in range(2)]
        q = s.sem
        passes = 2 if center else 1

        @s.body.tensor
        def _(pe):
            n = 0
            for ps_no in range(passes):
                for u in range(units):
                    pe.wait_ge(q["asked"], n + 1)
                    if n >= 2:
                        pe.wait_ge(q["sums_read"], n - 1)
                    for half in range(2):
                        for j in range(per):
                            src = x[:, u * per + j, :] if center and ps_no == 0 else sq[:, u % 2, j, :]
                            last = pe.matmul(ps[n % 2][half][:, 0:HALF], g.c(const), src[:, half * HALF:(half + 1) * HALF],
                                             start=j == 0, stop=j == per - 1)
                    last.then_inc(q["summed"], 1)
                    n += 1

        @s.body.vector
        def _(v):
            ln = s.line(v, "dve")
            n = 0
            if center:
                ln.tell(q["asked"], units)
                for u in range(units):
                    v.wait_ge(q["summed"], n + 1)
                    for half in range(2):
                        cut = slice(half * HALF, (half + 1) * HALF)
                        for j in range(per):
                            xs = x[:, u * per + j, cut]
                            ln.link(v.scalar_tensor_tensor(xs, ps[n % 2][half][:, 0:HALF], -factor, xs, ALU.mult, ALU.add))
                    ln.tell(q["sums_read"])
                    n += 1

            def square(u):
                for j in range(per):
                    ln.link(v.tensor_tensor(sq[:, u % 2, j, :], x[:, u * per + j, :], x[:, u * per + j, :], ALU.mult))
                ln.tell(q["asked"])

            def scale(u):
                v.wait_ge(q["root_done"], u + 1)
                for j in range(per):
                    ln.link(v.tensor_tensor(x[:, u * per + j, :], x[:, u * per + j, :], rs[:, u % 2, :], ALU.mult))

            square(0)
            for u in range(units):
                v.wait_ge(q["summed"], n + 1)
                for half in range(2):
                    ln.link(v.tensor_scalar(rs[:, u % 2, half * HALF:(half + 1) * HALF], ps[n % 2][half][:, 0:HALF],
                                            factor, EPS, ALU.mult, ALU.add))
                ln.tell(q["sums_read"])
                n += 1
                ln.link(v.reciprocal(rs[:, u % 2, :], rs[:, u % 2, :]))
                ln.tell(q["root_asked"])
                if u + 1 < units:
                    square(u + 1)
                if u >= 1:
                    scale(u - 1)
            scale(units - 1)

        @s.body.scalar
        def _(act):
            ln = s.line(act, "act")
            for u in range(units):
                act.wait_ge(q["root_asked"], u + 1)
                ln.link(act.activation(rs[:, u % 2, :], rs[:, u % 2, :], ACT.Sqrt))
                ln.tell(q["root_done"])


PADC = CONV_C // 2
LONG = PADC + CTX + PADC + SEQ + PADC
X_AT = CTX + PADC


def conv(v, ln, out, padded, tap, taps, bias, pad):
    n = CTX + pad + SEQ
    order = [taps // 2] + [k for k in range(taps) if k != taps // 2]
    for k in order:
        src = padded[:, k:k + n]
        if k == taps // 2:
            if bias is None:
                ln.link(v.tensor_scalar(out[:, 0:n], src, tap(k), None, ALU.mult))
            else:
                ln.link(v.tensor_scalar(out[:, 0:n], src, tap(k), bias, ALU.mult, ALU.add))
        else:
            ln.link(v.scalar_tensor_tensor(out[:, 0:n], src, tap(k), out[:, 0:n], ALU.mult, ALU.add))


def conformer(nc, g, l, sgu_p):
    with ExitStack() as top:
        pc = top.enter_context(sbuf(nc, "conf_p", [P, 4, T]))
        y = top.enter_context(sbuf(nc, "conf_y", [P, WT, T]))
        vec = top.enter_context(sbuf(nc, "conf_v", [P, 3, WT]))
        project(nc, g, f"confp{l}", g.w_in[l][:, CONF0:CONF0 + 2 * W], 4, g.hT, SEG_ALL, out=pc)
        with ExitStack() as mem:
            pad = mem.enter_context(sbuf(nc, "conf_pad", [P, WT, LONG]))
            acc = mem.enter_context(sbuf(nc, "conf_acc", [P, WT, LONG]))
            taps = mem.enter_context(sbuf(nc, "conf_w", [P, WT, CONV_C]))

            def loads(sp, q):
                with nc.allow_non_contiguous_dma(reason="small weights onto partitions"):
                    for n, a in enumerate((g.conf_dw_b, g.conf_ln_g, g.conf_ln_b)):
                        sp.dma_start(vec[:, n, :], a[l].rearrange("(t p) -> p t", p=P)).then_inc(q["vec_in"], 16)
                    for n in range(WT):
                        sp.dma_start(taps[:, n, :], g.conf_dw_w[l][:, n * P:(n + 1) * P].rearrange("k p -> p k")).then_inc(q["vec_in"], 16)

            def gates(act, ln, q):
                ln.link(act.activation(pc[:, 2:4, :], pc[:, 2:4, :], ACT.Sigmoid))
                ln.tell(q["sig_ready"])

            def convolve(v, ln, q):
                ln.link(v.memset(pad[:, :, :], 0.0))
                v.wait_ge(q["sig_ready"], 1)
                ln.link(v.tensor_tensor(pad[:, :, PADC:PADC + CTX], pc[:, 0:2, 0:CTX], pc[:, 2:4, 0:CTX], ALU.mult))
                ln.link(v.tensor_tensor(pad[:, :, PADC + X_AT:PADC + X_AT + SEQ], pc[:, 0:2, CTX:T], pc[:, 2:4, CTX:T], ALU.mult))
                v.wait_ge(q["vec_in"], 80)
                for n in range(WT):
                    conv(v, ln, acc[:, n, :], pad[:, n, :], lambda k: taps[:, n, k:k + 1], CONV_C, vec[:, 0, n:n + 1], PADC)
                ln.link(v.tensor_copy(y[:, :, 0:CTX], acc[:, :, 0:CTX]))
                ln.link(v.tensor_copy(y[:, :, CTX:T], acc[:, :, X_AT:X_AT + SEQ]))

            project(nc, g, f"sgup{l}", g.w_in[l][:, SGU0:SGU0 + 2 * W], 4, g.hT, SEG_ALL, out=sgu_p, func=ACT.Gelu_apprx_tanh,
                    sems="vec_in sig_ready", beside={"sync": loads, "scalar": gates, "vector": convolve})
        normalize(nc, g, f"confn{l}", y[:, :, :], ONES, 1.0 / W, center=True, pooled=True)
        with ExitStack() as mem, Stage(nc, f"confo{l}", "lin_ready sig_ready") as s:
            sig = mem.enter_context(sbuf(nc, "conf_s", [P, WT, T]))
            q = s.sem

            @s.body.vector
            def _(v):
                ln = s.line(v, "dve")
                for n in range(WT):
                    ln.link(v.tensor_scalar(y[:, n, :], y[:, n, :], vec[:, 1, n:n + 1], vec[:, 2, n:n + 1], ALU.mult, ALU.add))
                    ln.tell(q["lin_ready"])
                for n in range(WT):
                    v.wait_ge(q["sig_ready"], n + 1)
                    ln.link(v.tensor_tensor(g.oT[:, 3, n, :], y[:, n, :], sig[:, n, :], ALU.mult))

            @s.body.scalar
            def _(act):
                ln = s.line(act, "act")
                for n in range(WT):
                    act.wait_ge(q["lin_ready"], n + 1)
                    ln.link(act.activation(sig[:, n, :], y[:, n, :], ACT.Sigmoid))
                    ln.tell(q["sig_ready"])


def sgu(nc, g, l, pc):
    normalize(nc, g, f"sgun{l}", pc[:, 2:4, :], ONES, 1.0 / W, center=True, pooled=True)
    with ExitStack() as mem, Stage(nc, f"sgu{l}", "w_in turned moved mixed read lin_ready") as s:
        vec = mem.enter_context(sbuf(nc, "sgu_v", [P, 2, WT]))
        ws = mem.enter_context(sbuf(nc, "sgu_w", [P, H, P]))
        wsT = mem.enter_context(sbuf(nc, "sgu_wT", [P, H, P]))
        bs = mem.enter_context(sbuf(nc, "sgu_b", [1, H * P]))
        vt = mem.enter_context(sbuf(nc, "sgu_vt", [P, TT, W]))
        ps = [mem.enter_context(psum(nc, "sgu_ps", [P, 512])) for _ in range(4)]
        q = s.sem

        @s.body.sync
        def _(sp):
            with nc.allow_non_contiguous_dma(reason="small weights onto partitions"):
                sp.dma_start(vec[:, 0, :], g.sgu_ln_g[l].rearrange("(t p) -> p t", p=P)).then_inc(q["w_in"], 16)
                sp.dma_start(vec[:, 1, :], g.sgu_ln_b[l].rearrange("(t p) -> p t", p=P)).then_inc(q["w_in"], 16)
            sp.dma_start(ws[:, :, :], g.sgu_w_s[l].rearrange("g p s -> p g s")).then_inc(q["w_in"], 16)
            sp.dma_start(bs[:, :], g.sgu_b_s[l:l + 1].rearrange("a g p -> a (g p)")).then_inc(q["w_in"], 16)

        @s.body.tensor
        def _(pe):
            pe.wait_ge(q["w_in"], 64)
            for h in range(H):
                last = pe.transpose(ps[0][:, h * P:(h + 1) * P], ws[:, h, :], g.c(IDENT))
            last.then_inc(q["turned"], 1)
            pe.wait_ge(q["lin_ready"], WT)
            for t in range(TT):
                if t >= 1:
                    pe.wait_ge(q["moved"], t)
                for n in range(WT):
                    last = pe.transpose(ps[(t + 1) % 2][:, n * P:(n + 1) * P], pc[:, 2 + n, t * P:(t + 1) * P], g.c(IDENT))
                last.then_inc(q["turned"], 1)
            pe.wait_ge(q["moved"], TT + 1)
            for t in range(TT):
                if t >= 2:
                    pe.wait_ge(q["read"], t - 1)
                for h in range(H):
                    o = ps[2 + t % 2][h % 2 * HD:(h % 2 + 1) * HD, h // 2 * P:(h // 2 + 1) * P]
                    pe.matmul(o, vt[:, t, h * HD:(h + 1) * HD], wsT[:, h, :], start=True, stop=False)
                    last = pe.matmul(o, g.c(ONES)[0:1, 0:HD], bs[0:1, h * P:(h + 1) * P], start=False, stop=True)
                last.then_inc(q["mixed"], 1)

        @s.body.vector
        def _(v):
            ln = s.line(v, "dve")
            v.wait_ge(q["w_in"], 64)
            for n in range(WT):
                ln.link(v.tensor_scalar(pc[:, 2 + n, :], pc[:, 2 + n, :], vec[:, 0, n:n + 1], vec[:, 1, n:n + 1], ALU.mult, ALU.add))
                ln.tell(q["lin_ready"])
            v.wait_ge(q["turned"], 1)
            ln.link(v.tensor_copy(wsT[:, :, :], ps[0][:, :].rearrange("p (h s) -> p h s", h=H)))
            ln.tell(q["moved"])
            for t in range(TT):
                v.wait_ge(q["turned"], t + 2)
                ln.link(v.tensor_copy(vt[:, t, :], ps[(t + 1) % 2][:, 0:W]))
                ln.tell(q["moved"])
            for t in range(TT):
                v.wait_ge(q["mixed"], t + 1)
                ln.link(v.tensor_tensor(g.oT[:, 2, :, t * P:(t + 1) * P], pc[:, 0:2, t * P:(t + 1) * P],
                                        ps[2 + t % 2][:, 0:2 * P].rearrange("p (n t) -> p n t", n=2), ALU.mult))
                ln.tell(q["read"])


def merge(nc, g, l, segs):
    with ExitStack() as mem, Stage(nc, f"merge{l}", "g0_in g1_in b0_in b1_in w0_used w1_used gate0 gate1 val0 val1 sig0 sig1 free0 free1") as s:
        wg = [mem.enter_context(sbuf(nc, "wg", [P, KD, 4, P])) for _ in range(2)]
        wb = [mem.enter_context(sbuf(nc, "wb", [P, 4, WT, P])) for _ in range(2)]
        sg = [mem.enter_context(sbuf(nc, "sg", [P, T])) for _ in range(2)]
        tmp = mem.enter_context(sbuf(nc, "tmp", [P, T]))
        pg = [[mem.enter_context(psum(nc, "pg", [P, 512])) for _ in segs] for _ in range(2)]
        pv = [[mem.enter_context(psum(nc, "pv", [P, 512])) for _ in segs] for _ in range(2)]
        q = s.sem
        g_in, b_in, used = [q["g0_in"], q["g1_in"]], [q["b0_in"], q["b1_in"]], [q["w0_used"], q["w1_used"]]
        gate, val, sig, free = [q["gate0"], q["gate1"]], [q["val0"], q["val1"]], [q["sig0"], q["sig1"]], [q["free0"], q["free1"]]
        lo, hi = segs[0][0], segs[-1][1]

        @s.body.sync
        def _(sp):
            ln = s.line(sp, "sp")
            gw = g.w_in[l][:, GATE0:].rearrange("(k p) (b n) -> p k b n", p=P, b=4)
            bw = g.w_branch[l].rearrange("b (k p) n -> p b k n", p=P)
            with sp.Fori(0, KD // 2) as i:
                for j in range(2):
                    ln.hold(used[j], i + 1)
                    at = bass.ds(i * (2 * P) + j * P, P)
                    for b in range(4):
                        sp.dma_start(wg[j][:, :, b, :], gw[:, :, b, at]).then_inc(g_in[j], 16)
                        sp.dma_start(wb[j][:, b, :, :], bw[:, b, :, at]).then_inc(b_in[j], 16)

        @s.body.tensor
        def _(pe):
            ln = s.line(pe, "pe")
            ln.credit(*used)
            with pe.Fori(0, KD // 2) as i:
                for j in range(2):
                    ln.hold(g_in[j], i * 64 + 64)
                    ln.hold(b_in[j], i * 64 + 64)
                    for b in range(4):
                        u = b % 2
                        ln.hold(free[u], i * 4 + j * 2 + b // 2 + 1)
                        for n, (a, e, _) in enumerate(segs):
                            for k in range(KD):
                                last = pe.matmul(pg[u][n][:, 0:e - a], wg[j][:, k, b, :], g.hT[:, k, a:e], start=k == 0, stop=k == KD - 1)
                        last.then_inc(gate[u], 1)
                        for n, (a, e, _) in enumerate(segs):
                            for k in range(WT):
                                last = pe.matmul(pv[u][n][:, 0:e - a], wb[j][:, b, k, :], g.oT[:, b, k, a:e], start=k == 0, stop=k == WT - 1)
                        last.then_inc(val[u], 1)
                    ln.hold(val[1], i * 4 + j * 2 + 2)
                    ln.tell(used[j])

        @s.body.scalar
        def _(act):
            ln = s.line(act, "act")
            with act.Fori(0, KD // 2) as i:
                for j in range(2):
                    for b in range(4):
                        u, n_done = b % 2, i * 4 + j * 2 + b // 2
                        ln.hold(gate[u], n_done + 1)
                        ln.hold(free[u], n_done + 1)
                        for n, (a, e, _) in enumerate(segs):
                            ln.link(act.activation(sg[u][:, a:e], pg[u][n][:, 0:e - a], ACT.Sigmoid))
                        ln.tell(sig[u])
                ln.restart()

        @s.body.vector
        def _(v):
            ln = s.line(v, "dve")
            ln.credit(*free)
            with v.Fori(0, KD // 2) as i:
                for j in range(2):
                    m = g.mT[:, bass.ds(i * 2 + j, 1), lo:hi]
                    for b in range(4):
                        u, n_done = b % 2, i * 4 + j * 2 + b // 2
                        ln.hold(sig[u], n_done + 1)
                        ln.hold(val[u], n_done + 1)
                        for n, (a, e, _) in enumerate(segs):
                            o = m[:, :, a - lo:e - lo] if b == 0 else tmp[:, a:e].unsqueeze(1)
                            ln.link(v.tensor_tensor(o, sg[u][:, a:e].unsqueeze(1), pv[u][n][:, 0:e - a].unsqueeze(1), ALU.mult))
                        ln.tell(free[u])
                        if b:
                            ln.link(v.tensor_tensor(m, m, tmp[:, lo:hi].unsqueeze(1), ALU.add))
                ln.restart()


def shift_tiles(v, ln, src, out, mmu, omu):
    for t in range(src.shape[1]):
        ln.link(v.tensor_scalar(out[:, t, :], src[:, t, :], omu[:, t:t + 1], None, ALU.mult))

        def add(o, i, kind):
            ln.link(v.scalar_tensor_tensor(o, i, mmu[:, t, kind:kind + 1], o, ALU.mult, ALU.add))

        add(out[:, t, 1:CTX], src[:, t, 0:CTX - 1], 0)
        add(out[:, t, 0:CTX - 1], src[:, t, 1:CTX], 1)
        og = out[:, t, CTX:T].rearrange("p (r w) -> p r w", w=GW)
        sg = src[:, t, CTX:T].rearrange("p (r w) -> p r w", w=GW)
        add(og[:, :, 1:GW], sg[:, :, 0:GW - 1], 0)
        add(og[:, :, 0:GW - 1], sg[:, :, 1:GW], 1)
        add(og[:, 1:GR, :], sg[:, 0:GR - 1, :], 2)
        add(og[:, 0:GR - 1, :], sg[:, 1:GR, :], 3)


def rwkv_front(nc, g, l, vec, gd_raw):
    HALF = T // 2
    with ExitStack() as prep:
        def tmp(name, shape):
            return prep.enter_context(sbuf(nc, name, shape))

        gate, bonus = tmp("rk_gate", [P, WT, T]), tmp("rk_bonus", [P, WT, T])
        pq = tmp("rk_q", [P, 8, T])
        with ExitStack() as first:
            raw = first.enter_context(sbuf(nc, "rk_p", [P, 8, T]))
            project(nc, g, f"rkp{l}", g.w_in[l][:, RWKV0:RWKV0 + 8 * P], 8, g.hT, SEG_ALL, out=raw)
            mu = first.enter_context(sbuf(nc, "mu", [P, 2, 8]))
            mmu = first.enter_context(sbuf(nc, "mmu", [P, 8, 4]))

            def loads(sp, q):
                with nc.allow_non_contiguous_dma(reason="vectors onto partitions"):
                    sp.dma_start(mu[:, 0, :], g.rwkv_mu[l].rearrange("(t p) -> p t", p=P)).then_inc(q["vec_in"], 16)
                    for n, a in enumerate((g.rwkv_k_k[l], g.rwkv_k_a[l], g.rwkv_r_k[l].rearrange("h n -> (h n)"),
                                           g.rwkv_gn_g[l].rearrange("h n -> (h n)"), g.rwkv_gn_b[l].rearrange("h n -> (h n)"))):
                        sp.dma_start(vec[:, n, :], a.rearrange("(t p) -> p t", p=P)).then_inc(q["vec_in"], 16)

            def shift(v, ln, q):
                v.wait_ge(q["vec_in"], 96)
                ln.link(v.tensor_scalar(mu[:, 1, :], mu[:, 0, :], -1.0, 1.0, ALU.mult, ALU.add))
                ln.link(v.tensor_tensor(mmu[:, :, :], mu[:, 0, :].unsqueeze(2).broadcast_to([P, 8, 4]),
                                        g.c(QUAD, 4).unsqueeze(1).broadcast_to([P, 8, 4]), ALU.mult))
                shift_tiles(v, ln, raw, pq, mmu, mu[:, 1, :])

            project(nc, g, f"gdp{l}", g.w_in[l][:, GDN0:GDN0 + 8 * P], 8, g.hT, SEG_ALL, out=gd_raw, sems="vec_in",
                    beside={"sync": loads, "vector": shift})

        aT, kd = tmp("rk_a", [P, 2 * WT, T]), tmp("rk_kd", [P, 2 * WT, T])
        kk, lw = tmp("rk_kk", [P, WT, T]), tmp("rk_lw", [P, TT, 2 * W])
        with ExitStack() as mem, Stage(nc, f"rkl{l}", "w_in act_ready full read") as s:
            g2 = mem.enter_context(sbuf(nc, "g2", [P, W]))
            wa = mem.enter_context(sbuf(nc, "w2a2", [P, 2, W]))
            w0 = mem.enter_context(sbuf(nc, "w0", [1, 2 * W]))
            a0 = mem.enter_context(sbuf(nc, "a0", [P, 2, WT]))
            ps = [mem.enter_context(psum(nc, "lps", [P, 512])) for _ in range(8)]
            q = s.sem
            jobs = [("gate", 0, n) for n in range(WT)] + [("a", d, n) for d in range(2) for n in range(WT)]
            jobs += [("w", t, 0) for t in range(TT)]

            @s.body.sync
            def _(sp):
                sp.dma_start(g2[:, :], g.rwkv_g2[l]).then_inc(q["w_in"], 16)
                sp.dma_start(wa[0:HD, :, :], g.rwkv_w2[l].rearrange("d r w -> r d w")).then_inc(q["w_in"], 16)
                sp.dma_start(wa[HD:P, :, :], g.rwkv_a2[l].rearrange("d r w -> r d w")).then_inc(q["w_in"], 16)
                sp.dma_start(w0[:, :], g.rwkv_w0[l:l + 1].rearrange("a d w -> a (d w)")).then_inc(q["w_in"], 16)
                with nc.allow_non_contiguous_dma(reason="vectors onto partitions"):
                    for d in range(2):
                        sp.dma_start(a0[:, d, :], g.rwkv_a0[l, d].rearrange("(t p) -> p t", p=P)).then_inc(q["w_in"], 16)

            @s.body.tensor
            def _(pe):
                pe.wait_ge(q["w_in"], 96)
                pe.wait_ge(q["act_ready"], 1)
                for n, (kind, d, j) in enumerate(jobs):
                    if n >= 4:
                        pe.wait_ge(q["read"], n - 3)
                    b = n % 4 * 2
                    if kind == "w":
                        pe.matmul(ps[b][:, :], pq[0:HD, 6, d * P:(d + 1) * P], wa[0:HD, :, :].rearrange("r d w -> r (d w)"),
                                  start=True, stop=False)
                        last = pe.matmul(ps[b][:, :], g.c(ONES)[0:1, :], w0[0:1, :], start=False, stop=True)
                    for half in range(2 if kind != "w" else 0):
                        cut = slice(half * HALF, (half + 1) * HALF)
                        lhs, rhs = ((g2[:, j * P:(j + 1) * P], pq[:, 7, cut]) if kind == "gate" else
                                    (wa[HD:P, d, j * P:(j + 1) * P], pq[HD:P, 6, cut]))
                        last = pe.matmul(ps[b + half][:, 0:HALF], lhs, rhs, start=True, stop=True)
                    last.then_inc(q["full"], 1)

            @s.body.scalar
            def _(act):
                ln = s.line(act, "act")
                ln.link(act.activation(pq[0:HD, 6, :], pq[0:HD, 6, :], ACT.Tanh))
                ln.link(act.activation(pq[:, 7, :], pq[:, 7, :], ACT.Sigmoid))
                ln.tell(q["act_ready"])
                act.wait_ge(q["w_in"], 96)
                for n, (kind, d, j) in enumerate(jobs):
                    act.wait_ge(q["full"], n + 1)
                    b = n % 4 * 2
                    if kind == "w":
                        ln.link(act.activation(lw[:, d, :], ps[b][:, :], ACT.Sigmoid))
                    for half in range(2 if kind != "w" else 0):
                        cut = slice(half * HALF, (half + 1) * HALF)
                        if kind == "gate":
                            ln.link(act.activation(gate[:, j, cut], ps[b + half][:, 0:HALF], ACT.Copy))
                        else:
                            ln.link(act.activation(aT[:, d * WT + j, cut], ps[b + half][:, 0:HALF], ACT.Sigmoid, bias=a0[:, d, j:j + 1]))
                    ln.tell(q["read"])

            @s.body.vector
            def _(v):
                ln = s.line(v, "dve")
                for n in range(WT):
                    ln.link(v.tensor_scalar(kk[:, n, :], pq[:, 2 + n, :], vec[:, 0, n:n + 1], None, ALU.mult))
        normalize(nc, g, f"rkn{l}", kk[:, :, :], BLK, 1.0)
        with ExitStack() as mem, Stage(nc, f"rkb{l}", "prod_ready summed ready bonus_ready stored") as s:
            one_ka = mem.enter_context(sbuf(nc, "one_ka", [P, WT]))
            t = mem.enter_context(sbuf(nc, "rk_t", [P, WT, T]))
            ps = [mem.enter_context(psum(nc, "bps", [P, 512])) for _ in range(4)]
            q = s.sem

            @s.body.vector
            def _(v):
                ln = s.line(v, "dve")
                ln.link(v.tensor_scalar(one_ka[:, :], vec[:, 1, :], -1.0, 1.0, ALU.mult, ALU.add))
                for d in range(2):
                    for n in range(WT):
                        m = d * WT + n
                        ln.link(v.tensor_scalar(kd[:, m, :], aT[:, m, :], vec[:, 1, n:n + 1], one_ka[:, n:n + 1], ALU.mult, ALU.add))
                        ln.link(v.tensor_tensor(kd[:, m, :], kd[:, m, :], pq[:, 2 + n, :], ALU.mult))
                        ln.link(v.tensor_tensor(aT[:, m, :], aT[:, m, :], kk[:, n, :], ALU.mult))
                ln.tell(q["ready"])
                ln.link(v.tensor_tensor(t[:, :, :], kd[:, 0:WT, :], kd[:, WT:2 * WT, :], ALU.add))
                for n in range(WT):
                    ln.link(v.scalar_tensor_tensor(t[:, n, :], t[:, n, :], vec[:, 2, n:n + 1], pq[:, n, :], ALU.mult, ALU.mult))
                ln.tell(q["prod_ready"])
                v.wait_ge(q["summed"], 1)
                for n in range(WT):
                    for half in range(2):
                        cut = slice(half * HALF, (half + 1) * HALF)
                        ln.link(v.tensor_tensor(bonus[:, n, cut], pq[:, 4 + n, cut], ps[2 * n + half][:, 0:HALF], ALU.mult))
                ln.tell(q["bonus_ready"])

            @s.body.tensor
            def _(pe):
                pe.wait_ge(q["prod_ready"], 1)
                for n in range(WT):
                    for half in range(2):
                        last = pe.matmul(ps[2 * n + half][:, 0:HALF], g.c(BLK), t[:, n, half * HALF:(half + 1) * HALF], start=True, stop=True)
                last.then_inc(q["summed"], 1)

            @s.body.sync
            def _(sp):
                f = g.rk_feat.rearrange("n p t -> p n t")
                sp.dma_start(f[:, 0:2, :], pq[:, 0:2, :]).then_inc(q["stored"], 16)
                sp.dma_start(f[:, 2:4, :], pq[:, 4:6, :]).then_inc(q["stored"], 16)
                sp.dma_start(f[:, 4:6, :], kk[:, :, :]).then_inc(q["stored"], 16)
                sp.dma_start(g.rk_logw.rearrange("(t p) n -> p t n", p=P), lw[:, :, :]).then_inc(q["stored"], 16)
                sp.wait_ge(q["ready"], 1)
                sp.dma_start(f[:, 6:10, :], kd[:, :, :]).then_inc(q["stored"], 16)
                sp.dma_start(f[:, 10:14, :], aT[:, :, :]).then_inc(q["stored"], 16)
                sp.dma_start(f[:, 14:16, :], gate[:, :, :]).then_inc(q["stored"], 16)
                sp.wait_ge(q["bonus_ready"], 1)
                sp.dma_start(f[:, 16:18, :], bonus[:, :, :]).then_inc(q["stored"], 16)
                sp.wait_ge(q["stored"], 128)


def rwkv_end(nc, g, l, y, vec):
    normalize(nc, g, f"rky{l}", y[:, :, :], BLK, 1.0 / HD, center=True)
    with ExitStack() as mem, Stage(nc, f"rko{l}", "back_in") as s:
        gb = mem.enter_context(sbuf(nc, "rk_gb", [P, 2 * WT, T]))

        @s.body.sync
        def _(sp):
            sp.dma_start(gb[:, :, :], g.rk_feat[14:18].rearrange("n p t -> p n t")).then_inc(s.sem["back_in"], 16)

        @s.body.vector
        def _(v):
            ln = s.line(v, "dve")
            for m in range(2 * WT):
                n = m % WT
                ln.link(v.tensor_scalar(y[:, m, :], y[:, m, :], vec[:, 3, n:n + 1], vec[:, 4, n:n + 1], ALU.mult, ALU.add))
            ln.link(v.tensor_tensor(y[:, 0:WT, :], y[:, 0:WT, :], y[:, WT:2 * WT, :], ALU.add))
            v.wait_ge(s.sem["back_in"], 16)
            ln.link(v.tensor_tensor(y[:, 0:WT, :], y[:, 0:WT, :], gb[:, WT:2 * WT, :], ALU.add))
            ln.link(v.tensor_tensor(g.oT[:, 0, :, :], y[:, 0:WT, :], gb[:, 0:WT, :], ALU.mult))


def gdn_front(nc, g, l, raw, zs, gd, beta):
    PADG = CONV_G // 2
    LONGG = PADG + CTX + PADG + SEQ + PADG
    with ExitStack() as prep:
        f = prep.enter_context(sbuf(nc, "gd_f", [P, 6, T]))
        with ExitStack() as mem, Stage(nc, f"gdc{l}", "w_in full conv_ready sig_ready asked given") as s:
            pad = mem.enter_context(sbuf(nc, "gd_pad", [P, 6, LONGG]))
            acc = mem.enter_context(sbuf(nc, "gd_acc", [P, LONGG]))
            taps = mem.enter_context(sbuf(nc, "gd_taps", [P, 6, CONV_G]))
            wab = mem.enter_context(sbuf(nc, "gd_wab", [P, KD, 16]))
            rowv = mem.enter_context(sbuf(nc, "gd_rowv", [P, 2, 8]))
            sp0 = mem.enter_context(sbuf(nc, "gd_sp0", [P, TT, 8]))
            sp1 = mem.enter_context(sbuf(nc, "gd_sp1", [P, TT, 8]))
            sig = mem.enter_context(sbuf(nc, "gd_sig", [P, 8, T]))
            ps = mem.enter_context(psum(nc, "gab", [P, 512]))
            q = s.sem
            ab = mem.enter_context(sbuf(nc, "gd_ab", [P, TT, 16]))

            @s.body.sync
            def _(sp):
                with nc.allow_non_contiguous_dma(reason="small weights onto partitions"):
                    for n in range(6):
                        sp.dma_start(taps[:, n, :], g.gdn_conv_w[l][:, n * P:(n + 1) * P].rearrange("k p -> p k")).then_inc(q["w_in"], 16)
                    sp.dma_start(wab[:, :, :], g.w_in[l][:, AB0:AB0 + 16].rearrange("(k p) n -> p k n", p=P)).then_inc(q["w_in"], 16)
                    for n, a in enumerate((g.gdn_a_log, g.gdn_dt_bias)):
                        sp.dma_start(rowv[:, n, :], a[l].rearrange("d h -> (d h)").partition_broadcast(P)).then_inc(q["w_in"], 16)

            @s.body.tensor
            def _(pe):
                pe.wait_ge(q["w_in"], 144)
                for t in range(TT):
                    for k in range(KD):
                        last = pe.matmul(ps[:, t * 16:t * 16 + 16], g.hT[:, k, t * P:(t + 1) * P], wab[:, k, :], start=k == 0, stop=k == KD - 1)
                last.then_inc(q["full"], 1)

            @s.body.scalar
            def _(act):
                ln = s.line(act, "act")
                ln.link(act.activation(sig[:, 6:8, :], raw[:, 6:8, :], ACT.Sigmoid))
                ln.tell(q["sig_ready"])
                act.wait_ge(q["asked"], 1)
                ln.link(act.activation(beta[:, :, :], ab[:, :, 8:16], ACT.Sigmoid))
                act.wait_ge(q["asked"], 2)
                ln.link(act.activation(sp1[:, :, :], sp1[:, :, :], ACT.Exp, scale=-1.0))
                ln.link(act.activation(rowv[:, 0, :], rowv[:, 0, :], ACT.Exp))
                ln.link(act.activation(sp1[:, :, :], sp1[:, :, :], ACT.Ln, bias=1.0))
                ln.tell(q["given"])
                for n in range(6):
                    act.wait_ge(q["conv_ready"], n + 1)
                    ln.link(act.activation(sig[:, n, :], f[:, n, :], ACT.Sigmoid))
                    ln.tell(q["sig_ready"])

            @s.body.vector
            def _(v):
                ln = s.line(v, "dve")
                ln.link(v.memset(pad[:, :, :], 0.0))
                v.wait_ge(q["w_in"], 144)
                v.wait_ge(q["full"], 1)
                ln.link(v.tensor_copy(ab[:, :, :], ps[:, 0:TT * 16].rearrange("p (t n) -> p t n", n=16)))
                ln.tell(q["asked"])
                dt = rowv[:, 1, :].unsqueeze(1).broadcast_to([P, TT, 8])
                ln.link(v.tensor_tensor(sp0[:, :, :], ab[:, :, 0:8], dt, ALU.add))
                ln.link(v.scalar_tensor_tensor(sp1[:, :, :], sp0[:, :, :], -1.0, sp0[:, :, :], ALU.mult, ALU.max))
                ln.tell(q["asked"])
                ln.link(v.tensor_copy(pad[:, :, PADG:PADG + CTX], raw[:, 0:6, 0:CTX]))
                ln.link(v.tensor_copy(pad[:, :, 2 * PADG + CTX:2 * PADG + T], raw[:, 0:6, CTX:T]))
                for n in range(6):
                    conv(v, ln, acc[:, :], pad[:, n, :], lambda k: taps[:, n, k:k + 1], CONV_G, None, PADG)
                    ln.link(v.tensor_copy(f[:, n, 0:CTX], acc[:, 0:CTX]))
                    ln.link(v.tensor_copy(f[:, n, CTX:T], acc[:, CTX + PADG:CTX + PADG + SEQ]))
                    ln.tell(q["conv_ready"])
                v.wait_ge(q["given"], 1)
                ln.link(v.scalar_tensor_tensor(sp0[:, :, :], sp0[:, :, :], 0.0, sp1[:, :, :], ALU.max, ALU.add))
                ln.link(v.scalar_tensor_tensor(gd[:, :, :], sp0[:, :, :], -1.0,
                                               rowv[:, 0, :].unsqueeze(1).broadcast_to([P, TT, 8]), ALU.mult, ALU.mult))
                v.wait_ge(q["sig_ready"], 7)
                ln.link(v.tensor_tensor(zs[:, :, :], raw[:, 6:8, :], sig[:, 6:8, :], ALU.mult))
                ln.link(v.tensor_tensor(f[:, :, :], f[:, :, :], sig[:, 0:6, :], ALU.mult))
        normalize(nc, g, f"gdn{l}", f[:, 0:4, :], BLK, 1.0)
        with Stage(nc, f"gdf{l}", "ready stored") as s:
            q = s.sem

            @s.body.vector
            def _(v):
                ln = s.line(v, "dve")
                ln.link(v.tensor_scalar(f[:, 0:WT, :], f[:, 0:WT, :], HD ** -0.5, None, ALU.mult))
                ln.tell(q["ready"])

            @s.body.sync
            def _(sp):
                sp.wait_ge(q["ready"], 1)
                sp.dma_start(g.gd_feat.rearrange("n p t -> p n t"), f[:, :, :]).then_inc(q["stored"], 16)
                sp.wait_ge(q["stored"], 16)


def gdn_end(nc, g, l, y, zs):
    with Stage(nc, f"gds{l}") as s:
        @s.body.vector
        def _(v):
            ln = s.line(v, "dve")
            ln.link(v.tensor_tensor(y[:, 0:WT, :], y[:, 0:WT, :], y[:, WT:2 * WT, :], ALU.add))
    normalize(nc, g, f"gdy{l}", y[:, 0:WT, :], BLK, 1.0 / HD)
    with ExitStack() as mem, Stage(nc, f"gdo{l}", "vec_in") as s:
        ng = mem.enter_context(sbuf(nc, "gd_ng", [P, 1]))

        @s.body.sync
        def _(sp):
            with nc.allow_non_contiguous_dma(reason="a vector onto partitions"):
                for hf in range(2):
                    sp.dma_start(ng[hf * HD:(hf + 1) * HD, :], g.gdn_norm_g[l].rearrange("(p a) -> p a", a=1)).then_inc(s.sem["vec_in"], 16)

        @s.body.vector
        def _(v):
            ln = s.line(v, "dve")
            v.wait_ge(s.sem["vec_in"], 32)
            for n in range(WT):
                ln.link(v.scalar_tensor_tensor(g.oT[:, 1, n, :], y[:, n, :], ng[:, 0:1], zs[:, n, :], ALU.mult, ALU.mult))


def mixers(nc, g, l):
    with ExitStack() as mem:
        def keep(name, shape):
            return mem.enter_context(sbuf(nc, name, shape))

        vec = keep("rk_vec", [P, 5, WT])
        zs = keep("gd_z", [P, WT, T])
        gd = keep("gd_g", [P, TT, 8])
        beta = keep("gd_beta", [P, TT, 8])
        with sbuf(nc, "gd_p", [P, 8, T]) as gd_raw:
            rwkv_front(nc, g, l, vec, gd_raw)
            gdn_front(nc, g, l, gd_raw, zs, gd, beta)
        y_rk, y_gd = (g.oT[:, 2 * n:2 * n + 2, :, :].rearrange("p b n t -> p (b n) t") for n in range(2))
        recurrence(nc, g, f"rec{l}", y_rk, y_gd, gd, beta)
        rwkv_end(nc, g, l, y_rk, vec)
        gdn_end(nc, g, l, y_gd, zs)


def recurrence(nc, g, name, y_rk, y_gd, gd, beta):
    ROUNDS = TT
    RK, GD = "rk", "gd"
    KINDS = (RK, GD)
    both_kinds = ("feat_in feat_free front_ready exp_ready turned moved lt_full lt_ready mo_full mats_done levels t_full "
                  "t_moved p_full x_ready rhs_full rhs_moved u_full u_moved o_full o_moved s_full s_ready act_end dve_end").split()
    sems = [f"{k}_{n}" for k in KINDS for n in both_kinds]
    sems += "rk_v_ready rk_ops_ready rk_ak_full rk_ak_read rk_mv_full gd_gb_ready gd_tok_ready gd_rows_ready gd_diff_ready gd_gamma_ready".split()
    with ExitStack() as mem, Stage(nc, name, " ".join(sems)) as s:
        q = s.sem

        def sb(n, shape):
            return mem.enter_context(sbuf(nc, n, shape))

        def each(n, shape):
            return {k: sb(f"{k}_{n}", shape) for k in KINDS}

        NF = {RK: 10, GD: 6}
        ft = {k: sb(f"{k}_ft", [P, 2, NF[k], P]) for k in KINDS}
        kkt, rt = each("kkt", [P, 4, P]), each("rt", [P, 4, P])
        vt, kt = each("vt", [P, 2, W]), each("kt", [P, 2, W])
        lt, x, xt, tt, mo = (each(n, [P, 8, C]) for n in ("lt", "x", "xt", "tt", "mo"))
        lk = each("lk", [P, LEVELS, 8, C])
        st = each("st", [P, 2, 4, HD])
        dec = each("dec", [P, 2, 4])
        rs, us = each("rs", [P, W]), each("us", [P, W])
        lw = sb("lw", [P, 2, W])
        e_in, e_ex, e_ng = (sb(n, [P, 2, 2, P]) for n in ("e_in", "e_ex", "e_ng"))
        kht, bht = sb("kht", [P, 4, P]), sb("bht", [P, 4, P])
        bt = sb("bt", [P, 2, W])
        ak, mv = sb("ak", [P, 8, C]), sb("mv", [P, 8, C])
        gs, be = sb("gs", [P, 2, 4]), sb("be", [P, 2, 4])
        gb = sb("gb", [P, 8, C])
        eg, gcs = sb("eg", [P, 32]), sb("gcs", [P, 8])
        kb, kbe, qe = (sb(n, [P, 8, HD]) for n in ("kb", "kbe", "qe"))
        kbt = sb("kbt", [P, 4, P])
        gam, gam_s = sb("gam", [P, 8, C]), sb("gam_s", [P, 8, C])
        BANKS = {k: [mem.enter_context(psum(nc, f"{k}_b{i}", [P, 512])) for i in range(4)] for k in KINDS}
        Y = {RK: y_rk, GD: y_gd}

        def half(bank):
            return bank[:, 0:4 * C].rearrange("p (z t) -> p z t", z=4)

        def whole(bank):
            return bank[:, :].rearrange("p (z t) -> p z t", z=8)

        def both(col, stride):
            return g.c(col, 2 * stride).rearrange("p (d s) -> p d s", d=2)[:, :, 0:C].unsqueeze(2).broadcast_to([P, 2, 2, C])

        def quad(a):
            return a.rearrange("p (d w) t -> p d w t", d=2)

        INCL, STRICT, MINUS = both(CINCL, C), both(CSTRICT, C), both(CMINUS, C)
        EYE = g.c(CEYE, C)
        EYES = EYE.unsqueeze(1).broadcast_to([P, 8, C])

        def z_of(d, h):
            pair = d * 2 + h // 2
            return h % 2 * 4 + pair, slice(h % 2 * HD, (h % 2 + 1) * HD), pair

        ZS = [(d, h) for h in range(H) for d in range(2)]
        CH = [slice(c * C, (c + 1) * C) for c in range(2)]

        def chunk(d, r):
            return CH[r if d == 0 else 1 - r]

        def tiles(i):
            return i, (7 - i) % TT

        loads = {RK: 8 * 16, GD: 2 * 16}

        @s.body.sync
        def _(sp):
            ln = s.line(sp, "sp")
            with sp.Fori(0, ROUNDS) as i:
                for k in KINDS:
                    ln.hold(q[f"{k}_feat_free"], i + 1)
                    f = (g.rk_feat if k == RK else g.gd_feat).rearrange("n p t -> p n t")
                    for d, t in enumerate(tiles(i)):
                        at, landed = bass.ds(t * P, P), q[f"{k}_feat_in"]
                        sp.dma_start(ft[k][:, d, 0:6, :], f[:, 0:6, at]).then_inc(landed, 16)
                        if k == RK:
                            sp.dma_start(ft[k][:, d, 6:8, :], f[:, 6 + 2 * d:8 + 2 * d, at]).then_inc(landed, 16)
                            sp.dma_start(ft[k][:, d, 8:10, :], f[:, 10 + 2 * d:12 + 2 * d, at]).then_inc(landed, 16)
                            sp.dma_start(lw[:, d, :], g.rk_logw[at, d * W:(d + 1) * W]).then_inc(landed, 16)

        @s.body.tensor
        def _(pe):
            ln = s.line(pe, "pe")

            def turn(bank, src):
                for n in range(4):
                    last = pe.transpose(bank[:, n * P:(n + 1) * P], src(n), g.c(IDENT))
                return last

            def grams(banks, lhs, rhs):
                for ch in CH:
                    for d in range(2):
                        for h in range(H):
                            _, part, pair = z_of(d, h)
                            last = pe.matmul(half(banks[h % 2])[ch, pair, :], lhs(part, d, h, pair, ch), rhs(part, d, h, pair, ch), start=True, stop=True)
                return last

            def squares(bank, lhs, rhs):
                for d, h in ZS:
                    z, _, _ = z_of(d, h)
                    for ch in CH:
                        last = pe.matmul(whole(bank)[ch, z, :], lhs[ch, z, :], rhs(z, ch), start=True, stop=True)
                return last

            with pe.Fori(0, ROUNDS) as i:
                for k in KINDS:
                    B, f = BANKS[k], ft[k]
                    ln.hold(q[f"{k}_act_end"], i + 1)
                    ln.hold(q[f"{k}_dve_end"], i + 1)
                    ln.hold(q[f"{k}_feat_in"], i * loads[k] + loads[k])
                    if k == RK:
                        turn(B[2], lambda n: f[:, n // 2, 2 + n % 2, :])
                        for d in range(2):
                            for hp in range(2):
                                last = pe.matmul(B[d][:, hp * 2 * P:(hp + 1) * 2 * P], lw[:, d, hp * P:(hp + 1) * P],
                                                 g.c(MASKS + d * 2 * P, 2 * P), start=True, stop=True)
                    else:
                        for n, at in enumerate((0, 2, 4)):
                            turn(B[n], lambda m: f[:, m // 2, at + m % 2, :])
                        ln.hold(q["gd_gb_ready"], i + 1)
                        for d in range(2):
                            pe.matmul(B[3][:, d * 4:d * 4 + 4], g.c(MASKS + d * 2 * P), gs[:, d, :], start=True, stop=True)
                            pe.matmul(B[3][:, 8 + d * 4:12 + d * 4], g.c(MASKS + (1 - d) * 2 * P + P), gs[:, d, :], start=True, stop=True)
                        for c in range(2):
                            last = pe.matmul(B[3][:, 16 + 8 * c:24 + 8 * c], g.c(CHUNK + c * P), gs[:, :, :].rearrange("p d h -> p (d h)"),
                                             start=True, stop=True)
                    last.then_inc(q[f"{k}_front_ready"], 1)
                B = BANKS[RK]
                ln.hold(q["rk_v_ready"], i + 1)
                ln.hold(q["rk_ops_ready"], i + 1)
                grams(B[0:2], lambda p, d, h, w, ch: bht[p, w, ch], lambda p, d, h, w, ch: kkt[RK][p, w, ch]).then_inc(q["rk_lt_full"], 1)
                turn(B[3], lambda n: kht[:, n, :])
                turn(B[2], lambda n: bht[:, n, :]).then_inc(q["rk_turned"], 1)
                B = BANKS[GD]
                ln.hold(q["gd_tok_ready"], i + 1)
                for n, src in enumerate((kb, kbe, qe)):
                    last = turn(B[n], lambda m: src[:, 2 * m:2 * m + 2, :].rearrange("p h e -> p (h e)"))
                last.then_inc(q["gd_turned"], 1)
                for d, h in ZS:
                    z, _, _ = z_of(d, h)
                    for ch in CH:
                        last = pe.matmul(whole(B[3])[ch, z, :], gb[ch, d * H + h, :], g.c(CINCL + d * C, C)[ch, :], start=True, stop=True)
                last.then_inc(q["gd_rows_ready"], 1)
                B = BANKS[RK]
                ln.hold(q["rk_moved"], i + 1)
                grams(B[2:4], lambda p, d, h, w, ch: kht[p, w, ch], lambda p, d, h, w, ch: kkt[RK][p, w, ch]).then_inc(q["rk_ak_full"], 1)
                ln.hold(q["rk_lt_ready"], i + 1)
                grams(B[0:2], lambda p, d, h, w, ch: kht[p, w, ch], lambda p, d, h, w, ch: rt[RK][p, w, ch]).then_inc(q["rk_mv_full"], 1)
                B, f = BANKS[GD], ft[GD]
                ln.hold(q["gd_moved"], i + 1)
                grams(B[0:2], lambda p, d, h, w, ch: f[p, d, 2 + h // 2, ch], lambda p, d, h, w, ch: kbt[p, w, ch]).then_inc(q["gd_lt_full"], 1)
                ln.hold(q["rk_ak_read"], i + 1)
                grams(BANKS[RK][2:4], lambda p, d, h, w, ch: bht[p, w, ch], lambda p, d, h, w, ch: rt[RK][p, w, ch]).then_inc(q["rk_mo_full"], 1)
                ln.hold(q["gd_diff_ready"], i + 1)
                grams(B[2:4], lambda p, d, h, w, ch: f[p, d, 2 + h // 2, ch], lambda p, d, h, w, ch: f[p, d, h // 2, ch]).then_inc(q["gd_mo_full"], 1)
                for n in range(LEVELS):
                    for k in KINDS:
                        if n == 0:
                            ln.hold(q[f"{k}_mats_done"], i + 1)
                        else:
                            ln.hold(q[f"{k}_x_ready"], i * LEVELS + n)
                        ln.hold(q[f"{k}_levels"], i * LEVELS + n + 1)
                        squares(BANKS[k][0], lk[k][:, n, :, :], (lambda z, ch: EYE[ch, :]) if n == 0 else
                                (lambda z, ch: x[k][ch, z, :])).then_inc(q[f"{k}_t_full"], 1)
                    for k in KINDS if n else ():
                        ln.hold(q[f"{k}_t_moved"], i * (LEVELS - 1) + n)
                        if n < LEVELS - 1:
                            squares(BANKS[k][1], xt[k], lambda z, ch: tt[k][ch, z, :])
                        squares(BANKS[k][2], tt[k], lambda z, ch: xt[k][ch, z, :]).then_inc(q[f"{k}_p_full"], 1)
                for r in range(2):
                    for k in KINDS:
                        B = BANKS[k]
                        if r == 0:
                            ln.hold(q[f"{k}_x_ready"], i * LEVELS + LEVELS)
                        ln.hold(q[f"{k}_s_ready"], i * 2 + r + 1)
                        for d, h in ZS:
                            z, part, pair = z_of(d, h)
                            ch, hv = chunk(d, r), slice(h * HD, (h + 1) * HD)
                            last = pe.matmul(B[0][ch, hv], kkt[k][:, pair, ch], st[k][:, h % 2, pair, :], start=True, stop=k == GD)
                            if k == RK:
                                last = pe.matmul(B[0][ch, hv], ak[ch, z, :], vt[k][ch, d, hv], start=False, stop=True)
                        last.then_inc(q[f"{k}_rhs_full"], 1)
                    for k in KINDS:
                        ln.hold(q[f"{k}_rhs_moved"], i * 2 + r + 1)
                        for d, h in ZS:
                            z, _, _ = z_of(d, h)
                            ch, hv = chunk(d, r), slice(h * HD, (h + 1) * HD)
                            last = pe.matmul(BANKS[k][1][ch, hv], xt[k][ch, z, :], rs[k][ch, hv], start=True, stop=True)
                        last.then_inc(q[f"{k}_u_full"], 1)
                    for k in KINDS:
                        B = BANKS[k]
                        ln.hold(q[f"{k}_u_moved"], i * 2 + r + 1)
                        for d, h in ZS:
                            _, part, pair = z_of(d, h)
                            ch, hv = chunk(d, r), slice(h * HD, (h + 1) * HD)
                            o = B[d][part, h // 2 * HD:(h // 2 + 1) * HD]
                            if k == RK:
                                pe.matmul(o, kt[k][ch, d, hv], vt[k][ch, d, hv], start=True, stop=False)
                            last = pe.matmul(o, (bt if k == RK else kt[k])[ch, d, hv], us[k][ch, hv], start=k != RK, stop=True)
                        last.then_inc(q[f"{k}_s_full"], 1)
                        ln.hold(q[f"{k}_o_moved"], i * 2 + r + 1)
                        for d, h in ZS:
                            z, part, pair = z_of(d, h)
                            ch, hv = chunk(d, r), slice(h * HD, (h + 1) * HD)
                            o = B[2 + d][part, h // 2 * C:(h // 2 + 1) * C]
                            pe.matmul(o, st[k][:, h % 2, pair, :], rt[k][:, pair, ch], start=True, stop=False)
                            if k == RK:
                                pe.matmul(o, vt[k][ch, d, hv], mv[ch, z, :], start=False, stop=False)
                            last = pe.matmul(o, us[k][ch, hv], mo[k][ch, z, :], start=False, stop=True)
                        last.then_inc(q[f"{k}_o_full"], 1)

        @s.body.scalar
        def _(act):
            ln = s.line(act, "act")
            for k in KINDS:
                ln.credit(q[f"{k}_act_end"], q[f"{k}_o_moved"])
            with act.Fori(0, ROUNDS) as i:
                for k in KINDS:
                    ln.hold(q[f"{k}_act_end"], i + 1)
                    ln.hold(q[f"{k}_dve_end"], i + 1)
                B = BANKS[RK]
                ln.hold(q["rk_front_ready"], i + 1)
                for d in range(2):
                    c = B[d][:, :].rearrange("p (h e t) -> p h e t", h=2, e=2)
                    ln.link(act.activation(e_in[:, d, :, :], c[:, :, 0, :], ACT.Exp, scale=-DECAY))
                    ln.link(act.activation(e_ng[:, d, :, :], c[:, :, 0, :], ACT.Exp, scale=DECAY))
                    ln.link(act.activation(e_ex[:, d, :, :], c[:, :, 1, :], ACT.Exp, scale=-DECAY))
                ln.tell(q["rk_exp_ready"])
                ln.hold(q["gd_front_ready"], i + 1)
                ln.link(act.activation(eg[:, :], BANKS[GD][3][:, 0:32], ACT.Exp))
                ln.tell(q["gd_exp_ready"])
                ln.link(act.activation(vt[RK][:, :, :], B[2][:, :].rearrange("p (d v) -> p d v", d=2), ACT.Copy))
                ln.tell(q["rk_v_ready"])
                ln.hold(q["rk_turned"], i + 1)
                ln.link(act.activation(kt[RK][:, :, :], B[3][:, :].rearrange("p (d v) -> p d v", d=2), ACT.Copy))
                ln.link(act.activation(bt[:, :, :], B[2][:, :].rearrange("p (d v) -> p d v", d=2), ACT.Copy, scale=-1.0))
                ln.tell(q["rk_moved"])
                ln.hold(q["gd_turned"], i + 1)
                for bank, dst in zip(BANKS[GD], (kbt, kkt[GD], rt[GD])):
                    ln.link(act.activation(dst[:, :, :], bank[:, :].rearrange("p (w t) -> p w t", w=4), ACT.Copy))
                ln.tell(q["gd_moved"])
                ln.hold(q["gd_diff_ready"], i + 1)
                ln.link(act.activation(gam[:, :, :], gam[:, :, :], ACT.Exp))
                ln.tell(q["gd_gamma_ready"])
                for n in range(1, LEVELS):
                    for k in KINDS:
                        ln.hold(q[f"{k}_t_full"], i * LEVELS + n + 1)
                        ln.link(act.activation(tt[k][:, :, :], whole(BANKS[k][0]), ACT.Copy))
                        ln.tell(q[f"{k}_t_moved"])
                for r in range(2):
                    ln.hold(q["rk_rhs_full"], i * 2 + r + 1)
                    ln.link(act.activation(rs[RK][:, :], BANKS[RK][0][:, 0:W], ACT.Copy))
                    ln.tell(q["rk_rhs_moved"])
                    for k in KINDS:
                        ln.hold(q[f"{k}_o_full"], i * 2 + r + 1)
                        for d, t in enumerate(tiles(i)):
                            c = r if d == 0 else 1 - r
                            ln.link(act.activation(Y[k][:, d * 2:d * 2 + 2, bass.ds(t * P + c * C, C)],
                                                   BANKS[k][2 + d][:, 0:2 * C].rearrange("p (h t) -> p h t", h=2), ACT.Copy))
                        ln.tell(q[f"{k}_o_moved"])
                for k in KINDS:
                    ln.tell(q[f"{k}_act_end"])
                ln.restart()

        @s.body.gpsimd
        def _(pool):
            ln = s.line(pool, "pool")
            with pool.Fori(0, ROUNDS) as i:
                for k in KINDS:
                    ln.hold(q[f"{k}_act_end"], i + 1)
                    ln.hold(q[f"{k}_dve_end"], i + 1)
                    ln.hold(q[f"{k}_lt_ready"], i + 1)
                    for n in range(LEVELS):
                        for e in range(2):
                            cut = slice(e * 4, e * 4 + 4)
                            ln.link(pool.tensor_tensor(quad(lk[k][:, n, cut, :]), quad(lt[k][:, cut, :]), both(CLEVEL + 2 * n * C, C), ALU.mult))
                        ln.tell(q[f"{k}_levels"])
                ln.restart()

        @s.body.vector
        def _(v):
            ln = s.line(v, "dve")
            for k in KINDS:
                ln.link(v.memset(st[k][:, :, :, :], 0.0))
                ln.credit(q[f"{k}_dve_end"], q[f"{k}_feat_free"], q[f"{k}_s_ready"])
            ln.restart()
            halves = [slice(e * 4, e * 4 + 4) for e in range(2)]

            def masked(out, banks, m):
                for cut, bank in zip(halves, banks):
                    ln.link(v.tensor_tensor(quad(out[:, cut, :]), quad(half(bank)), m, ALU.mult))

            with v.Fori(0, ROUNDS) as i:
                for k in KINDS:
                    ln.hold(q[f"{k}_act_end"], i + 1)
                    ln.hold(q[f"{k}_dve_end"], i + 1)
                for d, t in enumerate(tiles(i)):
                    ln.link(v.tensor_copy(gs[:, d, :].unsqueeze(1), gd[:, bass.ds(t, 1), d * H:(d + 1) * H]))
                    ln.link(v.tensor_copy(be[:, d, :].unsqueeze(1), beta[:, bass.ds(t, 1), d * H:(d + 1) * H]))
                ln.link(v.tensor_copy(gb[:, :, :], gs[:, :, :].rearrange("p d h -> p (d h)").unsqueeze(2).broadcast_to([P, 8, C])))
                ln.tell(q["gd_gb_ready"])

                ln.hold(q["rk_feat_in"], i * loads[RK] + loads[RK])
                ln.hold(q["rk_exp_ready"], i + 1)
                for d in range(2):
                    cut = slice(2 * d, 2 * d + 2)
                    for o, e, at in ((bht, e_ng, 8), (kkt[RK], e_ex, 4), (kht, e_ng, 6), (rt[RK], e_in, 0)):
                        ln.link(v.tensor_tensor(o[:, cut, :], e[:, d, :, :], ft[RK][:, d, at:at + 2, :], ALU.mult))
                ln.tell(q["rk_ops_ready"])
                ln.tell(q["rk_feat_free"])
                for d in range(2):
                    for c in range(2):
                        end = c * C + (C - 1 if d == 0 else 0)
                        ln.link(v.tensor_copy(dec[RK][:, c, 2 * d:2 * d + 2], e_in[:, d, :, end]))

                ln.hold(q["gd_exp_ready"], i + 1)
                B = BANKS[GD]
                ln.link(v.tensor_copy(gcs[:, :], B[3][:, 0:8]))

                def heads(bank):
                    return bank[:, :].rearrange("p (z e) -> p z e", z=8)

                def wide(a):
                    return a.unsqueeze(2).broadcast_to([P, 8, HD])

                bz = wide(be[:, :, :].rearrange("p d h -> p (d h)"))
                v8, k8 = (m[:, :, :].rearrange("p d (h e) -> p (d h) e", e=HD) for m in (vt[GD], kt[GD]))
                ln.link(v.tensor_tensor(kb[:, :, :], heads(B[1]), bz, ALU.mult))
                ln.link(v.scalar_tensor_tensor(kbe[:, :, :], kb[:, :, :], -1.0, wide(eg[:, 0:8]), ALU.mult, ALU.mult))
                ln.link(v.tensor_tensor(qe[:, :, :], heads(B[0]), wide(eg[:, 0:8]), ALU.mult))
                ln.link(v.tensor_tensor(k8, heads(B[1]), wide(eg[:, 8:16]), ALU.mult))
                ln.link(v.tensor_tensor(v8, heads(B[2]), bz, ALU.mult))
                ln.tell(q["gd_tok_ready"])
                ends = eg[:, 16:32].rearrange("p (c w h) -> p c w h", c=2, h=2)
                for hf in range(2):
                    part = slice(hf * HD, (hf + 1) * HD)
                    ln.link(v.tensor_copy(dec[GD][part, :, :], ends[part, :, :, hf]))

                ln.hold(q["rk_lt_full"], i + 1)
                masked(lt[RK], BANKS[RK][0:2], STRICT)
                ln.tell(q["rk_lt_ready"])
                ln.hold(q["gd_rows_ready"], i + 1)
                for d, h in ZS:
                    z, m = z_of(d, h)[0], d * H + h
                    ln.link(v.tensor_scalar(gam[:, z, :], whole(B[3])[:, z, :], gcs[:, m:m + 1], 0.0, ALU.subtract, ALU.min))
                ln.tell(q["gd_diff_ready"])
                ln.hold(q["rk_ak_full"], i + 1)
                masked(ak, BANKS[RK][2:4], STRICT)
                ln.tell(q["rk_ak_read"])
                ln.hold(q["gd_gamma_ready"], i + 1)
                for cut in halves:
                    ln.link(v.tensor_tensor(quad(gam_s[:, cut, :]), quad(gam[:, cut, :]), STRICT, ALU.mult))
                ln.hold(q["gd_lt_full"], i + 1)
                for cut, bank in zip(halves, B[0:2]):
                    ln.link(v.tensor_tensor(lt[GD][:, cut, :], half(bank), gam_s[:, cut, :], ALU.mult))
                ln.tell(q["gd_lt_ready"])
                ln.hold(q["rk_mv_full"], i + 1)
                masked(mv, BANKS[RK][0:2], INCL)
                ln.hold(q["rk_mo_full"], i + 1)
                masked(mo[RK], BANKS[RK][2:4], MINUS)
                ln.tell(q["rk_mats_done"])
                for cut in halves:
                    ln.link(v.tensor_tensor(quad(gam[:, cut, :]), quad(gam[:, cut, :]), INCL, ALU.mult))
                ln.hold(q["gd_mo_full"], i + 1)
                ln.tell(q["gd_feat_free"])
                for cut, bank in zip(halves, B[2:4]):
                    ln.link(v.tensor_tensor(mo[GD][:, cut, :], half(bank), gam[:, cut, :], ALU.mult))
                ln.tell(q["gd_mats_done"])

                for n in range(LEVELS):
                    for k in KINDS:
                        if n == 0:
                            ln.hold(q[f"{k}_levels"], i * LEVELS + 1)
                            ln.link(v.tensor_tensor(xt[k][:, :, :], EYES, lk[k][:, 0, :, :], ALU.subtract))
                            ln.hold(q[f"{k}_t_full"], i * LEVELS + 1)
                            ln.link(v.tensor_tensor(x[k][:, :, :], EYES, whole(BANKS[k][0]), ALU.subtract))
                        else:
                            ln.hold(q[f"{k}_p_full"], i * (LEVELS - 1) + n)
                            if n < LEVELS - 1:
                                ln.link(v.tensor_tensor(x[k][:, :, :], x[k][:, :, :], whole(BANKS[k][1]), ALU.subtract))
                            ln.link(v.tensor_tensor(xt[k][:, :, :], xt[k][:, :, :], whole(BANKS[k][2]), ALU.subtract))
                        ln.tell(q[f"{k}_x_ready"])
                for r in range(2):
                    ln.hold(q["gd_rhs_full"], i * 2 + r + 1)
                    for d in range(2):
                        ch = chunk(d, r)
                        ln.link(v.tensor_tensor(rs[GD][ch, :], BANKS[GD][0][ch, 0:W], vt[GD][ch, d, :], ALU.add))
                    ln.tell(q["gd_rhs_moved"])
                    for k in KINDS:
                        ln.hold(q[f"{k}_u_full"], i * 2 + r + 1)
                        ln.link(v.tensor_copy(us[k][:, :], BANKS[k][1][:, 0:W]))
                        ln.tell(q[f"{k}_u_moved"])
                    for k in KINDS:
                        ln.hold(q[f"{k}_o_full"], i * 2 + r + 1)
                        for d in range(2):
                            c = r if d == 0 else 1 - r
                            cut = slice(2 * d, 2 * d + 2)
                            for e in range(2):
                                part = slice(e * HD, (e + 1) * HD)
                                grown = BANKS[k][d][part, 0:2 * HD].rearrange("p (w e) -> p w e", w=2)
                                dd = dec[k][part, c, cut].unsqueeze(2).broadcast_to([HD, 2, HD])
                                sd = st[k][part, e, cut, :]
                                for by, op in ((grown, ALU.add), (dd, ALU.mult)) if k == RK else ((dd, ALU.mult), (grown, ALU.add)):
                                    ln.link(v.tensor_tensor(sd, sd, by, op))
                        ln.tell(q[f"{k}_s_ready"])
                for k in KINDS:
                    ln.tell(q[f"{k}_dve_end"])
                ln.restart()


def peer(nc, g, l, segs):
    lo = segs[0][0]
    with ExitStack() as front:
        qT = front.enter_context(sbuf(nc, "qT", [P, 2 * HEADS, T]))
        project(nc, g, f"q{l}", g.peer_w_q[l], 2 * HEADS, g.hT, segs, out=qT, spill=g.q_feat)
    M = 2 * HEADS
    HALF = RING // 2
    ROUNDS = PICKS // RING
    t0 = lo // P
    N = TT - t0
    before = g.rows_landed * 16
    g.rows_landed += N * 2 * ROUNDS
    with ExitStack() as mem, Stage(nc, f"peer{l}", "keys_in k_turned k_moved q_in q_used scored copied sc_free exp_asked exp_done "
                                   "picked dve_used pe_used h_in h_used h_turned h_moved dots_done gelu_done coef_ready diag_ready "
                                   "diag_used part_read f_ready f_turned f_moved") as s:
        def sb(n, shape, dt=F32):
            return mem.enter_context(sbuf(nc, n, shape, dt))

        idx, gates = sb("idx", [P, TT, PICKS], U32), sb("gates", [P, TT, PICKS])
        keysT = sb("keysT", [P, M, P])
        qs, sc, wk = sb("qs", [P, M, P]), sb("sc", [P, M, NKEYS]), sb("wk", [P, NKEYS])
        top, best = sb("top", [P, M, TOPK]), sb("best", [P, HEADS, TOPK])
        at, pos, ab = sb("at", [P, M, TOPK], U32), sb("pos", [P, PICKS], U32), sb("ab", [P, PICKS], U32)
        atf, abf = sb("atf", [P, M, TOPK]), sb("abf", [P, PICKS])
        cand, eq = sb("cand", [P, HEADS, TOPK * TOPK]), sb("eq", [P, PICKS, TOPK])
        wk2, sel = sb("wk2", [P, TOPK * TOPK]), sb("sel", [P, 2, PICKS])
        ex, den = sb("ex", [P, HEADS, TOPK]), sb("den", [P, HEADS])
        hs, ht, junk, acc = sb("hs", [P, KD, P]), sb("ht", [P, D]), sb("junk", [P, D]), sb("acc", [P, D])
        ring, diag = sb("ring", [P, RING, D]), sb("diag", [P, HALF, P])
        idxc = sb("idxc", [P, RING], U32)
        dots, dot16, coef = sb("dots", [P, PICKS]), sb("dot16", [P, RING]), sb("coef", [P, PICKS])
        mod_all, mod = sb("mod_all", [P, TT, KD]), sb("mod", [P, KD])
        SC = [mem.enter_context(psum(nc, "sc_b", [P, 512])) for _ in range(4)]
        TR = [mem.enter_context(psum(nc, "tr_b", [P, 512])) for _ in range(2)]
        PART = [mem.enter_context(psum(nc, "part_b", [P, 512])) for _ in range(2)]
        keys = sc
        q = s.sem

        def by_vector(j):
            return j % 4 < 2

        mine = [j for j in range(RING) if by_vector(j)]
        others = [j for j in range(RING) if not by_vector(j)]

        @s.body.sync
        def _(sp):
            ln = s.line(sp, "sp")
            sp.dma_start(keys[:, :, :], g.peer_keys[l].rearrange("h s k d -> k (h s) d")).then_inc(q["keys_in"], 16)
            with sp.Fori(0, N) as i:
                at_tile = bass.ds(i * P + lo, P)
                ln.hold(q["q_used"], i + 1)
                sp.dma_start(qs[:, :, :], g.q_feat.rearrange("m p t -> p m t")[:, :, at_tile]).then_inc(q["q_in"], 16)
                ln.hold(q["h_used"], i + 1)
                sp.dma_start(hs[:, :, :], g.hT[:, :, at_tile]).then_inc(q["h_in"], 16)

        @s.body.gpsimd
        def _(pool):
            ln = s.line(pool, "pool")
            tables = [a.rearrange("l e d -> (l e) d") for a in (g.peer_u, g.peer_v)]
            with pool.Fori(0, N) as i:
                ln.hold(q["picked"], i + 1)
                for n, table in enumerate(tables):
                    with pool.Fori(0, ROUNDS) as r:
                        for hf in range(2):
                            ln.hold(q["dve_used"], (i * (2 * ROUNDS) + r + n * ROUNDS) * 2 + hf + 1)
                            ln.hold(q["pe_used"], i * (2 * ROUNDS) + (r * 2 if n else 0) + hf + 1)
                            cut = slice(hf * HALF, (hf + 1) * HALF)
                            ln.link(pool.tensor_copy(idxc[:, cut].unsqueeze(1), idx[:, bass.ds(i + t0, 1), bass.ds(r * RING + hf * HALF, HALF)]))
                            for j in range(hf * HALF, (hf + 1) * HALF):
                                pool.indirect_dma_start(ring[:, j, :], None, table, bass.IndirectOffsetOnAxis(ap=idxc[:, j:j + 1], axis=0)).then_inc(g.row_in[j], 16)
                        ln.restart()

        @s.body.tensor
        def _(pe):
            ln = s.line(pe, "pe")
            ln.credit(q["q_used"], q["h_used"], q["f_moved"], q["part_read"], q["pe_used"], q["pe_used"])
            pe.wait_ge(q["keys_in"], 16)
            for n in range(4):
                for m in range(4):
                    last = pe.transpose(SC[n][:, m * P:(m + 1) * P], keys[:, 4 * n + m, :], g.c(IDENT))
            last.then_inc(q["k_turned"], 1)
            pe.wait_ge(q["k_moved"], 1)

            def prepare(p):
                ln.hold(q["h_in"], p * 16 + 16)
                if not isinstance(p, int):
                    ln.hold(q["h_moved"], p)
                    ln.hold(q["f_moved"], p)
                for k in range(KD):
                    last = pe.transpose(TR[k // 4][:, k % 4 * P:(k % 4 + 1) * P], hs[:, k, :], g.c(IDENT))
                last.then_inc(q["h_turned"], 1)
                ln.hold(q["h_turned"], p + 1)
                ln.tell(q["h_used"])
                ln.hold(q["q_in"], p * 16 + 16)
                ln.hold(q["copied"], p + 1)
                for n in range(M):
                    last = pe.matmul(SC[n // 4][:, n % 4 * P:(n % 4 + 1) * P], qs[:, n, :], keysT[:, n, :], start=True, stop=True)
                last.then_inc(q["scored"], 1)
                ln.hold(q["scored"], p + 1)
                ln.tell(q["q_used"])

            def tile(i, more):
                if more:
                    prepare(i + 1)
                ln.hold(q["part_read"], i + 1)
                for r in range(ROUNDS):
                    for j in others:
                        ln.hold(g.row_in[j], i * (2 * ROUNDS * 16) + (r + ROUNDS + 1) * 16 + before)
                        slot = others.index(j)
                        ln.hold(q["diag_ready"], i * (PICKS // 2) + r * HALF + slot + 1)
                        for n in range(2):
                            last = pe.matmul(PART[n][:, :], diag[:, slot, :], ring[:, j, n * 512:(n + 1) * 512],
                                             start=r == 0 and slot == 0, stop=r == ROUNDS - 1 and slot == HALF - 1)
                        last.then_inc(q["diag_used"], 1)
                        if j % HALF == HALF - 1:
                            ln.hold(q["diag_used"], i * (PICKS // 2) + r * HALF + slot + 1 + HALF)
                            ln.tell(q["pe_used"])
                ln.hold(q["f_ready"], i + 1)
                if more:
                    ln.hold(q["h_moved"], i + 2)
                for k in range(KD):
                    last = pe.transpose(TR[k // 4][:, k % 4 * P:(k % 4 + 1) * P], acc[:, k * P:(k + 1) * P], g.c(IDENT))
                last.then_inc(q["f_turned"], 1)

            prepare(0)
            with pe.Fori(0, N - 1) as i:
                tile(i, True)
            tile(N - 1, False)

        @s.body.scalar
        def _(act):
            ln = s.line(act, "act")
            ln.credit(q["copied"])
            act.wait_ge(q["k_turned"], 1)
            for n in range(4):
                ln.link(act.activation(keysT[:, 4 * n:4 * n + 4, :], SC[n][:, :].rearrange("p (m k) -> p m k", m=4), ACT.Copy))
            ln.tell(q["k_moved"])

            def copy_scores(p):
                ln.hold(q["scored"], p + 1)
                ln.hold(q["sc_free"], p + 1)
                for n in range(4):
                    ln.link(act.activation(sc[:, 4 * n:4 * n + 4, :], SC[n][:, :].rearrange("p (m k) -> p m k", m=4), ACT.Copy))
                ln.tell(q["copied"])

            def exponentials(p):
                ln.hold(q["exp_asked"], p + 1)
                ln.link(act.activation(ex[:, :, :], ex[:, :, :], ACT.Exp))
                ln.tell(q["exp_done"])

            def tile(i, more):
                if more:
                    copy_scores(i + 1)
                ln.hold(q["dots_done"], i + 1)
                ln.link(act.activation(dots[:, :], dots[:, :], ACT.Gelu_apprx_tanh))
                ln.tell(q["gelu_done"])
                ln.hold(q["coef_ready"], i + 1)
                for r in range(ROUNDS):
                    for slot, j in enumerate(others):
                        ln.hold(q["diag_used"], i * (PICKS // 2) + r * HALF + slot + 1)
                        ln.link(act.activation(diag[:, slot, :], g.c(IDENT), ACT.Copy, scale=coef[:, r * RING + j:r * RING + j + 1]))
                        ln.tell(q["diag_ready"])
                    if more and r == EXP_ROUND:
                        exponentials(i + 1)
                ln.restart()

            copy_scores(0)
            exponentials(0)
            ln.restart()
            with act.Fori(0, N - 1) as i:
                tile(i, True)
            tile(N - 1, False)

        @s.body.vector
        def _(v):
            ln = s.line(v, "dve")
            ln.credit(q["sc_free"], q["dve_used"], q["dve_used"])
            ln.tell(q["diag_used"], HALF)
            for t in range(t0, TT):
                c = 1 if t < CT else 0
                ln.link(v.tensor_copy(mod_all[:, t, :], g.mods[:, 5 * KD:6 * KD, c]))

            def top16(values, work, out, where):
                ln.link(v.max(out[:, 0:8], values))
                ln.link(v.max_index(where[:, 0:8], out[:, 0:8], values))
                ln.link(v.match_replace(work, out[:, 0:8], values, NEG))
                ln.link(v.max(out[:, 8:16], work))
                ln.link(v.max_index(where[:, 8:16], out[:, 8:16], work))

            def take_h(p):
                ln.hold(q["h_turned"], p + 1)
                for n in range(2):
                    ln.link(v.tensor_copy(ht[:, n * 512:(n + 1) * 512], TR[n][:, :]))
                ln.tell(q["h_moved"])

            def lists(p, m0, m1):
                if m0 == 0:
                    ln.hold(q["copied"], p + 2)
                for m in range(m0, m1):
                    top16(sc[:, m, :], wk[:, :], top[:, m, :], at[:, m, :])
                if m1 == M:
                    ln.tell(q["sc_free"])

            def candidates():
                tv = top[:, :, :].rearrange("p (h s) k -> p h s k", s=2)
                ln.link(v.tensor_copy(atf[:, :, :], at[:, :, :]))
                ln.link(v.tensor_tensor(cand[:, :, :].rearrange("p h (a b) -> p h a b", a=TOPK),
                                        tv[:, :, 0, :].unsqueeze(3).broadcast_to([P, HEADS, TOPK, TOPK]),
                                        tv[:, :, 1, :].unsqueeze(2).broadcast_to([P, HEADS, TOPK, TOPK]), ALU.add))

            def heads(h0, h1):
                for h in range(h0, h1):
                    top16(cand[:, h, :], wk2[:, :], best[:, h, :], pos[:, h * TOPK:(h + 1) * TOPK])

            def ask_softmax():
                ln.link(v.tensor_tensor(ex[:, :, :], best[:, :, :], best[:, :, 0:1].broadcast_to([P, HEADS, TOPK]), ALU.subtract))
                ln.tell(q["exp_asked"])

            def places(n):
                iota = g.c(IOTA, TOPK).unsqueeze(1).broadcast_to([P, PICKS, TOPK])
                fv = atf[:, :, :].rearrange("p (h s) k -> p h s k", s=2)
                op, by = ((ALU.logical_shift_right, 4), (ALU.bitwise_and, TOPK - 1))[n]
                ln.link(v.tensor_scalar(ab[:, :], pos[:, :], by, None, op))
                ln.link(v.tensor_copy(abf[:, :], ab[:, :]))
                ln.link(v.tensor_tensor(eq[:, :, :], abf[:, :].unsqueeze(2).broadcast_to([P, PICKS, TOPK]), iota, ALU.is_equal))
                e4 = eq[:, :, :].rearrange("p (h k) a -> p h k a", h=HEADS)
                ln.link(v.tensor_tensor(e4, e4, fv[:, :, n, :].unsqueeze(2).broadcast_to([P, HEADS, TOPK, TOPK]), ALU.mult))
                ln.link(v.tensor_reduce(sel[:, n, :], eq[:, :, :], AX_X, ALU.add))

            def finish(p):
                here = bass.ds(p + t0, 1)
                ln.link(v.tensor_scalar(sel[:, 0, :], sel[:, 0, :], float(NKEYS), float(l * EXPERTS), ALU.mult, ALU.add))
                ln.link(v.tensor_tensor(idx[:, here, :], sel[:, 0:1, :], sel[:, 1:2, :], ALU.add))
                ln.tell(q["picked"])
                ln.hold(q["exp_done"], p + 1)
                ln.link(v.tensor_reduce(den[:, :], ex[:, :, :], AX_X, ALU.add))
                ln.link(v.reciprocal(den[:, :], den[:, :]))
                ln.link(v.tensor_tensor(gates[:, here, :].rearrange("p a (h k) -> p (a h) k", h=HEADS), ex[:, :, :],
                                        den[:, :].unsqueeze(2).broadcast_to([P, HEADS, TOPK]), ALU.mult))

            def tile(i, more):
                with v.Fori(0, ROUNDS) as r:
                    for j in range(RING):
                        ln.hold(g.row_in[j], (i * (2 * ROUNDS) + r) * 16 + before + 16)
                        ln.link(v.tensor_tensor_reduce(junk[:, :], ring[:, j, :], ht[:, :], 1.0, 0.0, ALU.mult, ALU.add, dot16[:, j:j + 1]))
                        if j % HALF == HALF - 1:
                            ln.tell(q["dve_used"])
                    ln.link(v.tensor_copy(dots[:, bass.ds(r * RING, RING)], dot16[:, :]))
                    ln.restart()
                ln.tell(q["dots_done"])
                if more:
                    take_h(i + 1)
                ln.link(v.tensor_copy(mod[:, :].unsqueeze(1), mod_all[:, bass.ds(i + t0, 1), :]))
                ln.hold(q["gelu_done"], i + 1)
                ln.link(v.tensor_tensor(coef[:, :].unsqueeze(1), dots[:, :].unsqueeze(1), gates[:, bass.ds(i + t0, 1), :], ALU.mult))
                ln.tell(q["coef_ready"])
                for r in range(ROUNDS):
                    for j in mine:
                        ln.hold(g.row_in[j], i * (2 * ROUNDS * 16) + (r + ROUNDS + 1) * 16 + before)
                        by = coef[:, r * RING + j:r * RING + j + 1]
                        if r == 0 and j == 0:
                            ln.link(v.tensor_scalar(acc[:, :], ring[:, j, :], by, None, ALU.mult))
                        else:
                            ln.link(v.scalar_tensor_tensor(acc[:, :], ring[:, j, :], by, acc[:, :], ALU.mult, ALU.add))
                        if j in (mine[HALF // 2 - 1], mine[-1]):
                            ln.tell(q["dve_used"])
                    if more:
                        if r < 3:
                            lists(i + 1, (0, 6, 11, 16)[r], (0, 6, 11, 16)[r + 1])
                        elif r == 3:
                            candidates()
                            heads(0, 3)
                        elif r == 4:
                            heads(3, HEADS)
                            ask_softmax()
                        elif r == 5:
                            places(0)
                        elif r == 6:
                            places(1)
                            finish(i + 1)
                ln.hold(q["diag_used"], i * (PICKS // 2) + PICKS // 2 + HALF)
                for n in range(2):
                    ln.link(v.tensor_tensor(acc[:, n * 512:(n + 1) * 512], acc[:, n * 512:(n + 1) * 512], PART[n][:, :], ALU.add))
                ln.tell(q["part_read"])
                ln.tell(q["f_ready"])
                ln.hold(q["f_turned"], i + 1)
                tok = bass.ds(i * P + lo, P)
                for k in range(KD):
                    ln.link(v.scalar_tensor_tensor(g.xT[:, k, tok], TR[k // 4][:, k % 4 * P:(k % 4 + 1) * P],
                                                   mod[:, k:k + 1], g.xT[:, k, tok], ALU.mult, ALU.add))
                ln.tell(q["f_moved"])
                ln.restart()

            take_h(0)
            lists(0, 0, M)
            candidates()
            heads(0, HEADS)
            ask_softmax()
            places(0)
            places(1)
            finish(0)
            ln.restart()
            with v.Fori(0, N - 1) as i:
                tile(i, True)
            tile(N - 1, False)


def store_tokens(nc, g):
    with ExitStack() as mem, Stage(nc, "store", "turned moved stored") as s:
        rows = mem.enter_context(sbuf(nc, "orows", [P, TT - CT, D], F32))
        ps = [mem.enter_context(psum(nc, f"st{i}", [P, 4 * P], F32)) for i in range(2)]
        q = s.sem
        N = (TT - CT) * 2

        @s.body.tensor
        def _(pe):
            for n in range(N):
                if n >= 2:
                    pe.wait_ge(q["moved"], n - 1)
                for j in range(4):
                    t0 = CTX + n // 2 * P
                    last = pe.transpose(ps[n % 2][:, j * P:(j + 1) * P], g.hT[:, n % 2 * 4 + j, t0:t0 + P], g.c(IDENT))
                last.then_inc(q["turned"], 1)

        @s.body.vector
        def _(v):
            for n in range(N):
                v.wait_ge(q["turned"], n + 1)
                v.tensor_copy(rows[:, n // 2, n % 2 * 512:n % 2 * 512 + 512], ps[n % 2][:, :]).then_inc(q["moved"], 1)

        @s.body.sync
        def _(sp):
            sp.wait_ge(q["moved"], N)
            sp.dma_start(g.out[0].rearrange("(t p) d -> p t d", p=P), rows[:, :, :]).then_inc(q["stored"], 16)
            sp.wait_ge(q["stored"], 16)


def program(nc, args, consts, out):
    with ExitStack() as mem:
        def sb(name, shape, dt=F32):
            return mem.enter_context(sbuf(nc, name, shape, dt))

        g = Program()
        g.x, g.cvec, g.ctx, g.c_ctx, g.w_ada, g.b_ada = (args[n] for n in NAMES[0:6])
        g.norm1_g, g.norm2_g, g.w_in, g.rwkv_mu, g.rwkv_w0, g.rwkv_w2 = (args[n] for n in NAMES[6:12])
        g.rwkv_a0, g.rwkv_a2, g.rwkv_g2, g.rwkv_k_k, g.rwkv_k_a, g.rwkv_r_k = (args[n] for n in NAMES[12:18])
        g.rwkv_gn_g, g.rwkv_gn_b, g.gdn_conv_w, g.gdn_a_log, g.gdn_dt_bias, g.gdn_norm_g = (args[n] for n in NAMES[18:24])
        g.sgu_ln_g, g.sgu_ln_b, g.sgu_w_s, g.sgu_b_s, g.conf_dw_w, g.conf_dw_b = (args[n] for n in NAMES[24:30])
        g.conf_ln_g, g.conf_ln_b, g.w_branch, g.w_out, g.peer_w_q, g.peer_keys = (args[n] for n in NAMES[30:36])
        g.peer_u, g.peer_v, g.final_g = (args[n] for n in NAMES[36:39])
        g.out, g.consts = out, consts
        g.xT = sb("xT", [P, KD, T])
        g.hT = sb("hT", [P, KD, T])
        g.cst = sb("cst", [P, NCONST])
        g.cond = sb("cond", [P, KD, 2])
        g.cond_sig = sb("cond_sig", [P, KD, 2])
        g.mods = sb("mods", [P, 6 * KD, 2])
        g.gs = sb("gs", [P, 2, KD, 2])
        g.c = lambda col, n=P: g.cst[:, col:col + n]
        g.rk_feat = nc.dram_tensor("rk_feat", [18, P, T], F32, kind="Internal").ap()
        g.rk_logw = nc.dram_tensor("rk_logw", [T, 2 * W], F32, kind="Internal").ap()
        g.gd_feat = nc.dram_tensor("gd_feat", [6, P, T], F32, kind="Internal").ap()
        g.q_feat = nc.dram_tensor("q_feat", [2 * HEADS, P, T], F32, kind="Internal").ap()
        g.row_in = [mem.enter_context(nc.semaphore(f"row_in{j}")) for j in range(RING)]
        g.rows_landed = 0
        load_tokens(nc, g)
        for l in range(DEPTH):
            segs = SEG_ALL if l < DEPTH - 1 else SEG_X
            ada(nc, g, l)
            norm(nc, g, f"norm1_{l}", SEG_ALL, 0)
            with ExitStack() as mix:
                g.oT = mix.enter_context(sbuf(nc, "oT", [P, 4, WT, T]))
                mixers(nc, g, l)
                with sbuf(nc, "sgu_p", [P, 4, T]) as sgu_p:
                    conformer(nc, g, l, sgu_p)
                    sgu(nc, g, l, sgu_p)
                g.mT = mix.enter_context(sbuf(nc, "mT", [P, KD, T]))
                merge(nc, g, l, segs)
                project(nc, g, f"out{l}", g.w_out[l], KD, g.mT, segs, residual=2)
            norm(nc, g, f"norm2_{l}", segs, 1)
            peer(nc, g, l, segs)
        norm(nc, g, "final", SEG_X, 0, g.final_g)
        store_tokens(nc, g)


NAMES = ("x cvec ctx c_ctx w_ada b_ada norm1_g norm2_g w_in rwkv_mu rwkv_w0 rwkv_w2 rwkv_a0 rwkv_a2 rwkv_g2 rwkv_k_k "
         "rwkv_k_a rwkv_r_k rwkv_gn_g rwkv_gn_b gdn_conv_w gdn_a_log gdn_dt_bias gdn_norm_g sgu_ln_g sgu_ln_b sgu_w_s "
         "sgu_b_s conf_dw_w conf_dw_b conf_ln_g conf_ln_b w_branch w_out peer_w_q peer_keys peer_u peer_v final_g").split()


def kernel(**inputs):
    import concourse.bacc as bacc
    from concourse.bass_utils import run_bass_kernel_spmd as run

    nc = bacc.Bacc("TRN2", target_bir_lowering=False, num_devices=1)
    arrays, args = {}, {}
    for name in NAMES:
        a = np.ascontiguousarray(inputs["c" if name == "cvec" else name])
        arrays[f"in_{name}"] = a
        args[name] = nc.dram_tensor(f"in_{name}", a.shape, mybir.dt.from_np(a.dtype), kind="ExternalInput").ap()
    arrays["in_consts"] = constants()
    consts = nc.dram_tensor("in_consts", (P, NCONST), F32, kind="ExternalInput").ap()
    out = nc.dram_tensor("out_0", (1, SEQ, D), F32, kind="ExternalOutput").ap()
    program(nc, args, consts, out)
    return run(nc, [arrays], core_ids=[0]).results[0]["out_0"]
```
